# Optimizing a Trainium2 kernel written in Bass

```python
import math
import jax, jax.numpy as jnp
from jax import lax
import numpy as np

D_MODEL = 1024
BATCH = 1
SEQ = 256
DEPTH = 2

CHUNK = 64
Q_BLOCK = 128
A_HEADS = 8
A_HEAD_DIM = 64
A_WIDTH = A_HEADS * A_HEAD_DIM
B_WIDTH = 512
CONV_WIDTH = 3
C_HEADS = 4
C_KEY_DIM = 64
C_VAL_DIM = 128
C_KEY_WIDTH = C_HEADS * C_KEY_DIM
C_VAL_WIDTH = C_HEADS * C_VAL_DIM
C_LOWRANK = 16
C_GATE_TEMP = 16.0
N_BRANCHES = 3
D_FF = 2816
N_EXPERTS = 8
TOP_K = 2
N_DENSE = (DEPTH + 1) // 2
N_MOE = DEPTH // 2
EPS = 1e-6
IN_SIZES = (A_WIDTH, A_WIDTH, A_WIDTH, A_HEADS,
            B_WIDTH, B_WIDTH, B_WIDTH,
            C_KEY_WIDTH, C_KEY_WIDTH, C_VAL_WIDTH, C_LOWRANK, C_VAL_WIDTH)
IN_COLS = sum(IN_SIZES)

kernel_name = "hybrid_fox_conv_gla_moe_block"

def rms_norm(x, g):
    xf = x.astype(jnp.float32)
    y = xf * lax.rsqrt(jnp.mean(xf * xf, axis=-1, keepdims=True) + EPS)
    return (y * g.astype(jnp.float32)).astype(x.dtype)

def fox_attention(q, k, v, f_logit, b_f):
    B, S, H, Dh = q.shape
    nb = S // Q_BLOCK
    log_f = jax.nn.log_sigmoid(f_logit.astype(jnp.float32) + b_f.astype(jnp.float32))
    F = jnp.cumsum(log_f, axis=1).transpose(0, 2, 1)
    qh = q.transpose(0, 2, 1, 3)
    kh = k.transpose(0, 2, 1, 3)
    vh = v.transpose(0, 2, 1, 3)
    q_blocks = qh.reshape(B, H, nb, Q_BLOCK, Dh).transpose(2, 0, 1, 3, 4)
    F_blocks = F.reshape(B, H, nb, Q_BLOCK).transpose(2, 0, 1, 3)
    k_pos = jnp.arange(S)
    scale = 1.0 / math.sqrt(Dh)

    def one_block(args):
        qb, Fqb, blk = args
        s = jnp.einsum('bhqd,bhkd->bhqk', qb, kh).astype(jnp.float32) * scale
        s = s + (Fqb[..., :, None] - F[..., None, :])
        q_pos = blk * Q_BLOCK + jnp.arange(Q_BLOCK)
        s = jnp.where(k_pos[None, :] <= q_pos[:, None], s, -jnp.inf)
        p = jax.nn.softmax(s, axis=-1)
        return jnp.einsum('bhqk,bhkd->bhqd', p.astype(vh.dtype), vh)

    out = lax.map(one_block, (q_blocks, F_blocks, jnp.arange(nb)))
    return out.transpose(1, 0, 3, 2, 4).reshape(B, S, H * Dh)

def short_gated_conv(u, b_gate, c_gate, conv_w):
    S = u.shape[1]
    z = c_gate * u
    zp = jnp.pad(z, ((0, 0), (CONV_WIDTH - 1, 0), (0, 0)))
    conv = conv_w[0] * zp[:, 0:S] + conv_w[1] * zp[:, 1:S + 1] + conv_w[2] * zp[:, 2:S + 2]
    return b_gate * conv

def gla_chunked(q, k, v, a_lowrank, r, w_a2, b_a, g_gla):
    B, S, H, dk = q.shape
    dv = v.shape[-1]
    n = S // CHUNK
    log_a = jax.nn.log_sigmoid((a_lowrank @ w_a2 + b_a).astype(jnp.float32)) / C_GATE_TEMP
    log_a = log_a.reshape(B, S, H, dk)

    def chunks(t):
        return t.reshape(B, n, CHUNK, H, t.shape[-1]).transpose(0, 3, 1, 2, 4)

    qc = chunks(q).astype(jnp.float32) * (dk ** -0.5)
    kc = chunks(k).astype(jnp.float32)
    vc = chunks(v).astype(jnp.float32)
    bcum = jnp.cumsum(chunks(log_a), axis=3)
    b_last = bcum[..., -1, :]
    q_t = qc * jnp.exp(bcum)
    k_t = kc * jnp.exp(-bcum)
    tri = jnp.tril(jnp.ones((CHUNK, CHUNK), dtype=bool))
    A = jnp.where(tri, jnp.einsum('bhnqd,bhnkd->bhnqk', q_t, k_t), 0.0)
    o_intra = jnp.einsum('bhnqk,bhnke->bhnqe', A, vc)
    k_state = kc * jnp.exp(b_last[..., None, :] - bcum)
    chunk_kv = jnp.einsum('bhnkd,bhnke->bhnde', k_state, vc)
    decay = jnp.exp(b_last)

    def step(state, inp):
        dec, kv = inp
        return dec[..., None] * state + kv, state

    init = jnp.zeros((B, H, dk, dv), jnp.float32)
    _, states = lax.scan(step, init, (jnp.moveaxis(decay, 2, 0), jnp.moveaxis(chunk_kv, 2, 0)))
    states = jnp.moveaxis(states, 0, 2)
    o = o_intra + jnp.einsum('bhnqd,bhnde->bhnqe', q_t, states)
    o = o.transpose(0, 2, 3, 1, 4).reshape(B, S, H, dv)
    o = o * lax.rsqrt(jnp.mean(o * o, axis=-1, keepdims=True) + EPS)
    o = o * g_gla.astype(jnp.float32).reshape(H, dv)
    o = o.reshape(B, S, H * dv).astype(r.dtype)
    return o * jax.nn.silu(r)

def hybrid_mixer(h, w_in, b_f, conv_w, w_a2, b_a, g_gla, w_pa, w_pb, w_pc, w_gate, b_gate, w_o):
    B, S, _ = h.shape
    proj = h @ w_in
    split_points = np.cumsum(IN_SIZES)[:-1].tolist()
    (a_q, a_k, a_v, a_f, b_u, b_bg, b_cg,
     c_q, c_k, c_v, c_a, c_r) = jnp.split(proj, split_points, axis=-1)
    o_a = fox_attention(a_q.reshape(B, S, A_HEADS, A_HEAD_DIM),
                        a_k.reshape(B, S, A_HEADS, A_HEAD_DIM),
                        a_v.reshape(B, S, A_HEADS, A_HEAD_DIM), a_f, b_f)
    o_b = short_gated_conv(b_u, b_bg, b_cg, conv_w)
    o_c = gla_chunked(c_q.reshape(B, S, C_HEADS, C_KEY_DIM),
                      c_k.reshape(B, S, C_HEADS, C_KEY_DIM),
                      c_v.reshape(B, S, C_HEADS, C_VAL_DIM), c_a, c_r, w_a2, b_a, g_gla)
    g_a, g_b, g_c = jnp.split(jax.nn.sigmoid(h @ w_gate + b_gate), N_BRANCHES, axis=-1)
    merged = g_a * (o_a @ w_pa) + g_b * (o_b @ w_pb) + g_c * (o_c @ w_pc)
    return merged @ w_o

def swiglu(h, w1, w3, w2):
    return (jax.nn.silu(h @ w1) * (h @ w3)) @ w2

def moe_swiglu(h, w_router, w1, w3, w2):
    logits = (h @ w_router).astype(jnp.float32)
    top_vals, top_idx = lax.top_k(logits, TOP_K)
    top_w = jax.nn.softmax(top_vals, axis=-1)
    gate = jnp.sum(jax.nn.one_hot(top_idx, N_EXPERTS, dtype=jnp.float32) * top_w[..., None], axis=-2)
    gate = gate.astype(h.dtype)
    out = jnp.zeros_like(h)
    for e in range(N_EXPERTS):
        out = out + gate[..., e:e + 1] * swiglu(h, w1[e], w3[e], w2[e])
    return out

def setup_inputs(seed: int = 0) -> dict:
    key = jax.random.key(seed)
    ks = jax.random.split(key, 24)

    def nrm(k, shape, scale):
        return scale * jax.random.normal(k, shape, jnp.float32)

    D = D_MODEL
    return {
        "x": nrm(ks[0], (BATCH, SEQ, D), 1.0),
        "g_mix": 1.0 + nrm(ks[1], (DEPTH, D), 0.02),
        "w_in": nrm(ks[2], (DEPTH, D, IN_COLS), D ** -0.5),
        "b_f": 4.0 + nrm(ks[3], (DEPTH, A_HEADS), 0.1),
        "conv_w": nrm(ks[4], (DEPTH, CONV_WIDTH, B_WIDTH), CONV_WIDTH ** -0.5),
        "w_a2": nrm(ks[5], (DEPTH, C_LOWRANK, C_KEY_WIDTH), C_LOWRANK ** -0.5),
        "b_a": nrm(ks[6], (DEPTH, C_KEY_WIDTH), 0.1),
        "g_gla": 1.0 + nrm(ks[7], (DEPTH, C_VAL_WIDTH), 0.02),
        "w_pa": nrm(ks[8], (DEPTH, A_WIDTH, D), A_WIDTH ** -0.5),
        "w_pb": nrm(ks[9], (DEPTH, B_WIDTH, D), B_WIDTH ** -0.5),
        "w_pc": nrm(ks[10], (DEPTH, C_VAL_WIDTH, D), C_VAL_WIDTH ** -0.5),
        "w_gate": nrm(ks[11], (DEPTH, D, N_BRANCHES * D), D ** -0.5),
        "b_gate": nrm(ks[12], (DEPTH, N_BRANCHES * D), 0.1),
        "w_o": nrm(ks[13], (DEPTH, D, D), D ** -0.5),
        "g_ffn": 1.0 + nrm(ks[14], (DEPTH, D), 0.02),
        "ffn_w1": nrm(ks[15], (N_DENSE, D, D_FF), D ** -0.5),
        "ffn_w3": nrm(ks[16], (N_DENSE, D, D_FF), D ** -0.5),
        "ffn_w2": nrm(ks[17], (N_DENSE, D_FF, D), D_FF ** -0.5),
        "w_router": nrm(ks[18], (N_MOE, D, N_EXPERTS), D ** -0.5),
        "moe_w1": nrm(ks[19], (N_MOE, N_EXPERTS, D, D_FF), D ** -0.5),
        "moe_w3": nrm(ks[20], (N_MOE, N_EXPERTS, D, D_FF), D ** -0.5),
        "moe_w2": nrm(ks[21], (N_MOE, N_EXPERTS, D_FF, D), D_FF ** -0.5),
        "g_final": 1.0 + nrm(ks[22], (D,), 0.02),
    }

def reference(x, g_mix, w_in, b_f, conv_w, w_a2, b_a, g_gla, w_pa, w_pb, w_pc,
              w_gate, b_gate, w_o, g_ffn, ffn_w1, ffn_w3, ffn_w2,
              w_router, moe_w1, moe_w3, moe_w2, g_final):
    for l in range(DEPTH):
        h = rms_norm(x, g_mix[l])
        x = x + hybrid_mixer(h, w_in[l], b_f[l], conv_w[l], w_a2[l], b_a[l], g_gla[l],
                             w_pa[l], w_pb[l], w_pc[l], w_gate[l], b_gate[l], w_o[l])
        h = rms_norm(x, g_ffn[l])
        i = l // 2
        if l % 2 == 0:
            x = x + swiglu(h, ffn_w1[i], ffn_w3[i], ffn_w2[i])
        else:
            x = x + moe_swiglu(h, w_router[i], moe_w1[i], moe_w3[i], moe_w2[i])
    return rms_norm(x, g_final)


_drawn_inputs = setup_inputs


def setup_inputs(seed=0):
    import zlib

    import numpy as np

    out = dict(_drawn_inputs(seed))
    spreads = {}
    factors = {'g_gla': 2.827, 'g_final': 2.825}
    for name, (base, spread) in spreads.items():
        noise = np.random.default_rng([zlib.crc32(name.encode()), seed]).standard_normal(out[name].shape)
        drawn = base * np.exp(spread * noise) if base else spread * noise
        out[name] = __import__('jax').numpy.asarray(drawn.astype(out[name].dtype))
    for name, factor in factors.items():
        out[name] = (out[name] * factor).astype(out[name].dtype)
    return out
```

```python
import numpy as np
import concourse.bass as bass
from concourse import mybir
from contextlib import ExitStack


def hybrid_trunk(nc, x, g_mix, w_in, b_f, conv_w, w_a2, b_a, g_gla, w_pa, w_pb, w_pc, w_gate,
                 b_gate, w_o, g_ffn, ffn_w1, ffn_w3, ffn_w2, w_router, moe_w1, moe_w3, moe_w2,
                 g_final, out):
    F32, F32R, BF16, I32 = mybir.dt.float32, mybir.dt.float32r, mybir.dt.bfloat16, mybir.dt.int32
    ALU, ACT, AX = mybir.AluOpType, mybir.ActivationFunctionType, mybir.AxisListType
    ds = bass.ds

    P = 128
    S, D = x.shape[1], x.shape[2]
    TT, KD = S // P, D // P
    L = w_in.shape[0]
    HA, DH = b_f.shape[1], 64
    WB = conv_w.shape[2]
    LR, WK = w_a2.shape[1], w_a2.shape[2]
    HC, DK, DV = 4, 64, 128
    CH = 64
    NPAIR = WK // P
    NE, DF = moe_w1.shape[1], moe_w1.shape[3]
    FC = 256
    NF = DF // FC
    KW = 4
    UC = 512
    UN = KW * UC
    EPS = 1e-6
    NEG = -1e30
    CAP = P

    sizes = (WB, WB, WB, HA, WB, WB, WB, WK, WK, WB, LR, WB)
    offs = [sum(sizes[:i]) for i in range(len(sizes))]
    (C_AQ, C_AK, C_AV, C_AF, C_BU, C_BB, C_BC, C_CQ, C_CK, C_CV, C_CA, C_CR) = offs
    SM = HA + LR

    def panels_of(l):
        rows = [("k", w_in[l], C_AK, True, KD, "act", "act"), ("q", w_in[l], C_AQ, True, KD, "act", "act"),
                ("v", w_in[l], C_AV, False, KD, "act", "act"), ("cqk", w_in[l], C_CQ, True, KD, "act", "act"),
                ("cv", w_in[l], C_CV, False, KD, "act", "act"), ("cr", w_in[l], C_CR, False, KD, "act", "act"),
                ("u", w_in[l], C_BU, True, KD, "act", "act"), ("cg", w_in[l], C_BC, True, KD, "act", "dve"),
                ("bg", w_in[l], C_BB, True, KD, "act", "dve")]
        for br, wp in ((1, w_pb[l]), (0, w_pa[l]), (2, w_pc[l])):
            for half in range(2):
                rows.append((f"gate{br}{half}", w_gate[l], br * D + half * UC, True, KD, "act", "act"))
                rows.append((f"proj{br}{half}", wp, half * UC, True, WB // P, "o%d" % br, "dve"))
        for half in range(2):
            rows.append((f"out{half}", w_o[l], half * UC, False, KD, "act", "dve"))
        return rows

    NPAN = len(panels_of(0))
    NUNIT = sum(r[4] // KW for r in panels_of(0))
    NAMES = [r[0] for r in panels_of(0)]
    EVAC = [r[6] for r in panels_of(0)]

    def evacuated(g, engine):
        return sum(EVAC[i % NPAN] == engine for i in range(g + 1))

    def units_until(g):
        return sum(panels_of(0)[i % NPAN][4] // KW for i in range(g + 1))

    HS = 3

    MRING, SRING = 6, 3

    ctx = ExitStack()
    with ctx:
        def sb(name, shape, dt=F32, c=ctx):
            return c.enter_context(nc.sbuf_tensor(name, shape, dt))

        def sem(name):
            return ctx.enter_context(nc.semaphore(name))

        raw = sb("raw", [P, 9, UN])
        w_hi = sb("w_hi", [P, SRING, UN], F32R)
        w_lo = sb("w_lo", [P, SRING, UN], F32R)
        xres = sb("xres", [P, TT, D])
        hn = sb("hn", [P, TT, D])
        act_hi = sb("act_hi", [P, KD, S], F32R)
        act_lo = sb("act_lo", [P, KD, S], F32R)
        merged = sb("merged", [P, KD, S])
        gains = merged[:, 0:4, :].rearrange("p a b -> p (a b)")
        ident = sb("ident", [P, P])
        cmask = sb("cmask", [P, 2 * P])
        tri = sb("tri", [P, 3 * P])
        gmask = sb("gmask", [P, P])
        keep = sb("keep", [P, S])
        sumsq = sb("sumsq", [P, TT])
        rstd = sb("rstd", [P, TT])
        mhalf = sb("mhalf", [P, 8])
        zrow = sb("zrow", [1, UC], BF16)
        prm = sb("prm", [P, P])
        wsm = sb("wsm", [P, L, KD, SM])
        wsm_hi = sb("wsm_hi", [P, KD, SM], F32R)
        wsm_lo = sb("wsm_lo", [P, KD, SM], F32R)
        wa2 = sb("wa2", [LR, WK])
        bf = sb("bf", [P, L, HA])
        wr = sb("wr", [P, KD, NE])
        wr_hi = sb("wr_hi", [P, KD, NE], F32R)
        wr_lo = sb("wr_lo", [P, KD, NE], F32R)
        iota_i = keep[:, 0:P].bitcast(I32)

        NCONV, NBA, NGG, NBG = L * 3 * WB // P, L * WK // P, L * WB // P, L * 3 * D // P
        R_CONV, R_BA, R_GG, R_BG = 0, NCONV, NCONV + NBA, NCONV + NBA + NGG
        NPRM = R_BG + NBG
        prm_rows = hn[0:NPRM, 0, 0:P]

        mix = ExitStack()
        qT = sb("qT", [P, 4, S], c=mix)
        kT = sb("kT", [P, 4, S], c=mix)
        vA = sb("vA", [P, TT, WB], c=mix)
        oa_hi = sb("oa_hi", [P, 4, S], F32R, c=mix)
        oa_lo = sb("oa_lo", [P, 4, S], F32R, c=mix)
        obc_hi = sb("obc_hi", [P, 4, S], F32R, c=mix)
        obc_lo = sb("obc_lo", [P, 4, S], F32R, c=mix)
        probs = sb("probs", [P, 2, 3 * P], c=mix)
        f_query = sb("f_query", [98, 2, S], c=mix)
        f_key = sb("f_key", [98, 2, S], c=mix)
        f_rows = merged[0:HA, 4:6, :]
        logf = sb("logf", [P, TT, SM], c=mix)
        lsa = sb("lsa", [P, 2, TT * HA], c=mix)
        aT = merged[0:LR, 6, :]
        cum = merged[:, 0:NPAIR, :]
        decay = sb("decay", [P, NPAIR, S // CH], c=mix)
        mx = sb("mx", [P, 2 * HA], c=mix)
        nmx = sb("nmx", [P, 2 * HA], c=mix)
        sm = sb("sm", [P, 2 * HA], c=mix)
        rs = sb("rs", [P, 2 * HA], c=mix)
        oss = sb("oss", [P, 2 * HC], c=mix)
        ors = sb("ors", [P, 2 * HC], c=mix)
        spare = raw[:, 6:9, :].rearrange("p a n -> p (a n)")
        ZP = S + 2
        at = [0]

        def carve(n):
            at[0] += n
            return spare[:, at[0] - n:at[0]]
        cqkT = carve(4 * S).rearrange("p (a t) -> p a t", t=S)
        vC = carve(TT * WB).rearrange("p (a t) -> p a t", t=WB)
        rC = carve(TT * WB).rearrange("p (a t) -> p a t", t=WB)
        zB = carve(4 * ZP).rearrange("p (a t) -> p a t", t=ZP)
        cvB = carve(4 * S).rearrange("p (a t) -> p a t", t=S)
        kst = carve(NPAIR * S).rearrange("p (a t) -> p a t", t=S)
        probsT = carve(3 * P)
        assert at[0] <= 3 * UN
        attC = qT[:, :, :].rearrange("p a t -> p (a t)")
        states = kT[:, 0:3, :].rearrange("p a t -> p (a t)").rearrange("p (n m e) -> p n m e", n=3, m=NPAIR)
        oC = vA[:, :, :].rearrange("p a t -> p (a t)")
        kst_tok = cvB[:, 0:2, :].rearrange("p a t -> p (a t)")
        sqC = zB[:, :, 0:S]
        lg = [hn[:, 0, 0:512], hn[:, 0, 512:1024], hn[:, 1, 0:512], hn[:, 1, 512:1024]]
        gate_s = hn[:, 0, :].rearrange("p (a t) -> p a t", t=S)
        prod_s = hn[:, 1, :].rearrange("p (a t) -> p a t", t=S)
        mix.close()

        den = ExitStack()
        dsilu = sb("dsilu", [P, 2, S], c=den)
        dh_hi = sb("dh_hi", [P, 2, S], F32R, c=den)
        dh_lo = sb("dh_lo", [P, 2, S], F32R, c=den)
        den.close()
        moe = ExitStack()
        pick = sb("pick", [P, TT, CAP], c=moe)
        pickT = sb("pickT", [P, S], F32R, c=moe)
        xs_hi = sb("xs_hi", [P, KD, CAP], F32R, c=moe)
        xs_lo = sb("xs_lo", [P, KD, CAP], F32R, c=moe)
        esilu = sb("esilu", [P, FC], c=moe)
        hid = sb("hid", [P, FC], c=moe)
        eh_hi = sb("eh_hi", [P, 2, CAP], F32R, c=moe)
        eh_lo = sb("eh_lo", [P, 2, CAP], F32R, c=moe)
        y_hi = sb("y_hi", [P, D], F32R, c=moe)
        y_lo = sb("y_lo", [P, D], F32R, c=moe)
        gsel = sb("gsel", [P, 1], c=moe)
        iota = sb("iota", [P, CAP], c=moe)
        lgt = sb("lgt", [P, TT, NE], c=moe)
        lgt2 = sb("lgt2", [P, TT, NE], c=moe)
        eq = sb("eq", [P, TT, NE], c=moe)
        cnt = sb("cnt", [P, TT, NE], c=moe)
        first = sb("first", [P, TT, NE], c=moe)
        second = sb("second", [P, TT, NE], c=moe)
        one8 = sb("one8", [P, NE], c=moe)
        v1 = sb("v1", [P, TT], c=moe)
        v2 = sb("v2", [P, TT], c=moe)
        wt1 = sb("wt1", [P, TT], c=moe)
        wt2 = sb("wt2", [P, TT], c=moe)
        chosen = sb("chosen", [P, TT, NE], c=moe)
        gates = sb("gates", [P, TT, NE], c=moe)
        rank = sb("rank", [P, TT, NE + 1], c=moe)
        most = sb("most", [P, 1], I32, c=moe)
        moe.close()

        ps = ctx.enter_context(nc.psum_tensor("ps", [P, 8, 512], F32))

        def banks(a, n=1):
            return ps[:, a:a + n, :].rearrange("p b n -> p (b n)")
        BX, BY, BT, BO = 4, 5, 6, 7

        x_loaded, prm_loaded, bf_loaded = sem("x_loaded"), sem("prm_loaded"), sem("bf_loaded")
        wsm_loaded, wa2_loaded, wr_loaded = sem("wsm_loaded"), sem("wa2_loaded"), sem("wr_loaded")
        gain_loaded, out_stored = sem("gain_loaded"), sem("out_stored")
        consts, cstep = sem("consts"), sem("cstep")
        prm_tr, prm_ready = sem("prm_tr"), sem("prm_ready")
        x_ready, n_sq, n_ms, n_rstd = sem("x_ready"), sem("n_sq"), sem("n_ms"), sem("n_rstd")
        n_hn, n_tr, n_hi, n_act = sem("n_hn"), sem("n_tr"), sem("n_hi"), sem("n_act")
        m_raw = [sem(f"m_raw{i}") for i in range(MRING)]
        m_hi, m_lo, m_used = sem("m_hi"), sem("m_lo"), sem("m_used")
        evac_act, evac_dve = sem("evac_act"), sem("evac_dve")
        s_split_hi, s_split = sem("s_split_hi"), sem("s_split")
        s_done, s_biased, s_aTc, s_ln, s_logf = sem("s_done"), sem("s_biased"), sem("s_aTc"), sem("s_ln"), sem("s_logf")
        s_FT, s_rows, s_frow, s_aT, s_fone = sem("s_FT"), sem("s_rows"), sem("s_frow"), sem("s_aT"), sem("s_fone")
        g_lin, g_neg, g_exp, g_ln, g_cum = sem("g_lin"), sem("g_neg"), sem("g_exp"), sem("g_ln"), sem("g_cum")
        g_es, g_in = sem("g_es"), sem("g_in")
        a_score, a_max, a_exp, a_prob = sem("a_score"), sem("a_max"), sem("a_exp"), sem("a_prob")
        a_tr, a_pt, a_pv, a_ohi, a_out = sem("a_tr"), sem("a_pt"), sem("a_pv"), sem("a_ohi"), sem("a_out")
        b_conv, b_y, b_hi, b_out = sem("b_conv"), sem("b_y"), sem("b_hi"), sem("b_out")
        g_att, g_attm, g_kstT, g_kst, g_kv = sem("g_att"), sem("g_attm"), sem("g_kstT"), sem("g_kst"), sem("g_kv")
        g_state, g_o, g_ocopy, g_ms, g_rstd = sem("g_state"), sem("g_o"), sem("g_ocopy"), sem("g_ms"), sem("g_rstd")
        g_on, g_oT, g_ohi, g_out = sem("g_on"), sem("g_oT"), sem("g_ohi"), sem("g_out")
        mg_sum, mg_hi, mg_out = sem("mg_sum"), sem("mg_hi"), sem("mg_out")
        dchain, achain = sem("dchain"), sem("achain")
        d_raw = [sem(f"d_raw{i}") for i in range(6)]
        d_hi = [sem(f"d_hi{t}") for t in range(3)]
        d_lo = [sem(f"d_lo{t}") for t in range(3)]
        d_used = [sem(f"d_used{t}") for t in range(3)]
        d_silu, d_h, d_hhi, d_hT = sem("d_silu"), sem("d_h"), sem("d_hhi"), sem("d_hT")
        e_raw = [sem(f"e_raw{i}") for i in range(9)]
        e_hi = [sem(f"e_hi{t}") for t in range(3)]
        e_lo = [sem(f"e_lo{t}") for t in range(3)]
        e_used = [sem(f"e_used{t}") for t in range(3)]
        e_silu, e_h, e_tr, e_hhi, e_hT = (sem("e_silu"), sem("e_h"), sem("e_tr"),
                                                sem("e_hhi"), sem("e_hT"))
        e_pick, e_again, e_gath, e_xhi, e_x = sem("e_pick"), sem("e_again"), sem("e_gath"), sem("e_xhi"), sem("e_x")
        e_pt, e_ptc, e_gsel, e_yhi, e_ylo = (sem("e_pt"), sem("e_ptc"), sem("e_gsel"),
                                                  sem("e_yhi"), sem("e_ylo"))
        e_sc, e_add = sem("e_sc"), sem("e_add")
        r_split_hi, r_split, r_logit, r_iota = sem("r_split_hi"), sem("r_split"), sem("r_logit"), sem("r_iota")
        r_v, r_e, r_chosen, r_cum, r_rank = sem("r_v"), sem("r_e"), sem("r_chosen"), sem("r_cum"), sem("r_rank")
        f_scaled = sem("f_scaled")

        block = ctx.enter_context(nc.Block())

        def last_use(n_units, ring, slot):
            return max(n for n in range(n_units) if n % ring == slot) + 1

        def per_set(s):
            return len(range(s, NF, 3))

        def before_units(l):
            return l * NUNIT

        w1e = moe_w1[0].rearrange("e (k p) n -> e p k n", p=P)
        w3e = moe_w3[0].rearrange("e (k p) n -> e p k n", p=P)
        w2e = moe_w2[0].rearrange("e (k p) n -> e p k n", p=P)

        @block.sync
        def _(sp):
            for t in range(TT):
                sp.dma_start(xres[:, t, :], x[0, t * P:(t + 1) * P, :]).then_inc(x_loaded, 16)

            def mixer_stream(l):
                n = before_units(l)
                for name, w, c0, ws, kt, _, _ in panels_of(l):
                    wv = w.rearrange("(k p) n -> p k n", p=P)
                    for j in range(kt // KW):
                        slot = n % MRING
                        if n >= before_units(l) + MRING:
                            sp.wait_ge(m_lo, n - MRING + 1)
                        elif l > 0:
                            sp.wait_ge(d_lo[slot % 3], NF)
                        sp.dma_start(raw[:, slot, :].rearrange("p (k n) -> p k n", k=KW),
                                     wv[:, j * KW:(j + 1) * KW, c0:c0 + UC]).then_inc(m_raw[slot], 16)
                        n += 1
            for l in range(L):
                wl_ = w_in[l].rearrange("(k p) n -> p k n", p=P)
                sp.dma_start(wsm[:, l, :, 0:HA], wl_[:, :, C_AF:C_AF + HA]).then_inc(wsm_loaded, 16)
                sp.dma_start(wsm[:, l, :, HA:SM], wl_[:, :, C_CA:C_CA + LR]).then_inc(wsm_loaded, 16)
            sp.dma_start(bf[:, :, :].rearrange("p l h -> p (l h)"),
                         b_f.rearrange("l h -> (l h)").rearrange("(a n) -> a n", a=1).to_broadcast([P, L * HA])).then_inc(bf_loaded, 16)
            sp.dma_start(wr[:, :, :], w_router[0].rearrange("(k p) n -> p k n", p=P)).then_inc(wr_loaded, 16)

            mixer_stream(0)

            w1d = ffn_w1[0].rearrange("(k p) n -> p k n", p=P)
            w3d = ffn_w3[0].rearrange("(k p) n -> p k n", p=P)
            w2d = ffn_w2[0].rearrange("(k p) n -> p k n", p=P)

            def dense_step(s, parity, has_gu, has_w2, peeled):
                for t in range(2 if has_gu else 0):
                    slot = parity * 3 + t
                    if peeled:
                        sp.wait_ge(m_lo, last_use(NUNIT, MRING, slot))
                    else:
                        sp.wait_ge(d_lo[t], s - 1)
                    dst = raw[:, slot, :].rearrange("p (k w n) -> p k w n", k=KW, w=2)
                    sp.dma_start(dst[:, :, 0, :], w1d[:, t * KW:(t + 1) * KW, ds(s * FC, FC)]).then_inc(d_raw[slot], 16)
                    sp.dma_start(dst[:, :, 1, :], w3d[:, t * KW:(t + 1) * KW, ds(s * FC, FC)]).then_inc(d_raw[slot], 16)
                if has_w2:
                    slot = parity * 3 + 2
                    if peeled:
                        sp.wait_ge(m_lo, last_use(NUNIT, MRING, slot))
                    else:
                        sp.wait_ge(d_lo[2], s - 2)
                    sp.dma_start(raw[:, slot, :].rearrange("p (k n) -> p k n", k=2),
                                 w2d[:, ds((s - 1) * 2, 2), :]).then_inc(d_raw[slot], 16)

            dense_step(0, 0, True, False, True)
            dense_step(1, 1, True, True, True)
            for t in range(2):
                sp.wait_ge(d_lo[t], 1)
                dst = raw[:, t, :].rearrange("p (k w n) -> p k w n", k=KW, w=2)
                sp.dma_start(dst[:, :, 0, :], w1d[:, t * KW:(t + 1) * KW, 2 * FC:3 * FC]).then_inc(d_raw[t], 16)
                sp.dma_start(dst[:, :, 1, :], w3d[:, t * KW:(t + 1) * KW, 2 * FC:3 * FC]).then_inc(d_raw[t], 16)
            sp.wait_ge(m_lo, last_use(NUNIT, MRING, 2))
            sp.dma_start(raw[:, 2, :].rearrange("p (k n) -> p k n", k=2), w2d[:, 2:4, :]).then_inc(d_raw[2], 16)
            with sp.Fori(0, (NF - 3) // 2) as j:
                dense_step(2 * j + 3, 1, True, True, False)
                dense_step(2 * j + 4, 0, True, True, False)
            dense_step(NF, 1, False, True, False)

            mixer_stream(1)

            def expert_gu(e, ew, f, fs, fresh):
                for t in range(2):
                    slot = 3 * t + fs
                    if not fresh:
                        prev = NF * e + f - 3 + 1 if not isinstance(f, int) or f >= 3 else \
                            NF * (e - 1) + 3 * (per_set(fs) - 1) + fs + 1
                        sp.wait_ge(e_lo[t], prev)
                    dst = raw[:, slot, :].rearrange("p (k w n) -> p k w n", k=KW, w=2)
                    for w, src in ((0, w1e), (1, w3e)):
                        sp.dma_start(dst[:, :, w, :],
                                     src[ds(ew, 1), :, t * KW:(t + 1) * KW, ds(f * FC, FC)].rearrange(
                                         "a p k n -> p (a k) n")).then_inc(e_raw[slot], 16)

            def expert_w2(e, ew, f, fs, fresh):
                slot = 6 + fs
                if not fresh:
                    prev = NF * e + f - 3 + 1 if not isinstance(f, int) or f >= 3 else \
                        NF * (e - 1) + 3 * (per_set(fs) - 1) + fs + 1
                    sp.wait_ge(e_lo[2], prev)
                sp.dma_start(raw[:, slot, :].rearrange("p (k n) -> p k n", k=2),
                             w2e[ds(ew, 1), :, ds(f * 2, 2), :].rearrange("a p k n -> p (a k) n")).then_inc(e_raw[slot], 16)

            def expert_stream(e, ew, opening):
                fresh = isinstance(e, int) and e == 0
                for f in range(5):
                    expert_gu(e, ew, f, f % 3, fresh and f < 3)
                    if f == 2 and fresh:
                        sp.wait_ge(x_ready, 3)
                    if f >= 2:
                        expert_w2(e, ew, f - 2, f - 2, fresh)
                    elif not opening:
                        expert_w2(e - 1, ew - 1, NF - 2 + f, (NF - 2 + f) % 3, False)
                with sp.Fori(0, (NF - 5) // 3) as j:
                    for i in range(3):
                        expert_gu(e, ew, 3 * j + 5 + i, (i + 2) % 3, False)
                        expert_w2(e, ew, 3 * j + 3 + i, i, False)

            def experts_stream(k):
                expert_stream(NE * k, 0, True)
                with sp.Fori(NE * k + 1, NE * (k + 1)) as e:
                    expert_stream(e, e - NE * k, False)
                for f in (NF - 2, NF - 1):
                    expert_w2(NE * (k + 1) - 1, NE - 1, f, f % 3, False)

            sp.wait_ge(m_lo, L * NUNIT)
            experts_stream(0)
            sp.wait_ge(r_rank, 1)
            fullest = sp.value_load(most[0:1, 0:1])
            with sp.If(fullest > CAP):
                experts_stream(1)

            sp.wait_ge(f_scaled, 2)
            for t in range(TT):
                sp.dma_start(out[0, t * P:(t + 1) * P, :], hn[:, t, :]).then_inc(out_stored, 16)
            sp.wait_ge(out_stored, 16 * TT)

        @block.gpsimd
        def _(pool):
            for src, r0 in ((conv_w.rearrange("l t (c p) -> (l t c) p", p=P), R_CONV),
                            (b_a.rearrange("l (c p) -> (l c) p", p=P), R_BA),
                            (g_gla.rearrange("l (c p) -> (l c) p", p=P), R_GG),
                            (b_gate.rearrange("l (c p) -> (l c) p", p=P), R_BG)):
                pool.dma_start(hn[r0:r0 + src.shape[0], 0, 0:P], src).then_inc(prm_loaded, 16)
            step = [0]

            def link(ins):
                step[0] += 1
                ins.then_inc(cstep, 1)
                pool.wait_ge(cstep, step[0])
            link(pool.memset(ident[:, :], 0.0))
            link(pool.affine_select(out=ident[:, :], in_=ident[:, :], compare_op=ALU.not_equal, fill=1.0,
                                    base=0, pattern=[[-1, P]], channel_multiplier=1))
            pool.memset(mhalf[:, :], -0.5).then_inc(consts, 1)
            link(pool.memset(tri[:, :], 1.0))
            link(pool.memset(tri[:, 0:P], 0.0))
            link(pool.affine_select(out=tri[:, P:2 * P], in_=tri[:, P:2 * P], compare_op=ALU.is_ge, fill=0.0,
                                    base=0, pattern=[[1, P]], channel_multiplier=-1))
            link(pool.memset(cmask[:, :], 0.0))
            link(pool.affine_select(out=cmask[:, P:2 * P], in_=cmask[:, P:2 * P], compare_op=ALU.is_ge, fill=NEG,
                                    base=0, pattern=[[-1, P]], channel_multiplier=1))
            link(pool.memset(gmask[:, :], 1.0))
            link(pool.affine_select(out=gmask[:, :], in_=gmask[:, :], compare_op=ALU.is_ge, fill=0.0,
                                    base=0, pattern=[[1, P]], channel_multiplier=-1))
            link(pool.affine_select(out=gmask[:, CH:P], in_=gmask[:, CH:P], compare_op=ALU.is_ge, fill=0.0,
                                    base=-CH, pattern=[[0, P - CH]], channel_multiplier=1))
            link(pool.memset(keep[:, :], 1.0))
            for c in range(S // CH):
                link(pool.memset(keep[:, c * CH:c * CH + 1], 0.0))
            pool.memset(zrow[:, :], 0.0).then_inc(consts, 1)
            pool.memset(f_query[:, :, :], 1.0).then_inc(s_fone, 1)
            pool.memset(f_key[:, :, :], 1.0).then_inc(s_fone, 1)
            pool.wait_ge(s_fone, 2)

            def inverse_root(n):
                gain = (g_mix if n % 2 == 0 else g_ffn)[n // 2:n // 2 + 1, :] if n < 2 * L else \
                    g_final.rearrange("(a n) -> a n", a=1)
                if n == 1 or n == 3:
                    pool.wait_ge(mg_out, n // 2 + 1)
                elif n > 0:
                    pool.wait_ge(n_hn, TT * n)
                pool.dma_start(gains, gain.to_broadcast([P, D])).then_inc(gain_loaded, 16)
                pool.wait_ge(n_ms, n + 1)
                pool.tensor_tensor(rstd[:, :], sumsq[:, :], mhalf[:, 0:TT], ALU.pow).then_inc(n_rstd, 1)

            for l in range(L):
                inverse_root(2 * l)
                if l > 0:
                    pool.wait_ge(g_lin, l)
                pool.dma_start(wa2[:, :], w_a2[l]).then_inc(wa2_loaded, 16)
                pool.wait_ge(s_rows, 2 * (l + 1))
                for j in range(2):
                    pool.dma_start(f_query[0:97:32, j, :], f_rows[4 * j:4 * j + 4, 0, :]).then_inc(s_frow, 16)
                    pool.dma_start(f_key[1:98:32, j, :], f_rows[4 * j:4 * j + 4, 1, :]).then_inc(s_frow, 16)
                pool.wait_ge(g_ms, l + 1)
                pool.tensor_tensor(ors[:, :], oss[:, :], mhalf[:, 0:2 * HC], ALU.pow).then_inc(g_rstd, 1)
                inverse_root(2 * l + 1)
            pool.wait_ge(g_cum, 2 * L)
            pool.iota(iota_i, pattern=[[1, CAP]], base=0, channel_multiplier=0).then_inc(r_iota, 1)
            inverse_root(2 * L)

        @block.scalar
        def _(act):
            chain = [0]

            def link(ins):
                chain[0] += 1
                ins.then_inc(achain, 1)
                act.wait_ge(achain, chain[0])

            def square_sums(n):
                if n == 0:
                    act.wait_ge(x_loaded, 16 * TT)
                else:
                    act.wait_ge(x_ready, n)
                if n == 0:
                    act.wait_ge(prm_ready, 1)
                for t in range(TT):
                    act.activation(hn[:, t, :], xres[:, t, :], ACT.Square, accum_out=sumsq[:, t:t + 1]).then_inc(n_sq, 1)

            def act_hi_of(n):
                for b in range(4):
                    act.wait_ge(n_tr, 4 * n + b + 1)
                    act.copy(act_hi[:, 2 * b:2 * b + 2, :].rearrange("p a t -> p (a t)"), banks(b)).then_inc(n_hi, 1)

            def mixer(l):
                n = [before_units(l)]
                G0 = l * NPAN

                def split_panel(p):
                    for _ in range(panels_of(l)[p][4] // KW):
                        u = n[0]
                        act.wait_ge(m_raw[u % MRING], 16 * (u // MRING + 1))
                        if u >= before_units(l) + SRING:
                            act.wait_ge(m_used, u - SRING + 1)
                        elif l > 0:
                            act.wait_ge(d_used[u % SRING], NF)
                        act.copy(w_hi[:, u % SRING, :], raw[:, u % MRING, :]).then_inc(m_hi, 1)
                        n[0] += 1

                def done(p):
                    act.wait_ge(m_used, units_until(G0 + p))

                split_panel(0)
                act.wait_ge(s_biased, l + 1)
                link(act.activation(lsa[:, 1, :], lsa[:, 1, :], ACT.Exp))
                act.activation(lsa[:, 1, :], lsa[:, 1, :], ACT.Ln, bias=1.0).then_inc(s_ln, 1)
                split_panel(1)
                act.wait_ge(s_aT, l + 1)
                act.copy(aT, ps[0:LR, BT, 0:S]).then_inc(s_aTc, 1)
                act.wait_ge(s_FT, l + 1)
                act.copy(f_rows[:, 0, :], ps[0:HA, BY, 0:S]).then_inc(s_rows, 1)
                act.mul(f_rows[:, 1, :], ps[0:HA, BY, 0:S], -1.0).then_inc(s_rows, 1)
                act.wait_ge(g_neg, l + 1)
                link(act.activation(lg[2], lg[2], ACT.Exp))
                act.activation(lg[2], lg[2], ACT.Ln, bias=1.0).then_inc(g_ln, 1)
                done(0)
                act.copy(kT[:, :, :].rearrange("p a t -> p (a t)"), banks(0 if G0 % 2 == 0 else 2, 2)).then_inc(evac_act, 1)
                split_panel(2)
                act.wait_ge(g_cum, 2 * (l + 1))
                cumf = cum[:, :, :].rearrange("p a t -> p (a t)")
                act.activation(lg[0], cumf, ACT.Exp, scale=1.0 / 16).then_inc(g_es, 1)
                act.activation(lg[1], cumf, ACT.Exp, scale=-1.0 / 16).then_inc(g_es, 1)
                act.activation(lg[3], lg[3], ACT.Exp, scale=1.0 / 16).then_inc(g_es, 1)
                act.activation(decay[:, :, :], cum[:, :, CH - 1::CH], ACT.Exp, scale=1.0 / 16).then_inc(g_es, 1)
                done(1)
                act.mul(qT[:, :, :].rearrange("p a t -> p (a t)"), banks(2 if G0 % 2 == 0 else 0, 2), DH ** -0.5).then_inc(evac_act, 1)

                def evacuate(p):
                    name = NAMES[p]
                    bank = ((G0 + p) % 2) * 2
                    if EVAC[p] != "act":
                        return
                    done(p)
                    src = banks(bank, 2)
                    if name == "v":
                        act.copy(vA[:, :, :].rearrange("p a t -> p (a t)"), src).then_inc(evac_act, 1)
                    elif name == "cqk":
                        act.copy(cqkT.rearrange("p a t -> p (a t)"), src).then_inc(evac_act, 1)
                    elif name == "cv":
                        act.copy(vC.rearrange("p a t -> p (a t)"), src).then_inc(evac_act, 1)
                    elif name == "cr":
                        act.activation(rC.rearrange("p a t -> p (a t)"), src, ACT.Silu).then_inc(evac_act, 1)
                    elif name == "u":
                        act.copy(zB[:, :, 2:ZP], src.rearrange("p (a t) -> p a t", t=S)).then_inc(evac_act, 1)
                    else:
                        br, half = int(name[4]), int(name[5])
                        if NAMES[p] == "gate10":
                            act.wait_ge(g_in, l + 1)
                        else:
                            act.wait_ge(evac_dve, evacuated(G0 + p - 1, "dve"))
                        for c in range(4):
                            col = R_BG + l * 3 * KD + br * KD + half * 4 + c
                            ins = act.activation(gate_s[:, c, :], src[:, c * S:(c + 1) * S], ACT.Sigmoid,
                                                 bias=prm[:, col:col + 1])
                        ins.then_inc(evac_act, 1)

                def exps(h):
                    a = l * HA + h
                    act.wait_ge(a_max, a + 1)
                    act.activation(probs[:, h % 2, 0:P], probs[:, h % 2, 0:P], ACT.Exp, bias=nmx[:, 2 * h:2 * h + 1],
                                   accum_out=sm[:, 2 * h:2 * h + 1])
                    act.activation(probs[:, h % 2, P:3 * P], probs[:, h % 2, P:3 * P], ACT.Exp,
                                   bias=nmx[:, 2 * h + 1:2 * h + 2], accum_out=sm[:, 2 * h + 1:2 * h + 2]).then_inc(a_exp, 1)

                def probs_T(h):
                    a = l * HA + h
                    act.wait_ge(a_tr, a + 1)
                    if h > 0:
                        act.wait_ge(a_pv, a)
                    act.copy(probsT, ps[:, BT, 0:3 * P]).then_inc(a_pt, 1)

                def head_out(h):
                    if h % 2 == 1:
                        act.wait_ge(a_pv, l * HA + h + 1)
                        act.copy(oa_hi[:, h // 2, :], ps[:, BO, 0:S]).then_inc(a_ohi, 1)

                for p in range(2, NPAN):
                    if p + 1 < NPAN:
                        split_panel(p + 1)
                    if 0 <= p - HS < HA:
                        exps(p - HS)
                    if 0 <= p - HS - 1 < HA:
                        probs_T(p - HS - 1)
                    if 0 <= p - HS - 2 < HA:
                        head_out(p - HS - 2)
                    if NAMES[p] == "proj11":
                        act.wait_ge(g_kstT, l + 1)
                        act.copy(kst_tok, banks(BT)).then_inc(g_kst, 1)
                    if NAMES[p] == "proj00":
                        act.wait_ge(g_o, l + 1)
                        act.copy(oC, banks(BX, 2)).then_inc(g_ocopy, 1)
                    if NAMES[p] == "proj01":
                        act.wait_ge(g_oT, l + 1)
                        for h in range(HC):
                            col = R_GG + l * HC + h
                            act.activation(obc_hi[:, h, :], banks(BT, 2)[:, h * S:(h + 1) * S], ACT.Copy,
                                           scale=prm[:, col:col + 1]).then_inc(g_ohi, 1)
                    evacuate(p)
                    if NAMES[p] == "bg":
                        act.wait_ge(b_y, l + 1)
                        act.copy(obc_hi[:, :, :], cvB).then_inc(b_hi, 1)
                    if NAMES[p] == "proj21":
                        act.wait_ge(mg_sum, l + 1)
                        act.copy(act_hi[:, :, :], merged[:, :, :]).then_inc(mg_hi, 1)

            act.wait_ge(prm_tr, 1)
            act.copy(prm[:, 0:NPRM], ps[:, BX, 0:NPRM]).then_inc(prm_ready, 1)
            square_sums(0)
            act_hi_of(0)
            mixer(0)
            square_sums(1)
            act_hi_of(1)

            def dhi(t, slot, arrivals, used, first=False):
                act.wait_ge(d_raw[slot], arrivals)
                if first:
                    act.wait_ge(m_used, last_use(NUNIT, SRING, t))
                else:
                    act.wait_ge(d_used[t], used)
                act.copy(w_hi[:, t, :], raw[:, slot, :]).then_inc(d_hi[t], 1)

            def dense_hidden(s, parity, first):
                act.wait_ge(d_used[1], s + 1)
                if not first:
                    act.wait_ge(d_hT, s)
                act.activation(dsilu[:, :, :].rearrange("p a t -> p (a t)"), banks(2 * parity), ACT.Silu).then_inc(d_silu, 1)

            def dense_hidden_hi(s, first):
                act.wait_ge(d_h, s + 1)
                if not first:
                    act.wait_ge(d_used[2], s)
                act.copy(dh_hi[:, :, :], dsilu[:, :, :]).then_inc(d_hhi, 1)

            def dense_step(q, parity, up, down):
                s = 2 * q + parity
                if up:
                    for t in range(2):
                        dhi(t, 3 * parity + t, 32 * (q + 1), s, isinstance(s, int) and s == 0)
                if down:
                    dense_hidden(s - 1, 1 - parity, isinstance(s, int) and s == 1)
                    dhi(2, 3 * parity + 2, 16 * (q + parity), s - 1, isinstance(s, int) and s == 1)
                    dense_hidden_hi(s - 1, isinstance(s, int) and s == 1)

            dense_step(0, 0, True, False)
            dense_step(0, 1, True, True)
            with act.Fori(1, NF // 2) as q:
                dense_step(q, 0, True, True)
                dense_step(q, 1, True, True)
            dense_step(NF // 2, 0, True, True)
            dense_step(NF // 2, 1, False, True)

            square_sums(2)
            act_hi_of(2)
            mixer(1)
            square_sums(3)
            act_hi_of(3)

            def ehi(t, fs, arrivals, used, first=False):
                act.wait_ge(e_raw[3 * t + fs], arrivals)
                if first:
                    act.wait_ge(m_used, L * NUNIT)
                else:
                    act.wait_ge(e_used[t], used)
                act.copy(w_hi[:, t, :], raw[:, 3 * t + fs, :]).then_inc(e_hi[t], 1)

            def step_gu(e, f, q, fs, first=False):
                for t in range(2):
                    ehi(t, fs, 32 * (per_set(fs) * e + q + 1), NF * e + f, first)

            def step_w2(e, f, q, fs, first=False):
                ehi(2, fs, 16 * (per_set(fs) * e + q + 1), NF * e + f + 1)

            def silu_of(e, f, bank):
                act.wait_ge(e_used[1], NF * e + f + 1)
                act.wait_ge(e_h, NF * e + f + 2)
                act.activation(esilu[:, :], ps[:, bank, 0:FC], ACT.Silu).then_inc(e_silu, 1)

            def hidden_hi(e, f):
                act.wait_ge(e_tr, NF * e + f + 2)
                act.copy(eh_hi[:, :, :].rearrange("p a t -> p (a t)"), ps[:, 3, 0:2 * CAP]).then_inc(e_hhi, 1)

            def tokens_hi(e):
                act.wait_ge(e_gath, e + 1)
                act.copy(xs_hi[:, :, :].rearrange("p a t -> p (a t)"), banks(4, 2)).then_inc(e_xhi, 1)

            def output_hi(e):
                act.wait_ge(e_used[2], NF * (e + 1) + 1)
                act.wait_ge(e_gsel, e + 1)
                act.activation(y_hi[:, :], banks(6, 2), ACT.Copy, scale=gsel[:, 0:1]).then_inc(e_yhi, 1)

            def expert(e, opening):
                fresh = isinstance(e, int) and e == 0
                if not fresh:
                    step_gu(e, 0, 0, 0)
                if not opening:
                    silu_of(e - 1, NF - 1, (NF - 1) % 3)
                tokens_hi(e)
                if not opening:
                    step_w2(e - 1, NF - 2, 3, 0)
                    hidden_hi(e - 1, NF - 2)
                for f in range(1, 5):
                    step_gu(e, f, f // 3, f % 3, fresh and f < 1)
                    silu_of(e, f - 1, (f - 1) % 3)
                    if f == 1:
                        if not opening:
                            step_w2(e - 1, NF - 1, 3, 1)
                            hidden_hi(e - 1, NF - 1)
                        continue
                    step_w2(e, f - 2, 0, f - 2)
                    hidden_hi(e, f - 2)
                    if f == 2 and not opening:
                        output_hi(e - 1)
                act.wait_ge(e_pt, e + 1)
                act.copy(pickT[:, :], ps[:, 4, 0:S]).then_inc(e_ptc, 1)
                with act.Fori(0, (NF - 5) // 3) as j:
                    for i in range(3):
                        step_gu(e, 3 * j + 5 + i, j + (5 + i) // 3, (2 + i) % 3)
                        silu_of(e, 3 * j + 4 + i, (1 + i) % 3)
                        step_w2(e, 3 * j + 3 + i, j + 1, i)
                        hidden_hi(e, 3 * j + 3 + i)

            def expert_pass(k):
                expert(NE * k, True)
                with act.Fori(NE * k + 1, NE * (k + 1)) as e:
                    expert(e, False)
                e = NE * (k + 1) - 1
                silu_of(e, NF - 1, (NF - 1) % 3)
                for f in (NF - 2, NF - 1):
                    step_w2(e, f, 3, f % 3)
                    hidden_hi(e, f)
                output_hi(e)

            step_gu(0, 0, 0, 0, True)
            act.wait_ge(r_v, 1)
            act.activation(wt2[:, :], wt2[:, :], ACT.Exp).then_inc(r_e, 1)

            expert_pass(0)
            act.wait_ge(r_rank, 1)
            fullest = act.value_load(most[0:1, 0:1])
            with act.If(fullest > CAP):
                expert_pass(1)
            square_sums(4)

        @block.vector
        def _(dve):
            chain = [0]

            def link(ins):
                chain[0] += 1
                ins.then_inc(dchain, 1)
                dve.wait_ge(dchain, chain[0])

            def f32(ap):
                return ap.bitcast(F32)

            def norm(n, transposed=True, final=False):
                dve.wait_ge(n_sq, TT * (n + 1))
                dve.tensor_scalar(sumsq[:, :], sumsq[:, :], 1.0 / D, EPS, ALU.mult, ALU.add).then_inc(n_ms, 1)
                dve.wait_ge(n_rstd, n + 1)
                dve.wait_ge(gain_loaded, 16 * (n + 1))
                for t in range(TT):
                    dve.scalar_tensor_tensor(out=hn[:, t, :], in0=xres[:, t, :], scalar=rstd[:, t:t + 1], in1=gains,
                                             op0=ALU.mult, op1=ALU.mult).then_inc(f_scaled if final else n_hn, 1)
                if final:
                    return
                for b in range(4):
                    dve.wait_ge(n_hi, 4 * n + b + 1)
                    o = act_lo[:, 2 * b:2 * b + 2, :].rearrange("p a t -> p (a t)")
                    h = f32(act_hi[:, 2 * b:2 * b + 2, :]).rearrange("p a t -> p (a t)")
                    dve.tensor_tensor(o, banks(b), h, ALU.subtract).then_inc(n_act, 1)

            def log_sigmoid_prep(lin, mn, neg):
                link(dve.tensor_scalar(mn, lin, 0.0, None, ALU.min))
                return dve.scalar_tensor_tensor(out=neg, in0=mn, scalar=2.0, in1=lin, op0=ALU.mult, op1=ALU.subtract)

            def mixer(l):
                n = [before_units(l)]
                G0 = l * NPAN

                def split_panel(p):
                    for _ in range(panels_of(l)[p][4] // KW):
                        u = n[0]
                        dve.wait_ge(m_hi, u + 1)
                        dve.tensor_tensor(w_lo[:, u % SRING, :], raw[:, u % MRING, :], f32(w_hi[:, u % SRING, :]),
                                          ALU.subtract).then_inc(m_lo, 1)
                        n[0] += 1

                dve.wait_ge(wsm_loaded, 32 * L)
                if l > 0:
                    dve.wait_ge(s_done, l)
                link(dve.tensor_copy(wsm_hi[:, :, :], wsm[:, l, :, :]))
                dve.tensor_tensor(wsm_lo[:, :, :], wsm[:, l, :, :], f32(wsm_hi[:, :, :]), ALU.subtract).then_inc(s_split, 1)
                split_panel(0)
                dve.wait_ge(s_done, l + 1)
                dve.wait_ge(bf_loaded, 16)
                small = ps[:, BO, 0:TT * SM].rearrange("p (t c) -> p t c", c=SM)
                link(dve.tensor_copy(logf[:, :, :], small))
                link(dve.tensor_tensor(logf[:, :, 0:HA], logf[:, :, 0:HA],
                                       bf[:, l:l + 1, :].to_broadcast([P, TT, HA]), ALU.add))
                mn = lsa[:, 0, :].rearrange("p (t h) -> p t h", h=HA)
                ng = lsa[:, 1, :].rearrange("p (t h) -> p t h", h=HA)
                log_sigmoid_prep(logf[:, :, 0:HA], mn, ng).then_inc(s_biased, 1)
                dve.wait_ge(s_ln, l + 1)
                dve.tensor_tensor(logf[:, :, 0:HA], mn, ng, ALU.subtract).then_inc(s_logf, 1)
                split_panel(1)
                dve.wait_ge(g_lin, l + 1)
                for m in range(NPAIR):
                    col = R_BA + l * NPAIR + m
                    link(dve.tensor_scalar(lg[0][:, m * S:(m + 1) * S], ps[:, BX, m * S:(m + 1) * S],
                                           prm[:, col:col + 1], None, ALU.add))
                log_sigmoid_prep(lg[0], lg[1], lg[2]).then_inc(g_neg, 1)
                dve.wait_ge(g_ln, l + 1)
                link(dve.tensor_tensor(lg[0], lg[1], lg[2], ALU.subtract))
                for m in range(NPAIR):
                    dve.tensor_tensor_scan(out=cum[:, m, :], data0=keep[:, :], data1=lg[0][:, m * S:(m + 1) * S],
                                           initial=0.0, op0=ALU.mult, op1=ALU.add).then_inc(dchain, 1)
                chain[0] += NPAIR
                dve.wait_ge(dchain, chain[0])
                c4 = cum[:, :, :].rearrange("p m (c t) -> p m c t", t=CH)
                for m in range(NPAIR):
                    dve.tensor_tensor(lg[3][:, m * S:(m + 1) * S].rearrange("p (c t) -> p c t", t=CH),
                                      c4[:, m, :, CH - 1:CH].to_broadcast([P, S // CH, CH]), c4[:, m, :, :],
                                      ALU.subtract).then_inc(g_cum, 1)
                split_panel(2)

                def evacuate(p):
                    name = NAMES[p]
                    bank = ((G0 + p) % 2) * 2
                    if EVAC[p] != "dve":
                        return
                    dve.wait_ge(m_used, units_until(G0 + p))
                    src = banks(bank, 2)
                    if name == "cg":
                        dve.wait_ge(evac_act, evacuated(G0 + NAMES.index("u"), "act"))
                        dve.memset(zB[:, :, 0:2], 0.0)
                        link(dve.tensor_tensor(zB[:, :, 2:ZP], zB[:, :, 2:ZP], src.rearrange("p (a t) -> p a t", t=S),
                                               ALU.mult))
                        dve.sem_inc(evac_dve, 1)
                        for tap in range(3):
                            for c in range(4):
                                col = R_CONV + (l * 3 + tap) * 4 + c
                                w = prm[:, col:col + 1]
                                if tap == 0:
                                    link(dve.tensor_scalar(cvB[:, c, :], zB[:, c, 0:S], w, None, ALU.mult))
                                else:
                                    link(dve.scalar_tensor_tensor(out=cvB[:, c, :], in0=zB[:, c, tap:tap + S], scalar=w,
                                                                  in1=cvB[:, c, :], op0=ALU.mult, op1=ALU.add))
                    elif name == "bg":
                        cvf = cvB.rearrange("p a t -> p (a t)")
                        link(dve.tensor_tensor(cvf, cvf, src, ALU.mult))
                        dve.sem_inc(evac_dve, 1)
                        dve.sem_inc(b_y, 1)
                        dve.wait_ge(b_hi, l + 1)
                        dve.tensor_tensor(obc_lo[:, :, :], cvB, f32(obc_hi[:, :, :]), ALU.subtract).then_inc(b_out, 1)
                    elif name.startswith("proj"):
                        half = int(name[5])
                        dve.wait_ge(evac_act, evacuated(G0 + p - 1, "act"))
                        mh = merged[:, half * 4:half * 4 + 4, :].rearrange("p a t -> p (a t)")
                        gs = gate_s.rearrange("p a t -> p (a t)")
                        if name[4] == "1":
                            dve.tensor_tensor(mh, gs, src, ALU.mult).then_inc(evac_dve, 1)
                        else:
                            pr = prod_s.rearrange("p a t -> p (a t)")
                            link(dve.tensor_tensor(pr, gs, src, ALU.mult))
                            dve.sem_inc(evac_dve, 1)
                            ins = dve.tensor_tensor(mh, mh, pr, ALU.add)
                            link(ins)
                    else:
                        half = int(name[3])
                        ins = dve.tensor_tensor(xres[:, :, half * UC:(half + 1) * UC],
                                                xres[:, :, half * UC:(half + 1) * UC],
                                                src.rearrange("p (a t) -> p a t", t=UC), ALU.add)
                        link(ins)
                        dve.sem_inc(evac_dve, 1)

                def scores(h):
                    a = l * HA + h
                    dve.wait_ge(a_score, a + 1)
                    if h >= 2:
                        dve.wait_ge(a_tr, a - 1)
                    bank = BX + h % 2
                    dve.tensor_tensor_reduce(out=probs[:, h % 2, 0:P], in0=ps[:, bank, 0:P], in1=cmask[:, P:2 * P],
                                             scale=1.0, scalar=-3e38, op0=ALU.add, op1=ALU.max,
                                             accum_out=mx[:, 2 * h:2 * h + 1])
                    link(dve.tensor_tensor_reduce(out=probs[:, h % 2, P:3 * P], in0=ps[:, bank, P:3 * P],
                                                  in1=cmask[:, :], scale=1.0, scalar=-3e38, op0=ALU.add, op1=ALU.max,
                                                  accum_out=mx[:, 2 * h + 1:2 * h + 2]))
                    dve.tensor_scalar(nmx[:, 2 * h:2 * h + 2], mx[:, 2 * h:2 * h + 2], -1.0, None,
                                      ALU.mult).then_inc(a_max, 1)

                def normalise(h):
                    a = l * HA + h
                    dve.wait_ge(a_exp, a + 1)
                    link(dve.reciprocal(rs[:, 2 * h:2 * h + 2], sm[:, 2 * h:2 * h + 2]))
                    dve.tensor_scalar(probs[:, h % 2, 0:P], probs[:, h % 2, 0:P], rs[:, 2 * h:2 * h + 1], None, ALU.mult)
                    dve.tensor_scalar(probs[:, h % 2, P:3 * P], probs[:, h % 2, P:3 * P], rs[:, 2 * h + 1:2 * h + 2],
                                      None, ALU.mult).then_inc(a_prob, 1)

                def head_out(h):
                    if h % 2 == 1:
                        dve.wait_ge(a_ohi, l * HA // 2 + h // 2 + 1)
                        dve.tensor_tensor(oa_lo[:, h // 2, :], ps[:, BO, 0:S], f32(oa_hi[:, h // 2, :]),
                                          ALU.subtract).then_inc(a_out, 1)

                for p in range(2, NPAN):
                    if 0 <= p - HS < HA:
                        scores(p - HS)
                    if p + 1 < NPAN:
                        split_panel(p + 1)
                    if 0 <= p - HS < HA:
                        normalise(p - HS)
                    if 0 <= p - HS - 2 < HA:
                        head_out(p - HS - 2)
                    if NAMES[p] == "cqk":
                        dve.wait_ge(evac_act, evacuated(G0 + p, "act"))
                        dve.wait_ge(g_es, 4 * (l + 1))
                        cq = cqkT[:, 0:NPAIR, :].rearrange("p a t -> p (a t)")
                        ck = cqkT[:, NPAIR:2 * NPAIR, :].rearrange("p a t -> p (a t)")
                        link(dve.tensor_tensor(kst.rearrange("p a t -> p (a t)"), ck, lg[3], ALU.mult))
                        dve.tensor_tensor(ck, ck, lg[1], ALU.mult)
                        link(dve.scalar_tensor_tensor(out=cq, in0=cq, scalar=DK ** -0.5, in1=lg[0], op0=ALU.mult,
                                                      op1=ALU.mult))
                        dve.sem_inc(g_in, 1)
                    if NAMES[p] == "proj11":
                        dve.wait_ge(g_att, l + 1)
                        m3 = gmask[:, :].rearrange("p (a q) -> p a q", a=1).to_broadcast([P, 8, P])
                        dve.tensor_tensor(attC.rearrange("p (a q) -> p a q", q=P),
                                          banks(BX, 2).rearrange("p (a q) -> p a q", q=P), m3, ALU.mult).then_inc(g_attm, 1)
                    if NAMES[p] == "gate00":
                        dve.wait_ge(g_kv, l + 1)
                        link(dve.tensor_copy(states[:, 0, :, :].rearrange("p m e -> p (m e)"), ps[:, BO, 0:NPAIR * DV]))
                        for c in range(1, 3):
                            src = ps[:, BO, 256:512] if c == 2 else ps[:, BT, 0:256]
                            for m in range(NPAIR):
                                ins = dve.scalar_tensor_tensor(out=states[:, c, m, :], in0=states[:, c - 1, m, :],
                                                               scalar=decay[:, m, c:c + 1],
                                                               in1=src[:, m * DV:(m + 1) * DV], op0=ALU.mult, op1=ALU.add)
                            link(ins)
                        dve.sem_inc(g_state, 1)
                    if NAMES[p] == "gate01":
                        dve.wait_ge(g_ocopy, l + 1)
                        o3 = oC.rearrange("p (a e) -> p a e", e=DV)
                        s3 = sqC.rearrange("p a (b e) -> p a b e", e=DV)
                        link(dve.tensor_tensor(sqC, oC.rearrange("p (a t) -> p a t", t=S),
                                               oC.rearrange("p (a t) -> p a t", t=S), ALU.mult))
                        link(dve.tensor_reduce(out=oss[:, :], in_=s3, axis=AX.X, op=ALU.add))
                        dve.tensor_scalar(oss[:, :], oss[:, :], 1.0 / DV, EPS, ALU.mult, ALU.add).then_inc(g_ms, 1)
                        dve.wait_ge(g_rstd, l + 1)
                        link(dve.tensor_tensor(o3, o3, ors[:, :].rearrange("p (a b) -> p a b", b=1).to_broadcast([P, 8, DV]),
                                               ALU.mult))
                        r5 = rC.rearrange("p t (m r e) -> p t m r e", m=NPAIR, r=2)
                        o5 = oC.rearrange("p (r t m e) -> p r t m e", r=2, t=TT, m=NPAIR)
                        for r in range(2):
                            for t in range(TT):
                                ins = dve.tensor_tensor(o5[:, r, t, :, :], o5[:, r, t, :, :], r5[:, t, :, r, :], ALU.mult)
                        ins.then_inc(g_on, 1)
                    if NAMES[p] == "proj01":
                        for h in range(HC):
                            col = R_GG + l * HC + h
                            dve.wait_ge(g_ohi, l * HC + h // 2 * 2 + 2)
                            dve.scalar_tensor_tensor(out=obc_lo[:, h, :], in0=banks(BT, 2)[:, h * S:(h + 1) * S],
                                                     scalar=prm[:, col:col + 1], in1=f32(obc_hi[:, h, :]), op0=ALU.mult,
                                                     op1=ALU.subtract).then_inc(g_out, 1)
                    evacuate(p)
                    if NAMES[p] == "proj21":
                        dve.sem_inc(mg_sum, 1)
                        dve.wait_ge(mg_hi, l + 1)
                        dve.tensor_tensor(act_lo[:, :, :], merged[:, :, :], f32(act_hi[:, :, :]),
                                          ALU.subtract).then_inc(mg_out, 1)
                dve.sem_inc(x_ready, 1)

            dve.wait_ge(prm_ready, 1)
            dve.wait_ge(consts, 2)
            norm(0)
            mixer(0)
            norm(1)

            def dlo(t, slot, s):
                dve.wait_ge(d_hi[t], s + 1)
                dve.tensor_tensor(w_lo[:, t, :], raw[:, slot, :], f32(w_hi[:, t, :]), ALU.subtract).then_inc(d_lo[t], 1)

            def dense_hidden(s, parity):
                dve.wait_ge(d_silu, s + 1)
                f = dsilu[:, :, :].rearrange("p a t -> p (a t)")
                dve.tensor_tensor(f, f, banks(2 * parity + 1), ALU.mult).then_inc(d_h, 1)

            def dense_hidden_lo(s):
                dve.wait_ge(d_hhi, s + 1)
                dve.tensor_tensor(dh_lo[:, :, :], dsilu[:, :, :], f32(dh_hi[:, :, :]), ALU.subtract).then_inc(d_hT, 1)

            def dense_step(q, parity, up, down):
                s = 2 * q + parity
                if up:
                    for t in range(2):
                        dlo(t, 3 * parity + t, s)
                if down:
                    dense_hidden(s - 1, 1 - parity)
                    dlo(2, 3 * parity + 2, s - 1)
                    dense_hidden_lo(s - 1)

            dense_step(0, 0, True, False)
            dense_step(0, 1, True, True)
            with dve.Fori(1, NF // 2) as q:
                dense_step(q, 0, True, True)
                dense_step(q, 1, True, True)
            dense_step(NF // 2, 0, True, True)
            dense_step(NF // 2, 1, False, True)
            dve.wait_ge(d_used[2], NF)
            for t in range(TT):
                link(dve.tensor_tensor(xres[:, t, :], xres[:, t, :], banks(4 + 2 * t, 2), ALU.add))
            dve.sem_inc(x_ready, 1)

            norm(2)
            mixer(1)
            norm(3)

            def elo(t, fs, s):
                dve.wait_ge(e_hi[t], s + 1)
                dve.tensor_tensor(w_lo[:, t, :], raw[:, 3 * t + fs, :], f32(w_hi[:, t, :]),
                                  ALU.subtract).then_inc(e_lo[t], 1)

            def step_gu(e, f, fs):
                for t in range(2):
                    elo(t, fs, NF * e + f)

            def hidden(e, f, bank):
                dve.wait_ge(e_silu, NF * e + f + 1)
                dve.wait_ge(e_tr, NF * e + f + 1)
                dve.tensor_tensor(hid[:, :], esilu[:, :], ps[:, bank, FC:2 * FC], ALU.mult).then_inc(e_h, 1)

            def hidden_lo(e, f):
                dve.wait_ge(e_hhi, NF * e + f + 1)
                dve.tensor_tensor(eh_lo[:, :, :].rearrange("p a t -> p (a t)"), ps[:, 3, 0:2 * CAP],
                                  f32(eh_hi[:, :, :]).rearrange("p a t -> p (a t)"), ALU.subtract).then_inc(e_hT, 1)

            def pick_of(e, ew):
                for t in range(TT):
                    dve.tensor_scalar(pick[:, t, :], iota[:, :], rank[:, t, ds(ew, 1)], None, ALU.is_equal).then_inc(e_pick, 1)

            def tokens_lo(e):
                dve.wait_ge(e_xhi, e + 1)
                dve.tensor_tensor(xs_lo[:, :, :].rearrange("p a t -> p (a t)"), banks(4, 2),
                                  f32(xs_hi[:, :, :]).rearrange("p a t -> p (a t)"), ALU.subtract).then_inc(e_x, 1)

            def output_lo(e):
                dve.wait_ge(e_yhi, e + 1)
                dve.wait_ge(e_gsel, e + 1)
                dve.scalar_tensor_tensor(out=y_lo[:, :], in0=banks(6, 2), scalar=gsel[:, 0:1], in1=f32(y_hi[:, :]),
                                         op0=ALU.mult, op1=ALU.subtract).then_inc(e_ylo, 1)

            def scatter_add(e, t):
                dve.wait_ge(e_sc, TT * e + t + 1)
                dve.wait_ge(e_add, TT * e + t + 1)
                dve.tensor_tensor(xres[:, t, :], xres[:, t, :], banks(4, 2), ALU.add).then_inc(e_add, 1)

            def expert(e, ew, opening):
                if not (isinstance(e, int) and e == 0):
                    step_gu(e, 0, 0)
                if not opening:
                    hidden(e - 1, NF - 1, (NF - 1) % 3)
                tokens_lo(e)
                if not opening:
                    elo(2, 0, NF * (e - 1) + NF - 2)
                    hidden_lo(e - 1, NF - 2)
                for f in range(1, 5):
                    step_gu(e, f, f % 3)
                    hidden(e, f - 1, (f - 1) % 3)
                    if f == 1:
                        if not opening:
                            elo(2, 1, NF * (e - 1) + NF - 1)
                            hidden_lo(e - 1, NF - 1)
                        continue
                    if f >= 3 and not opening:
                        scatter_add(e - 1, f - 3)
                    elo(2, f - 2, NF * e + f - 2)
                    hidden_lo(e, f - 2)
                    if f == 2 and not opening:
                        output_lo(e - 1)
                dve.wait_ge(e_pt, e + 1)
                dve.tensor_copy(gsel[:, :], ps[:, 5, ds(ew, 1)]).then_inc(e_gsel, 1)
                pick_of(e + 1, ew + 1)
                with dve.Fori(0, (NF - 5) // 3) as j:
                    for i in range(3):
                        step_gu(e, 3 * j + 5 + i, (2 + i) % 3)
                        hidden(e, 3 * j + 4 + i, (1 + i) % 3)
                        elo(2, i, NF * e + 3 * j + 3 + i)
                        hidden_lo(e, 3 * j + 3 + i)

            def expert_pass(k):
                expert(NE * k, 0, True)
                with dve.Fori(NE * k + 1, NE * (k + 1)) as e:
                    expert(e, e - NE * k, False)
                e = NE * (k + 1) - 1
                hidden(e, NF - 1, (NF - 1) % 3)
                for f in (NF - 2, NF - 1):
                    elo(2, f % 3, NF * e + f)
                    hidden_lo(e, f)
                output_lo(e)
                for t in range(TT):
                    scatter_add(e, t)

            dve.sem_inc(e_h, 2)
            dve.sem_inc(e_add, 1)
            step_gu(0, 0, 0)

            dve.wait_ge(wr_loaded, 16)
            link(dve.tensor_copy(wr_hi[:, :, :], wr[:, :, :]))
            dve.tensor_tensor(wr_lo[:, :, :], wr[:, :, :], f32(wr_hi[:, :, :]), ALU.subtract).then_inc(r_split, 1)
            dve.wait_ge(r_iota, 1)
            link(dve.tensor_copy(iota[:, :], iota_i))
            link(dve.memset(one8[:, :], 1.0))
            link(dve.memset(rank[:, :, NE:NE + 1], -1.0))
            dve.wait_ge(r_logit, 1)
            lf = lgt[:, :, :].rearrange("p t e -> p (t e)")
            link(dve.tensor_copy(lf, ps[:, BX, 0:TT * NE]))

            def wide(v):
                return v[:, :].rearrange("p (t a) -> p t a", a=1).to_broadcast([P, TT, NE])

            def first_of_largest(src, v, pickd):
                link(dve.tensor_reduce(out=v[:, :], in_=src[:, :, :], axis=AX.X, op=ALU.max))
                link(dve.tensor_tensor(eq[:, :, :], src[:, :, :], wide(v), ALU.is_equal))
                for t in range(TT):
                    ins = dve.tensor_tensor_scan(out=cnt[:, t, :], data0=eq[:, t, :], data1=one8[:, :], initial=0.0,
                                                 op0=ALU.add, op1=ALU.mult)
                    link(ins)
                link(dve.scalar_tensor_tensor(out=pickd[:, :, :], in0=cnt[:, :, :], scalar=1.0, in1=eq[:, :, :],
                                              op0=ALU.is_le, op1=ALU.mult))
            first_of_largest(lgt, v1, first)
            link(dve.scalar_tensor_tensor(out=lgt2[:, :, :], in0=first[:, :, :], scalar=-3e38, in1=lgt[:, :, :],
                                          op0=ALU.mult, op1=ALU.add))
            first_of_largest(lgt2, v2, second)
            dve.tensor_tensor(wt2[:, :], v2[:, :], v1[:, :], ALU.subtract).then_inc(r_v, 1)
            dve.tensor_tensor(chosen[:, :, :], first[:, :, :], second[:, :, :], ALU.add).then_inc(r_chosen, 1)
            dve.wait_ge(r_e, 1)
            link(dve.tensor_scalar(wt1[:, :], wt2[:, :], 1.0, None, ALU.add))
            link(dve.reciprocal(wt1[:, :], wt1[:, :]))
            link(dve.tensor_tensor(wt2[:, :], wt2[:, :], wt1[:, :], ALU.mult))
            link(dve.tensor_tensor(first[:, :, :], first[:, :, :], wide(wt1), ALU.mult))
            link(dve.tensor_tensor(second[:, :, :], second[:, :, :], wide(wt2), ALU.mult))
            link(dve.tensor_tensor(gates[:, :, :], first[:, :, :], second[:, :, :], ALU.add))
            dve.wait_ge(r_cum, 1)
            link(dve.tensor_tensor(rank[:, :, 0:NE], ps[:, BY, 0:TT * NE].rearrange("p (t e) -> p t e", e=NE),
                                   chosen[:, :, :], ALU.mult))
            link(dve.tensor_scalar(rank[:, :, 0:NE], rank[:, :, 0:NE], -1.0, None, ALU.add))
            dve.tensor_reduce(out=most[:, :], in_=ps[:, BY, TT * NE:(TT + 1) * NE], axis=AX.X, op=ALU.max).then_inc(r_rank, 1)

            dve.wait_ge(r_rank, 1)
            pick_of(0, 0)
            expert_pass(0)
            fullest = dve.value_load(most[0:1, 0:1])
            with dve.If(fullest > CAP):
                dve.wait_ge(e_pick, 2 * (NE + 1))
                link(dve.tensor_scalar(rank[:, :, 0:NE], rank[:, :, 0:NE], -float(CAP), None, ALU.add))
                for t in range(TT):
                    dve.tensor_scalar(pick[:, t, :], iota[:, :], rank[:, t, 0:1], None, ALU.is_equal).then_inc(e_again, 1)
                expert_pass(1)
                dve.wait_ge(e_add, 2 * TT * NE + 1)
            dve.wait_ge(e_add, TT * NE + 1)
            dve.sem_inc(x_ready, 1)
            norm(4, final=True)

        @block.tensor
        def _(pe):
            def mm3(o, a_hi, a_lo, b_hi, b_lo, start, stop):
                pe.matmul(o, a_hi, b_hi, start=start, stop=False, skip_group_check=True)
                pe.matmul(o, a_hi, b_lo, start=False, stop=False, skip_group_check=True)
                return pe.matmul(o, a_lo, b_hi, start=False, stop=stop, skip_group_check=True)

            def norm(n):
                for b in range(4):
                    for kk in range(2):
                        k = 2 * b + kk
                        for t in range(TT):
                            if b == 0 and kk == 0:
                                pe.wait_ge(n_hn, TT * n + t + 1)
                            ins = pe.transpose(ps[:, b, kk * S + t * P:kk * S + (t + 1) * P],
                                               hn[:, t, k * P:(k + 1) * P], ident[:, :])
                    ins.then_inc(n_tr, 1)

            def mixer(l):
                n = [before_units(l)]
                G0 = l * NPAN
                operands = {"act": (act_hi, act_lo), "o0": (oa_hi, oa_lo), "o1": (obc_hi, obc_lo),
                            "o2": (obc_hi, obc_lo)}

                def panel(p):
                    name, _, _, ws, kt, operand, _ = panels_of(l)[p]
                    g = G0 + p
                    b0 = (g % 2) * 2
                    if p >= 2:
                        who = EVAC[p - 2]
                        pe.wait_ge(evac_act if who == "act" else evac_dve, evacuated(g - 2, who))
                    if p == 0:
                        pe.wait_ge(n_act, 4 * (2 * l + 1))
                    if name == "proj10":
                        pe.wait_ge(b_out, l + 1)
                    if name == "proj00":
                        pe.wait_ge(a_out, HA // 2 * (l + 1))
                    if name == "proj20":
                        pe.wait_ge(g_out, HC * (l + 1))
                    if name == "out0":
                        pe.wait_ge(mg_out, l + 1)
                    hi, lo = operands[operand]
                    for j in range(kt // KW):
                        u = n[0]
                        pe.wait_ge(m_lo, u + 1)
                        for kk in range(KW):
                            k = j * KW + kk
                            for c in range(4 if ws else TT):
                                last = k == kt - 1
                                if ws:
                                    w = slice(kk * UC + c * P, kk * UC + (c + 1) * P)
                                    ins = mm3(ps[:, b0 + c // 2, (c % 2) * S:(c % 2 + 1) * S],
                                              w_hi[:, u % SRING, w], w_lo[:, u % SRING, w], hi[:, k, :], lo[:, k, :],
                                              k == 0 and c % 2 == 0, last)
                                else:
                                    w = slice(kk * UC, (kk + 1) * UC)
                                    tok = slice(c * P, (c + 1) * P)
                                    ins = mm3(ps[:, b0 + c, :], hi[:, k, tok], lo[:, k, tok],
                                              w_hi[:, u % SRING, w], w_lo[:, u % SRING, w], k == 0, last)
                        ins.then_inc(m_used, 1)
                        n[0] += 1

                def narrow():
                    pe.wait_ge(n_act, 4 * (2 * l + 1))
                    pe.wait_ge(s_split, l + 1)
                    for k in range(KD):
                        for t in range(TT):
                            tok = slice(t * P, (t + 1) * P)
                            ins = mm3(ps[:, BO, t * SM:(t + 1) * SM], act_hi[:, k, tok], act_lo[:, k, tok],
                                      wsm_hi[:, k, :], wsm_lo[:, k, :], k == 0 and t == 0, k == KD - 1)
                    ins.then_inc(s_done, 1)

                def narrow_sums():
                    pe.wait_ge(s_biased, l + 1)
                    pe.wait_ge(consts, 2)
                    for t in range(TT):
                        ins = pe.matmul(ps[0:LR, BT, t * P:(t + 1) * P], logf[:, t, HA:SM], ident[:, :], start=t == 0,
                                        stop=True, skip_group_check=True)
                    ins.then_inc(s_aT, 1)
                    pe.wait_ge(s_logf, l + 1)
                    for t in range(TT):
                        ins = pe.matmul(ps[0:HA, BY, 0:S], logf[:, t, 0:HA], tri[:, (1 - t) * P:(3 - t) * P],
                                        start=t == 0, stop=t == TT - 1)
                    ins.then_inc(s_FT, 1)
                    pe.wait_ge(s_aTc, l + 1)
                    pe.wait_ge(wa2_loaded, 16 * (l + 1))
                    for m in range(NPAIR):
                        ins = pe.matmul(ps[:, BX, m * S:(m + 1) * S], wa2[:, m * P:(m + 1) * P], aT,
                                        start=m == 0, stop=True, skip_group_check=True)
                    ins.then_inc(g_lin, 1)

                def head_scores(h):
                    a = l * HA + h
                    if h == 0:
                        pe.wait_ge(s_frow, 64 * (l + 1))
                        pe.wait_ge(evac_act, evacuated(G0 + 1, "act"))
                        pe.wait_ge(s_rows, 2 * (l + 1))
                        pe.wait_ge(g_neg, l + 1)
                    if h >= 2:
                        pe.wait_ge(a_max, a - 1)
                    r, m, g = (h % 2) * DH, h // 2, 32 * (h % 4)
                    bank = BX + h % 2
                    for t, cols in ((0, slice(0, P)), (1, slice(P, 3 * P))):
                        q = slice(t * P, (t + 1) * P)
                        nk = (t + 1) * P
                        pe.matmul(ps[:, bank, cols], qT[r:r + DH, m, q], kT[r:r + DH, m, 0:nk], start=True, stop=False)
                        ins = pe.matmul(ps[:, bank, cols], f_query[g:g + 2, h // 4, q], f_key[g:g + 2, h // 4, 0:nk],
                                        start=False, stop=True)
                    ins.then_inc(a_score, 1)

                def head_transpose(h):
                    a = l * HA + h
                    pe.wait_ge(a_prob, a + 1)
                    if h > 0:
                        pe.wait_ge(a_pt, a)
                    for i in range(3):
                        ins = pe.transpose(ps[:, BT, i * P:(i + 1) * P], probs[:, h % 2, i * P:(i + 1) * P], ident[:, :])
                    ins.then_inc(a_tr, 1)

                def head_values(h):
                    a = l * HA + h
                    pe.wait_ge(a_pt, a + 1)
                    if h % 2 == 0:
                        if h > 0:
                            pe.wait_ge(a_out, HA // 2 * l + h // 2)
                        else:
                            pe.wait_ge(evac_act, evacuated(G0 + 2, "act"))
                    r = (h % 2) * DH
                    v = slice(h * DH, (h + 1) * DH)
                    pe.matmul(ps[r:r + DH, BO, 0:S], vA[:, 0, v], probsT[:, 0:S], start=True, stop=False)
                    pe.matmul(ps[r:r + DH, BO, P:S], vA[:, 1, v], probsT[:, 2 * P:3 * P], start=False,
                              stop=True).then_inc(a_pv, 1)

                def gla_scores():
                    pe.wait_ge(g_in, l + 1)
                    pe.wait_ge(a_max, HA * (l + 1))
                    for r in range(2):
                        for t in range(TT):
                            for m in range(NPAIR):
                                rows, tok = slice(r * DK, (r + 1) * DK), slice(t * P, (t + 1) * P)
                                c = (t * NPAIR + m) * P
                                ins = pe.matmul(ps[:, BX + r, c:c + P], cqkT[rows, NPAIR + m, tok], cqkT[rows, m, tok],
                                                start=c == 0, stop=True, skip_group_check=True)
                    ins.then_inc(g_att, 1)
                    pe.wait_ge(a_pt, HA * (l + 1))
                    for t in range(TT):
                        for m in range(NPAIR):
                            c = (t * NPAIR + m) * P
                            ins = pe.transpose(ps[:, BT, c:c + P], kst[:, m, t * P:(t + 1) * P], ident[:, :])
                    ins.then_inc(g_kstT, 1)

                def gla_states():
                    pe.wait_ge(g_kst, l + 1)
                    pe.wait_ge(a_out, HA // 2 * (l + 1))
                    for i, c in enumerate((0, 2, 1)):
                        bank, col = (BT, 0) if c == 1 else (BO, (c // 2) * NPAIR * DV)
                        rows = slice((c % 2) * CH, (c % 2 + 1) * CH)
                        for m in range(NPAIR):
                            for r in range(2):
                                kc = ((c // 2) * NPAIR + m) * P + r * DK
                                h = 2 * m + r
                                ins = pe.matmul(ps[r * DK:(r + 1) * DK, bank, col + m * DV:col + (m + 1) * DV],
                                                kst_tok[rows, kc:kc + DK], vC[rows, c // 2, h * DV:(h + 1) * DV],
                                                start=(i != 1 and m == 0), stop=True, skip_group_check=True)
                    ins.then_inc(g_kv, 1)

                def gla_out():
                    pe.wait_ge(g_attm, l + 1)
                    for r in range(2):
                        for t in range(TT):
                            for m in range(NPAIR):
                                c = (t * NPAIR + m) * P
                                h = 2 * m + r
                                pe.matmul(ps[:, BX + r, c:c + P], attC[:, r * 4 * P + c:r * 4 * P + c + P],
                                          vC[:, t, h * DV:(h + 1) * DV], start=c == 0, stop=False, skip_group_check=True)
                    pe.wait_ge(g_state, l + 1)
                    for r in range(2):
                        rows = slice(r * DK, (r + 1) * DK)
                        for c in range(1, S // CH):
                            for m in range(NPAIR):
                                col = ((c // 2) * NPAIR + m) * P
                                ins = pe.matmul(ps[(c % 2) * CH:(c % 2 + 1) * CH, BX + r, col:col + P],
                                                cqkT[rows, m, c * CH:(c + 1) * CH], states[rows, c - 1, m, :],
                                                start=False, stop=True, skip_group_check=True)
                    ins.then_inc(g_o, 1)

                def gla_transpose():
                    pe.wait_ge(g_on, l + 1)
                    for h in range(HC):
                        for t in range(TT):
                            c = (((h % 2) * TT + t) * NPAIR + h // 2) * P
                            ins = pe.transpose(banks(BT, 2)[:, h * S + t * P:h * S + (t + 1) * P], oC[:, c:c + P],
                                               ident[:, :])
                    ins.then_inc(g_oT, 1)

                narrow()
                panel(0)
                narrow_sums()
                panel(1)
                for p in range(2, NPAN):
                    if 0 <= p - HS < HA:
                        head_scores(p - HS)
                    if 0 <= p - HS - 1 < HA:
                        head_transpose(p - HS - 1)
                    if 0 <= p - HS - 2 < HA:
                        head_values(p - HS - 2)
                    if NAMES[p] == "proj11":
                        gla_scores()
                    if NAMES[p] == "gate00":
                        gla_states()
                    if NAMES[p] == "proj00":
                        gla_out()
                    if NAMES[p] == "proj01":
                        gla_transpose()
                    panel(p)

            pe.wait_ge(consts, 1)
            pe.wait_ge(prm_loaded, 64)
            pe.transpose(ps[:, BX, 0:NPRM], prm_rows, ident[0:NPRM, 0:NPRM]).then_inc(prm_tr, 1)
            norm(0)
            mixer(0)
            norm(1)

            def up(s, parity):
                for t in range(2):
                    pe.wait_ge(d_lo[t], s + 1)
                    w_h = w_hi[:, t, :].rearrange("p (k w n) -> p k w n", k=KW, w=2)
                    w_l = w_lo[:, t, :].rearrange("p (k w n) -> p k w n", k=KW, w=2)
                    for kk in range(KW):
                        k = t * KW + kk
                        for w in range(2):
                            for c in range(2):
                                cc = slice(c * P, (c + 1) * P)
                                ins = mm3(ps[:, 2 * parity + w, c * S:(c + 1) * S], w_h[:, kk, w, cc], w_l[:, kk, w, cc],
                                          act_hi[:, k, :], act_lo[:, k, :], k == 0 and c == 0, k == KD - 1)
                    ins.then_inc(d_used[t], 1)

            def down(s, stop):
                pe.wait_ge(d_hT, s + 1)
                pe.wait_ge(d_lo[2], s + 1)
                for k in range(2):
                    for t in range(TT):
                        tok = slice(t * P, (t + 1) * P)
                        for half in range(2):
                            cols = slice(k * D + half * UC, k * D + (half + 1) * UC)
                            ins = mm3(ps[:, 4 + 2 * t + half, :], dh_hi[:, k, tok], dh_lo[:, k, tok],
                                      w_hi[:, 2, cols], w_lo[:, 2, cols], False, stop and k == 1)
                ins.then_inc(d_used[2], 1)

            def open_sums(first, nb):
                for b in range(first, first + nb):
                    pe.matmul(ps[:, b, :], zrow[0:1, 0:P], zrow[0:1, :], start=True, stop=False, skip_group_check=True)

            pe.wait_ge(n_act, 8)
            open_sums(4, 4)
            up(0, 0)
            up(1, 1)
            down(0, False)
            with pe.Fori(0, (NF - 3) // 2) as j:
                for i in range(2):
                    s = 2 * j + 2 + i
                    pe.wait_ge(d_h, s - 1)
                    up(s, i)
                    down(s - 1, False)
            pe.wait_ge(d_h, NF - 2)
            up(NF - 1, (NF - 1) % 2)
            down(NF - 2, False)
            down(NF - 1, True)

            norm(2)
            mixer(1)
            norm(3)

            pe.wait_ge(n_act, 16)
            pe.wait_ge(r_split, 1)
            for k in range(KD):
                for t in range(TT):
                    tok = slice(t * P, (t + 1) * P)
                    ins = mm3(ps[:, BX, t * NE:(t + 1) * NE], act_hi[:, k, tok], act_lo[:, k, tok], wr_hi[:, k, :],
                              wr_lo[:, k, :], k == 0 and t == 0, k == KD - 1)
            ins.then_inc(r_logit, 1)
            pe.wait_ge(r_chosen, 1)
            for t in range(TT):
                for s in range(TT):
                    ins = pe.matmul(ps[:, BY, t * NE:(t + 1) * NE], tri[:, (1 - s + t) * P:(2 - s + t) * P], chosen[:, s, :],
                                    start=t == 0 and s == 0, stop=s == TT - 1, skip_group_check=True)
            for s in range(TT):
                ins = pe.matmul(ps[:, BY, TT * NE:(TT + 1) * NE], tri[:, 2 * P:3 * P], chosen[:, s, :], start=False,
                                stop=s == TT - 1, skip_group_check=True)
            ins.then_inc(r_cum, 1)

            def eup(e, f, bank):
                for t in range(2):
                    pe.wait_ge(e_lo[t], NF * e + f + 1)
                    for kk in range(KW):
                        k = t * KW + kk
                        cols = slice(kk * UC, (kk + 1) * UC)
                        ins = mm3(ps[:, bank, :], xs_hi[:, k, :], xs_lo[:, k, :], w_hi[:, t, cols], w_lo[:, t, cols],
                                  k == 0, k == KD - 1)
                    ins.then_inc(e_used[t], 1)

            def edown(e, f, stop=False):
                pe.wait_ge(e_hT, NF * e + f + 1)
                pe.wait_ge(e_lo[2], NF * e + f + 1)
                for k in range(2):
                    for half in range(2):
                        cols = slice(k * D + half * UC, k * D + (half + 1) * UC)
                        ins = mm3(ps[:, 6 + half, :], eh_hi[:, k, :], eh_lo[:, k, :], w_hi[:, 2, cols], w_lo[:, 2, cols],
                                  False, stop and k == 1)
                ins.then_inc(e_used[2], 1)

            def etranspose(e, f):
                pe.wait_ge(e_h, NF * e + f + 3)
                for k in range(2):
                    ins = pe.transpose(ps[:, 3, k * CAP:(k + 1) * CAP], hid[:, k * P:(k + 1) * P], ident[:, :])
                ins.then_inc(e_tr, 1)

            def gather(e):
                pe.wait_ge(e_pick, 2 * (e + 1))
                for k in range(KD):
                    for t in range(TT):
                        ins = pe.matmul(ps[:, 4 + k // 4, (k % 4) * CAP:(k % 4 + 1) * CAP], hn[:, t, k * P:(k + 1) * P],
                                        pick[:, t, :], start=k % 4 == 0 and t == 0, stop=t == TT - 1, skip_group_check=True)
                ins.then_inc(e_gath, 1)

            def scatter(e, t):
                if t == 0:
                    pe.wait_ge(e_ylo, e + 1)
                else:
                    pe.wait_ge(e_add, TT * e + 2)
                for half in range(2):
                    cols = slice(half * UC, (half + 1) * UC)
                    pe.matmul(ps[:, 4 + half, :], pickT[:, t * P:(t + 1) * P], y_hi[:, cols], start=True, stop=False)
                    ins = pe.matmul(ps[:, 4 + half, :], pickT[:, t * P:(t + 1) * P], y_lo[:, cols], start=False, stop=True)
                ins.then_inc(e_sc, 1)

            def slots(e):
                for t in range(TT):
                    pe.transpose(ps[:, 4, t * P:(t + 1) * P], pick[:, t, :], ident[:, :])
                for t in range(TT):
                    ins = pe.matmul(ps[:, 5, 0:NE], pick[:, t, :], gates[:, t, :], start=t == 0, stop=t == TT - 1)
                ins.then_inc(e_pt, 1)

            def eup_step(e, f, bank):
                pe.wait_ge(e_h, NF * e + f)
                eup(e, f, bank)

            def expert(e, opening):
                if not (isinstance(e, int) and e == 0):
                    pe.wait_ge(e_ptc, e)
                    pe.wait_ge(e_gsel, e)
                gather(e)
                if not opening:
                    edown(e - 1, NF - 3)
                    etranspose(e - 1, NF - 2)
                pe.wait_ge(e_x, e + 1)
                pe.wait_ge(e_h, NF * e + 1)
                eup(e, 0, 0)
                if not opening:
                    edown(e - 1, NF - 2)
                    etranspose(e - 1, NF - 1)
                pe.wait_ge(e_h, NF * e + 2)
                eup(e, 1, 1)
                if not opening:
                    edown(e - 1, NF - 1, True)
                etranspose(e, 0)
                eup_step(e, 2, 2)
                if not opening:
                    pe.wait_ge(e_ylo, e)
                open_sums(6, 2)
                for f in (3, 4):
                    edown(e, f - 3)
                    etranspose(e, f - 2)
                    if not opening:
                        scatter(e - 1, f - 3)
                    eup_step(e, f, f % 3)
                if not opening:
                    pe.wait_ge(e_add, TT * e + 1)
                slots(e)
                with pe.Fori(0, (NF - 5) // 3) as j:
                    for i in range(3):
                        edown(e, 3 * j + 2 + i)
                        etranspose(e, 3 * j + 3 + i)
                        eup_step(e, 3 * j + 5 + i, (2 + i) % 3)

            def expert_pass(k):
                expert(NE * k, True)
                with pe.Fori(NE * k + 1, NE * (k + 1)) as e:
                    expert(e, False)
                e = NE * (k + 1) - 1
                edown(e, NF - 3)
                for f in (NF - 2, NF - 1):
                    etranspose(e, f)
                    edown(e, f, f == NF - 1)
                for t in range(TT):
                    scatter(e, t)

            pe.sem_inc(e_used[2], 1)
            pe.sem_inc(e_tr, 1)
            pe.wait_ge(r_rank, 1)
            expert_pass(0)
            fullest = pe.value_load(most[0:1, 0:1])
            with pe.If(fullest > CAP):
                pe.wait_ge(e_again, TT)
                pe.wait_ge(e_add, TT * NE + 1)
                expert_pass(1)


_INS = ["x", "g_mix", "w_in", "b_f", "conv_w", "w_a2", "b_a", "g_gla", "w_pa", "w_pb", "w_pc", "w_gate", "b_gate",
        "w_o", "g_ffn", "ffn_w1", "ffn_w3", "ffn_w2", "w_router", "moe_w1", "moe_w3", "moe_w2", "g_final"]


def kernel(**inputs):
    import numpy as _np
    import concourse.bacc as _bacc
    from concourse import mybir as _mybir
    from concourse.bass_utils import run_bass_kernel_spmd as _run

    nc = _bacc.Bacc("TRN2", target_bir_lowering=False, num_devices=1)
    arrays, args = {}, []
    for name in _INS:
        a = _np.ascontiguousarray(inputs[name])
        arrays[f"in_{name}"] = a
        args.append(nc.dram_tensor(f"in_{name}", a.shape, _mybir.dt.from_np(a.dtype), kind="ExternalInput").ap())
    shape = arrays["in_x"].shape
    args.append(nc.dram_tensor("out_y", shape, _mybir.dt.float32, kind="ExternalOutput").ap())
    hybrid_trunk(nc, *args)
    r = _run(nc, [arrays], core_ids=[0])
    return r.results[0]["out_y"]
```

```python
import numpy as np
import concourse.bass as bass
from concourse import mybir
from contextlib import ExitStack


def hybrid_trunk(nc, x, g_mix, w_in, b_f, conv_w, w_a2, b_a, g_gla, w_pa, w_pb, w_pc, w_gate,
                 b_gate, w_o, g_ffn, ffn_w1, ffn_w3, ffn_w2, w_router, moe_w1, moe_w3, moe_w2,
                 g_final, out):
    F32, F32R, BF16, I32 = mybir.dt.float32, mybir.dt.float32r, mybir.dt.bfloat16, mybir.dt.int32
    ALU, ACT, AX = mybir.AluOpType, mybir.ActivationFunctionType, mybir.AxisListType
    ds = bass.ds

    P = 128
    S, D = x.shape[1], x.shape[2]
    TT, KD = S // P, D // P
    L = w_in.shape[0]
    HA, DH = b_f.shape[1], 64
    WB = conv_w.shape[2]
    LR, WK = w_a2.shape[1], w_a2.shape[2]
    HC, DK, DV = 4, 64, 128
    CH = 64
    NPAIR = WK // P
    NE, DF = moe_w1.shape[1], moe_w1.shape[3]
    FC = 256
    NF = DF // FC
    KW = 4
    UC = 512
    UN = KW * UC
    EPS = 1e-6
    NEG = -1e30
    CAP = P

    sizes = (WB, WB, WB, HA, WB, WB, WB, WK, WK, WB, LR, WB)
    offs = [sum(sizes[:i]) for i in range(len(sizes))]
    (C_AQ, C_AK, C_AV, C_AF, C_BU, C_BB, C_BC, C_CQ, C_CK, C_CV, C_CA, C_CR) = offs
    SM = HA + LR
    DR = 32
    NW = 96

    def panels_of(l):
        rows = [("k", w_in[l], C_AK, True, KD, "act", "act"), ("q", w_in[l], C_AQ, True, KD, "act", "act"),
                ("v", w_in[l], C_AV, False, KD, "act", "act"), ("cqk", w_in[l], C_CQ, True, KD, "act", "act"),
                ("cv", w_in[l], C_CV, False, KD, "act", "act"), ("cr", w_in[l], C_CR, False, KD, "act", "act"),
                ("u", w_in[l], C_BU, True, KD, "act", "act"), ("cg", w_in[l], C_BC, True, KD, "act", "dve"),
                ("bg", w_in[l], C_BB, True, KD, "act", "dve")]
        for br, wp in ((1, w_pb[l]), (0, w_pa[l]), (2, w_pc[l])):
            for half in range(2):
                rows.append((f"gate{br}{half}", w_gate[l], br * D + half * UC, True, KD, "act", "act"))
                rows.append((f"proj{br}{half}", wp, half * UC, True, WB // P, "o%d" % br, "dve"))
        for half in range(2):
            rows.append((f"out{half}", w_o[l], half * UC, False, KD, "act", "dve"))
        return rows

    NPAN = len(panels_of(0))
    NUNIT = sum(r[4] // KW for r in panels_of(0))
    NAMES = [r[0] for r in panels_of(0)]
    EVAC = [r[6] for r in panels_of(0)]

    def evacuated(g, engine):
        return sum(EVAC[i % NPAN] == engine for i in range(g + 1))

    def units_until(g):
        return sum(panels_of(0)[i % NPAN][4] // KW for i in range(g + 1))

    HS = 3

    MRING, SRING = 6, 3

    ctx = ExitStack()
    with ctx:
        def sb(name, shape, dt=F32, c=ctx):
            return c.enter_context(nc.sbuf_tensor(name, shape, dt))

        def sem(name):
            return ctx.enter_context(nc.semaphore(name))

        raw = sb("raw", [P, 9, UN])
        w_hi = sb("w_hi", [P, SRING, UN], F32R)
        w_lo = sb("w_lo", [P, SRING, UN], F32R)
        xres = sb("xres", [P, TT, D])
        hn = sb("hn", [P, TT, D])
        act_hi = sb("act_hi", [P, KD, S], F32R)
        act_lo = sb("act_lo", [P, KD, S], F32R)
        merged = sb("merged", [P, KD, S])
        gains = merged[:, 0:4, :].rearrange("p a b -> p (a b)")
        ident = sb("ident", [P, P])
        cmask = sb("cmask", [P, 2 * P])
        tri = sb("tri", [P, 3 * P])
        gmask = sb("gmask", [P, P])
        keep = sb("keep", [P, S])
        sumsq = sb("sumsq", [P, TT])
        rstd = sb("rstd", [P, TT])
        mhalf = sb("mhalf", [P, 8])
        zrow = sb("zrow", [1, UC], BF16)
        prm = sb("prm", [P, P])
        wsm = sb("wsm", [P, L, KD, SM])
        wa2_rows = sb("wa2", [DR + LR, WK])
        wa2 = wa2_rows[DR:DR + LR, :]
        bf = sb("bf", [HA, L])
        wr = sb("wr", [P, KD, NE])
        iota_i = keep[:, 0:P].bitcast(I32)

        NCONV, NBA, NGG, NBG = L * 3 * WB // P, L * WK // P, L * WB // P, L * 3 * D // P
        R_CONV, R_BA, R_GG, R_BG = 0, NCONV, NCONV + NBA, NCONV + NBA + NGG
        NPRM = R_BG + NBG
        prm_rows = merged[0:NPRM, 7, 0:P]

        mix = ExitStack()
        qT = sb("qT", [P, 4, S], c=mix)
        kT = sb("kT", [P, 4, S], c=mix)
        vA = sb("vA", [P, TT, WB], c=mix)
        oa_hi = sb("oa_hi", [P, 4, S], F32R, c=mix)
        oa_lo = sb("oa_lo", [P, 4, S], F32R, c=mix)
        obc_hi = sb("obc_hi", [P, 4, S], F32R, c=mix)
        obc_lo = sb("obc_lo", [P, 4, S], F32R, c=mix)
        probs = sb("probs", [P, 2, 3 * P], c=mix)
        f_query = sb("f_query", [98, 2, S], c=mix)
        f_key = sb("f_key", [98, 2, S], c=mix)
        f_rows = merged[0:HA, 4:6, :]
        logf = merged[0:HA, 2, :]
        lsa = merged[0:HA, 3, :]
        lsb = merged[0:HA, 6, :]
        ones8 = merged[0:HA, 7, :]
        aT = merged[DR:DR + LR, 6, :]
        wsm_hi = obc_hi[:, :, :].rearrange("p a t -> p (a t)")[:, 0:KD * NW].rearrange("p (k n) -> p k n", n=NW)
        wsm_lo = obc_lo[:, :, :].rearrange("p a t -> p (a t)")[:, 0:KD * NW].rearrange("p (k n) -> p k n", n=NW)
        cum = merged[:, 0:NPAIR, :]
        decay = sb("decay", [P, NPAIR, S // CH], c=mix)
        mx = sb("mx", [P, 2 * HA], c=mix)
        nmx = sb("nmx", [P, 2 * HA], c=mix)
        sm = sb("sm", [P, 2 * HA], c=mix)
        rs = sb("rs", [P, 2 * HA], c=mix)
        oss = sb("oss", [P, 2 * HC], c=mix)
        ors = sb("ors", [P, 2 * HC], c=mix)
        spare = raw[:, 6:9, :].rearrange("p a n -> p (a n)")
        ZP = S + 2
        at = [0]

        def carve(n):
            at[0] += n
            return spare[:, at[0] - n:at[0]]
        cqkT = carve(4 * S).rearrange("p (a t) -> p a t", t=S)
        vC = carve(TT * WB).rearrange("p (a t) -> p a t", t=WB)
        rC = carve(TT * WB).rearrange("p (a t) -> p a t", t=WB)
        zB = carve(4 * ZP).rearrange("p (a t) -> p a t", t=ZP)
        cvB = carve(4 * S).rearrange("p (a t) -> p a t", t=S)
        kst = carve(NPAIR * S).rearrange("p (a t) -> p a t", t=S)
        probsT = carve(3 * P)
        assert at[0] <= 3 * UN
        attC = qT[:, :, :].rearrange("p a t -> p (a t)")
        states = kT[:, 0:3, :].rearrange("p a t -> p (a t)").rearrange("p (n m e) -> p n m e", n=3, m=NPAIR)
        oC = vA[:, :, :].rearrange("p a t -> p (a t)")
        kst_tok = cvB[:, 0:2, :].rearrange("p a t -> p (a t)")
        sqC = zB[:, :, 0:S]
        lg = [hn[:, 0, 0:512], hn[:, 0, 512:1024], hn[:, 1, 0:512], hn[:, 1, 512:1024]]
        gate_s = hn[:, 0, :].rearrange("p (a t) -> p a t", t=S)
        prod_s = hn[:, 1, :].rearrange("p (a t) -> p a t", t=S)
        mix.close()

        den = ExitStack()
        dsilu = sb("dsilu", [P, 2, S], c=den)
        dh_hi = sb("dh_hi", [P, 2, S], F32R, c=den)
        dh_lo = sb("dh_lo", [P, 2, S], F32R, c=den)
        den.close()
        moe = ExitStack()
        pick = sb("pick", [P, TT, CAP], c=moe)
        pickT = sb("pickT", [P, S], F32R, c=moe)
        xs_hi = sb("xs_hi", [P, KD, CAP], F32R, c=moe)
        xs_lo = sb("xs_lo", [P, KD, CAP], F32R, c=moe)
        esilu = sb("esilu", [P, FC], c=moe)
        hid = sb("hid", [P, FC], c=moe)
        eh_hi = sb("eh_hi", [P, 2, CAP], F32R, c=moe)
        eh_lo = sb("eh_lo", [P, 2, CAP], F32R, c=moe)
        lgT = sb("lgT", [NE, S], c=moe)
        y_hi = sb("y_hi", [P, D], F32R, c=moe)
        y_lo = sb("y_lo", [P, D], F32R, c=moe)
        gsel = sb("gsel", [P, 1], c=moe)
        iota = sb("iota", [P, CAP], c=moe)
        lgt = sb("lgt", [P, TT, NE], c=moe)
        lgt2 = sb("lgt2", [P, TT, NE], c=moe)
        eq = sb("eq", [P, TT, NE], c=moe)
        cnt = sb("cnt", [P, TT, NE], c=moe)
        first = sb("first", [P, TT, NE], c=moe)
        second = sb("second", [P, TT, NE], c=moe)
        one8 = sb("one8", [P, NE], c=moe)
        v1 = sb("v1", [P, TT], c=moe)
        v2 = sb("v2", [P, TT], c=moe)
        wt1 = sb("wt1", [P, TT], c=moe)
        wt2 = sb("wt2", [P, TT], c=moe)
        chosen = sb("chosen", [P, TT, NE], c=moe)
        gates = sb("gates", [P, TT, NE], c=moe)
        rank = sb("rank", [P, TT, NE + 1], c=moe)
        most = sb("most", [P, 1], I32, c=moe)
        moe.close()

        ps = ctx.enter_context(nc.psum_tensor("ps", [P, 8, 512], F32))

        def banks(a, n=1):
            return ps[:, a:a + n, :].rearrange("p b n -> p (b n)")
        BX, BY, BT, BO = 4, 5, 6, 7

        x_loaded = [sem(f"x_loaded{t}") for t in range(TT)]
        prm_loaded, bf_loaded = sem("prm_loaded"), sem("bf_loaded")
        wsm_loaded, wa2_loaded, wr_loaded = sem("wsm_loaded"), sem("wa2_loaded"), sem("wr_loaded")
        gain_loaded, out_stored = sem("gain_loaded"), sem("out_stored")
        consts, cstep = sem("consts"), sem("cstep")
        prm_tr, prm_ready = sem("prm_tr"), sem("prm_ready")
        x_ready, n_sq, n_ms, n_rstd = sem("x_ready"), sem("n_sq"), sem("n_ms"), sem("n_rstd")
        n_hn, n_tr, n_hi, n_act = sem("n_hn"), sem("n_tr"), sem("n_hi"), sem("n_act")
        m_raw = [sem(f"m_raw{i}") for i in range(MRING)]
        m_hi, m_lo, m_used = sem("m_hi"), sem("m_lo"), sem("m_used")
        evac_act, evac_dve = sem("evac_act"), sem("evac_dve")
        s_zero, s_split, s_done, s_biased = sem("s_zero"), sem("s_split"), sem("s_done"), sem("s_biased")
        s_aTc, s_ln, s_rows, s_frow, s_fone = sem("s_aTc"), sem("s_ln"), sem("s_rows"), sem("s_frow"), sem("s_fone")
        o_tile, gain0_loaded = sem("o_tile"), sem("gain0_loaded")
        g_lin, g_neg, g_exp, g_ln, g_cum = sem("g_lin"), sem("g_neg"), sem("g_exp"), sem("g_ln"), sem("g_cum")
        g_es, g_in = sem("g_es"), sem("g_in")
        a_score, a_max, a_exp, a_prob = sem("a_score"), sem("a_max"), sem("a_exp"), sem("a_prob")
        a_tr, a_pt, a_pv, a_ohi, a_out = sem("a_tr"), sem("a_pt"), sem("a_pv"), sem("a_ohi"), sem("a_out")
        b_conv, b_y, b_hi, b_out = sem("b_conv"), sem("b_y"), sem("b_hi"), sem("b_out")
        g_att, g_attm, g_kstT, g_kst, g_kv = sem("g_att"), sem("g_attm"), sem("g_kstT"), sem("g_kst"), sem("g_kv")
        g_state, g_o, g_ocopy, g_ms, g_rstd = sem("g_state"), sem("g_o"), sem("g_ocopy"), sem("g_ms"), sem("g_rstd")
        g_on, g_oT, g_ohi, g_out = sem("g_on"), sem("g_oT"), sem("g_ohi"), sem("g_out")
        mg_sum, mg_hi, mg_out = sem("mg_sum"), sem("mg_hi"), sem("mg_out")
        dchain, achain = sem("dchain"), sem("achain")
        d_raw = [sem(f"d_raw{i}") for i in range(6)]
        d_hi = [sem(f"d_hi{t}") for t in range(3)]
        d_lo = [sem(f"d_lo{t}") for t in range(3)]
        d_used = [sem(f"d_used{t}") for t in range(3)]
        d_silu, d_h, d_hhi, d_hT = sem("d_silu"), sem("d_h"), sem("d_hhi"), sem("d_hT")
        d_tile = sem("d_tile")
        e_raw = [sem(f"e_raw{i}") for i in range(9)]
        e_hi = [sem(f"e_hi{t}") for t in range(3)]
        e_lo = [sem(f"e_lo{t}") for t in range(3)]
        e_used = [sem(f"e_used{t}") for t in range(3)]
        e_silu, e_h, e_tr, e_hhi, e_hT = (sem("e_silu"), sem("e_h"), sem("e_tr"),
                                                sem("e_hhi"), sem("e_hT"))
        e_pick, e_again, e_gath, e_xhi, e_x = sem("e_pick"), sem("e_again"), sem("e_gath"), sem("e_xhi"), sem("e_x")
        e_pt, e_ptc, e_gsel, e_yhi, e_ylo = (sem("e_pt"), sem("e_ptc"), sem("e_gsel"),
                                                  sem("e_yhi"), sem("e_ylo"))
        e_sc, e_add = sem("e_sc"), sem("e_add")
        r_zero, r_split, r_logit, r_lgT, r_iota = sem("r_zero"), sem("r_split"), sem("r_logit"), sem("r_lgT"), sem("r_iota")
        r_gates = sem("r_gates")
        r_v, r_e, r_chosen, r_cum, r_rank = sem("r_v"), sem("r_e"), sem("r_chosen"), sem("r_cum"), sem("r_rank")
        f_scaled = sem("f_scaled")

        block = ctx.enter_context(nc.Block())

        def last_use(n_units, ring, slot):
            return max(n for n in range(n_units) if n % ring == slot) + 1

        def per_set(s):
            return len(range(s, NF, 3))

        def before_units(l):
            return l * NUNIT

        w1e = moe_w1[0].rearrange("e (k p) n -> e p k n", p=P)
        w3e = moe_w3[0].rearrange("e (k p) n -> e p k n", p=P)
        w2e = moe_w2[0].rearrange("e (k p) n -> e p k n", p=P)

        @block.sync
        def _(sp):
            for t in range(TT):
                sp.dma_start(xres[:, t, :], x[0, t * P:(t + 1) * P, :]).then_inc(x_loaded[t], 16)
            sp.dma_start(gains, g_mix[0:1, :].to_broadcast([P, D])).then_inc(gain0_loaded, 16)

            def mixer_stream(l):
                n = before_units(l)
                for name, w, c0, ws, kt, _, _ in panels_of(l):
                    wv = w.rearrange("(k p) n -> p k n", p=P)
                    for j in range(kt // KW):
                        slot = n % MRING
                        if n >= before_units(l) + MRING:
                            sp.wait_ge(m_lo, n - MRING + 1)
                        elif l > 0:
                            sp.wait_ge(d_lo[slot % 3], NF)
                        sp.dma_start(raw[:, slot, :].rearrange("p (k n) -> p k n", k=KW),
                                     wv[:, j * KW:(j + 1) * KW, c0:c0 + UC]).then_inc(m_raw[slot], 16)
                        n += 1
                        if n == 3:
                            small_inputs()

            def small_inputs():
                for l in range(L):
                    wl_ = w_in[l].rearrange("(k p) n -> p k n", p=P)
                    sp.dma_start(wsm[:, l, :, 0:HA], wl_[:, :, C_AF:C_AF + HA]).then_inc(wsm_loaded, 16)
                    sp.dma_start(wsm[:, l, :, HA:SM], wl_[:, :, C_CA:C_CA + LR]).then_inc(wsm_loaded, 16)
                for l in range(L):
                    sp.dma_start(bf[:, l:l + 1], b_f[l].rearrange("(h a) -> h a", a=1)).then_inc(bf_loaded, 16)
                sp.dma_start(wr[:, :, :], w_router[0].rearrange("(k p) n -> p k n", p=P)).then_inc(wr_loaded, 16)

            mixer_stream(0)

            w1d = ffn_w1[0].rearrange("(k p) n -> p k n", p=P)
            w3d = ffn_w3[0].rearrange("(k p) n -> p k n", p=P)
            w2d = ffn_w2[0].rearrange("(k p) n -> p k n", p=P)

            def dense_step(s, parity, has_gu, has_w2, peeled):
                for t in range(2 if has_gu else 0):
                    slot = parity * 3 + t
                    if peeled:
                        sp.wait_ge(m_lo, last_use(NUNIT, MRING, slot))
                    else:
                        sp.wait_ge(d_lo[t], s - 1)
                    dst = raw[:, slot, :].rearrange("p (k w n) -> p k w n", k=KW, w=2)
                    sp.dma_start(dst[:, :, 0, :], w1d[:, t * KW:(t + 1) * KW, ds(s * FC, FC)]).then_inc(d_raw[slot], 16)
                    sp.dma_start(dst[:, :, 1, :], w3d[:, t * KW:(t + 1) * KW, ds(s * FC, FC)]).then_inc(d_raw[slot], 16)
                if has_w2:
                    slot = parity * 3 + 2
                    if peeled:
                        sp.wait_ge(m_lo, last_use(NUNIT, MRING, slot))
                    else:
                        sp.wait_ge(d_lo[2], s - 2)
                    sp.dma_start(raw[:, slot, :].rearrange("p (k n) -> p k n", k=2),
                                 w2d[:, ds((s - 1) * 2, 2), :]).then_inc(d_raw[slot], 16)

            dense_step(0, 0, True, False, True)
            dense_step(1, 1, True, True, True)
            for t in range(2):
                sp.wait_ge(d_lo[t], 1)
                dst = raw[:, t, :].rearrange("p (k w n) -> p k w n", k=KW, w=2)
                sp.dma_start(dst[:, :, 0, :], w1d[:, t * KW:(t + 1) * KW, 2 * FC:3 * FC]).then_inc(d_raw[t], 16)
                sp.dma_start(dst[:, :, 1, :], w3d[:, t * KW:(t + 1) * KW, 2 * FC:3 * FC]).then_inc(d_raw[t], 16)
            sp.wait_ge(m_lo, last_use(NUNIT, MRING, 2))
            sp.dma_start(raw[:, 2, :].rearrange("p (k n) -> p k n", k=2), w2d[:, 2:4, :]).then_inc(d_raw[2], 16)
            with sp.Fori(0, (NF - 3) // 2) as j:
                dense_step(2 * j + 3, 1, True, True, False)
                dense_step(2 * j + 4, 0, True, True, False)
            dense_step(NF, 1, False, True, False)

            mixer_stream(1)

            def expert_gu(e, ew, f, fs, fresh):
                for t in range(2):
                    slot = 3 * t + fs
                    if not fresh:
                        prev = NF * e + f - 3 + 1 if not isinstance(f, int) or f >= 3 else \
                            NF * (e - 1) + 3 * (per_set(fs) - 1) + fs + 1
                        sp.wait_ge(e_lo[t], prev)
                    dst = raw[:, slot, :].rearrange("p (k w n) -> p k w n", k=KW, w=2)
                    for w, src in ((0, w1e), (1, w3e)):
                        sp.dma_start(dst[:, :, w, :],
                                     src[ds(ew, 1), :, t * KW:(t + 1) * KW, ds(f * FC, FC)].rearrange(
                                         "a p k n -> p (a k) n")).then_inc(e_raw[slot], 16)

            def expert_w2(e, ew, f, fs, fresh):
                slot = 6 + fs
                if not fresh:
                    prev = NF * e + f - 3 + 1 if not isinstance(f, int) or f >= 3 else \
                        NF * (e - 1) + 3 * (per_set(fs) - 1) + fs + 1
                    sp.wait_ge(e_lo[2], prev)
                sp.dma_start(raw[:, slot, :].rearrange("p (k n) -> p k n", k=2),
                             w2e[ds(ew, 1), :, ds(f * 2, 2), :].rearrange("a p k n -> p (a k) n")).then_inc(e_raw[slot], 16)

            def expert_stream(e, ew, opening):
                fresh = isinstance(e, int) and e == 0
                for f in range(5):
                    expert_gu(e, ew, f, f % 3, fresh and f < 3)
                    if f == 2 and fresh:
                        sp.wait_ge(x_ready, 3 * TT)
                    if f >= 2:
                        expert_w2(e, ew, f - 2, f - 2, fresh)
                    elif not opening:
                        expert_w2(e - 1, ew - 1, NF - 2 + f, (NF - 2 + f) % 3, False)
                with sp.Fori(0, (NF - 5) // 3) as j:
                    for i in range(3):
                        expert_gu(e, ew, 3 * j + 5 + i, (i + 2) % 3, False)
                        expert_w2(e, ew, 3 * j + 3 + i, i, False)

            def experts_stream(k):
                expert_stream(NE * k, 0, True)
                with sp.Fori(NE * k + 1, NE * (k + 1)) as e:
                    expert_stream(e, e - NE * k, False)
                for f in (NF - 2, NF - 1):
                    expert_w2(NE * (k + 1) - 1, NE - 1, f, f % 3, False)

            sp.wait_ge(m_lo, L * NUNIT)
            experts_stream(0)
            sp.wait_ge(r_rank, 1)
            fullest = sp.value_load(most[0:1, 0:1])
            with sp.If(fullest > CAP):
                experts_stream(1)

            for t in range(TT):
                sp.wait_ge(f_scaled, t + 1)
                sp.dma_start(out[0, t * P:(t + 1) * P, :], hn[:, t, :]).then_inc(out_stored, 16)
            sp.wait_ge(out_stored, 16 * TT)

        @block.gpsimd
        def _(pool):
            def inverse_root(n):
                gain = (g_mix if n % 2 == 0 else g_ffn)[n // 2:n // 2 + 1, :] if n < 2 * L else \
                    g_final.rearrange("(a n) -> a n", a=1)
                if n % 2 == 1:
                    pool.wait_ge(mg_out, n // 2 + 1)
                elif n > 0:
                    pool.wait_ge(n_hn, TT * n)
                if n > 0:
                    pool.dma_start(gains, gain.to_broadcast([P, D])).then_inc(gain_loaded, 16)
                if n == 2 * L - 1:
                    pool.memset(xs_hi[:, :, :].bitcast(F32), 0.0).then_inc(r_zero, 1)
                    pool.memset(xs_lo[:, :, :].bitcast(F32), 0.0).then_inc(r_zero, 1)
                for t in range(TT):
                    pool.wait_ge(n_ms, TT * n + t + 1)
                    pool.tensor_tensor(rstd[:, t:t + 1], sumsq[:, t:t + 1], mhalf[:, 0:1], ALU.pow).then_inc(n_rstd, 1)

            for src, r0 in ((conv_w.rearrange("l t (c p) -> (l t c) p", p=P), R_CONV),
                            (b_a.rearrange("l (c p) -> (l c) p", p=P), R_BA),
                            (g_gla.rearrange("l (c p) -> (l c) p", p=P), R_GG),
                            (b_gate.rearrange("l (c p) -> (l c) p", p=P), R_BG)):
                pool.dma_start(prm_rows[r0:r0 + src.shape[0], :], src).then_inc(prm_loaded, 16)
            step = [0]

            def link(ins):
                step[0] += 1
                ins.then_inc(cstep, 1)
                pool.wait_ge(cstep, step[0])
            link(pool.memset(ident[:, :], 0.0))
            link(pool.affine_select(out=ident[:, :], in_=ident[:, :], compare_op=ALU.not_equal, fill=1.0,
                                    base=0, pattern=[[-1, P]], channel_multiplier=1))
            pool.memset(mhalf[:, :], -0.5).then_inc(consts, 1)
            pool.memset(obc_hi[:, :, :].bitcast(F32), 0.0).then_inc(s_zero, 1)
            pool.memset(obc_lo[:, :, :].bitcast(F32), 0.0).then_inc(s_zero, 1)
            pool.wait_ge(consts, 1)
            inverse_root(0)
            link(pool.memset(tri[:, :], 1.0))
            link(pool.memset(tri[:, 0:P], 0.0))
            link(pool.affine_select(out=tri[:, P:2 * P], in_=tri[:, P:2 * P], compare_op=ALU.is_ge, fill=0.0,
                                    base=0, pattern=[[1, P]], channel_multiplier=-1))
            link(pool.memset(cmask[:, :], 0.0))
            link(pool.affine_select(out=cmask[:, P:2 * P], in_=cmask[:, P:2 * P], compare_op=ALU.is_ge, fill=NEG,
                                    base=0, pattern=[[-1, P]], channel_multiplier=1))
            link(pool.memset(gmask[:, :], 1.0))
            link(pool.affine_select(out=gmask[:, :], in_=gmask[:, :], compare_op=ALU.is_ge, fill=0.0,
                                    base=0, pattern=[[1, P]], channel_multiplier=-1))
            link(pool.affine_select(out=gmask[:, CH:P], in_=gmask[:, CH:P], compare_op=ALU.is_ge, fill=0.0,
                                    base=-CH, pattern=[[0, P - CH]], channel_multiplier=1))
            link(pool.memset(keep[:, :], 1.0))
            for c in range(S // CH):
                link(pool.memset(keep[:, c * CH:c * CH + 1], 0.0))
            pool.memset(zrow[:, :], 0.0).then_inc(consts, 1)
            pool.memset(f_query[:, :, :], 1.0).then_inc(s_fone, 1)
            pool.memset(f_key[:, :, :], 1.0).then_inc(s_fone, 1)
            pool.wait_ge(s_fone, 2)

            for l in range(L):
                if l > 0:
                    inverse_root(2 * l)
                if l > 0:
                    pool.wait_ge(g_lin, l)
                pool.dma_start(wa2[:, :], w_a2[l]).then_inc(wa2_loaded, 16)
                pool.wait_ge(s_rows, 2 * (l + 1))
                for j in range(2):
                    pool.dma_start(f_query[0:97:32, j, :], f_rows[4 * j:4 * j + 4, 0, :]).then_inc(s_frow, 16)
                    pool.dma_start(f_key[1:98:32, j, :], f_rows[4 * j:4 * j + 4, 1, :]).then_inc(s_frow, 16)
                pool.wait_ge(g_ms, l + 1)
                pool.tensor_tensor(ors[:, :], oss[:, :], mhalf[:, 0:2 * HC], ALU.pow).then_inc(g_rstd, 1)
                inverse_root(2 * l + 1)
            pool.wait_ge(g_cum, 2 * L)
            pool.iota(iota_i, pattern=[[1, CAP]], base=0, channel_multiplier=0).then_inc(r_iota, 1)
            inverse_root(2 * L)

        @block.scalar
        def _(act):
            chain = [0]

            def link(ins):
                chain[0] += 1
                ins.then_inc(achain, 1)
                act.wait_ge(achain, chain[0])

            def square_sums(n):
                for t in range(TT):
                    if n == 0:
                        act.wait_ge(x_loaded[t], 16)
                    else:
                        act.wait_ge(x_ready, TT * (n - 1) + t + 1)
                    act.activation(hn[:, t, :], xres[:, t, :], ACT.Square, accum_out=sumsq[:, t:t + 1]).then_inc(n_sq, 1)

            def act_hi_of(n):
                for b in range(4):
                    act.wait_ge(n_tr, 4 * n + b + 1)
                    act.copy(act_hi[:, 2 * b:2 * b + 2, :].rearrange("p a t -> p (a t)"), banks(4 + b)).then_inc(n_hi, 1)

            def split_unit(l, u):
                act.wait_ge(m_raw[u % MRING], 16 * (u // MRING + 1))
                if u >= before_units(l) + SRING:
                    act.wait_ge(m_used, u - SRING + 1)
                elif l > 0:
                    act.wait_ge(d_used[u % SRING], NF)
                act.copy(w_hi[:, u % SRING, :], raw[:, u % MRING, :]).then_inc(m_hi, 1)

            def mixer(l):
                G0 = l * NPAN

                def split_panel(p):
                    for u in range(units_until(G0 + p - 1), units_until(G0 + p)):
                        split_unit(l, u)

                def done(p):
                    act.wait_ge(m_used, units_until(G0 + p))

                split_panel(1)
                act.wait_ge(s_done, l + 1)
                act.copy(aT, ps[DR:DR + LR, BO, 0:S]).then_inc(s_aTc, 1)
                act.wait_ge(s_biased, l + 1)
                link(act.activation(lsb, lsb, ACT.Exp))
                act.activation(lsb, lsb, ACT.Ln, bias=1.0).then_inc(s_ln, 1)
                done(0)
                act.copy(kT[:, :, :].rearrange("p a t -> p (a t)"), banks(0 if G0 % 2 == 0 else 2, 2)).then_inc(evac_act, 1)
                split_panel(2)
                act.wait_ge(g_neg, l + 1)
                link(act.activation(lg[2], lg[2], ACT.Exp))
                act.activation(lg[2], lg[2], ACT.Ln, bias=1.0).then_inc(g_ln, 1)
                act.wait_ge(g_cum, 2 * (l + 1))
                cumf = cum[:, :, :].rearrange("p a t -> p (a t)")
                act.activation(lg[0], cumf, ACT.Exp, scale=1.0 / 16).then_inc(g_es, 1)
                act.activation(lg[1], cumf, ACT.Exp, scale=-1.0 / 16).then_inc(g_es, 1)
                act.activation(lg[3], lg[3], ACT.Exp, scale=1.0 / 16).then_inc(g_es, 1)
                act.activation(decay[:, :, :], cum[:, :, CH - 1::CH], ACT.Exp, scale=1.0 / 16).then_inc(g_es, 1)
                done(1)
                act.mul(qT[:, :, :].rearrange("p a t -> p (a t)"), banks(2 if G0 % 2 == 0 else 0, 2), DH ** -0.5).then_inc(evac_act, 1)

                def evacuate(p):
                    name = NAMES[p]
                    bank = ((G0 + p) % 2) * 2
                    if EVAC[p] != "act":
                        return
                    done(p)
                    src = banks(bank, 2)
                    if name == "v":
                        act.copy(vA[:, :, :].rearrange("p a t -> p (a t)"), src).then_inc(evac_act, 1)
                    elif name == "cqk":
                        act.copy(cqkT.rearrange("p a t -> p (a t)"), src).then_inc(evac_act, 1)
                    elif name == "cv":
                        act.copy(vC.rearrange("p a t -> p (a t)"), src).then_inc(evac_act, 1)
                    elif name == "cr":
                        act.activation(rC.rearrange("p a t -> p (a t)"), src, ACT.Silu).then_inc(evac_act, 1)
                    elif name == "u":
                        act.copy(zB[:, :, 2:ZP], src.rearrange("p (a t) -> p a t", t=S)).then_inc(evac_act, 1)
                    else:
                        br, half = int(name[4]), int(name[5])
                        if NAMES[p] == "gate10":
                            act.wait_ge(g_in, l + 1)
                        else:
                            act.wait_ge(evac_dve, evacuated(G0 + p - 1, "dve"))
                        for c in range(4):
                            col = R_BG + l * 3 * KD + br * KD + half * 4 + c
                            ins = act.activation(gate_s[:, c, :], src[:, c * S:(c + 1) * S], ACT.Sigmoid,
                                                 bias=prm[:, col:col + 1])
                        ins.then_inc(evac_act, 1)

                def exps(h):
                    a = l * HA + h
                    act.wait_ge(a_max, a + 1)
                    act.activation(probs[:, h % 2, 0:P], probs[:, h % 2, 0:P], ACT.Exp, bias=nmx[:, 2 * h:2 * h + 1],
                                   accum_out=sm[:, 2 * h:2 * h + 1])
                    act.activation(probs[:, h % 2, P:3 * P], probs[:, h % 2, P:3 * P], ACT.Exp,
                                   bias=nmx[:, 2 * h + 1:2 * h + 2], accum_out=sm[:, 2 * h + 1:2 * h + 2]).then_inc(a_exp, 1)

                def probs_T(h):
                    a = l * HA + h
                    act.wait_ge(a_tr, a + 1)
                    if h > 0:
                        act.wait_ge(a_pv, a)
                    act.copy(probsT, ps[:, BT, 0:3 * P]).then_inc(a_pt, 1)

                def head_out(h):
                    if h % 2 == 1:
                        act.wait_ge(a_pv, l * HA + h + 1)
                        act.copy(oa_hi[:, h // 2, :], ps[:, BO, 0:S]).then_inc(a_ohi, 1)

                for p in range(2, NPAN):
                    if p + 1 < NPAN:
                        split_panel(p + 1)
                    if 0 <= p - HS < HA:
                        exps(p - HS)
                    if 0 <= p - HS - 1 < HA:
                        probs_T(p - HS - 1)
                    if 0 <= p - HS - 2 < HA:
                        head_out(p - HS - 2)
                    if NAMES[p] == "proj11":
                        act.wait_ge(g_kstT, l + 1)
                        act.copy(kst_tok, banks(BT)).then_inc(g_kst, 1)
                    if NAMES[p] == "proj00":
                        act.wait_ge(g_o, l + 1)
                        act.copy(oC, banks(BX, 2)).then_inc(g_ocopy, 1)
                    if NAMES[p] == "proj01":
                        act.wait_ge(g_oT, l + 1)
                        for h in range(HC):
                            col = R_GG + l * HC + h
                            act.activation(obc_hi[:, h, :], banks(BT, 2)[:, h * S:(h + 1) * S], ACT.Copy,
                                           scale=prm[:, col:col + 1]).then_inc(g_ohi, 1)
                    evacuate(p)
                    if NAMES[p] == "bg":
                        act.wait_ge(b_y, l + 1)
                        act.copy(obc_hi[:, :, :], cvB).then_inc(b_hi, 1)
                    if NAMES[p] == "proj21":
                        act.wait_ge(mg_sum, l + 1)
                        act.copy(act_hi[:, :, :], merged[:, :, :]).then_inc(mg_hi, 1)

            square_sums(0)
            split_unit(0, 0)
            act_hi_of(0)
            act.wait_ge(prm_tr, 1)
            act.copy(prm[:, 0:NPRM], ps[:, 3, 0:NPRM]).then_inc(prm_ready, 1)
            split_unit(0, 1)
            mixer(0)

            def dhi(t, slot, arrivals, used, first=False):
                act.wait_ge(d_raw[slot], arrivals)
                if first:
                    act.wait_ge(m_used, last_use(NUNIT, SRING, t))
                else:
                    act.wait_ge(d_used[t], used)
                act.copy(w_hi[:, t, :], raw[:, slot, :]).then_inc(d_hi[t], 1)

            def dense_hidden(s, parity, first):
                act.wait_ge(d_used[1], s + 1)
                if not first:
                    act.wait_ge(d_hT, s)
                act.activation(dsilu[:, :, :].rearrange("p a t -> p (a t)"), banks(2 * parity), ACT.Silu).then_inc(d_silu, 1)

            def dense_hidden_hi(s, first):
                act.wait_ge(d_h, s + 1)
                if not first:
                    act.wait_ge(d_used[2], s)
                act.copy(dh_hi[:, :, :], dsilu[:, :, :]).then_inc(d_hhi, 1)

            def dense_step(q, parity, up, down):
                s = 2 * q + parity
                if up and not (isinstance(s, int) and s == 0):
                    for t in range(2):
                        dhi(t, 3 * parity + t, 32 * (q + 1), s)
                if down:
                    dense_hidden(s - 1, 1 - parity, isinstance(s, int) and s == 1)
                    dhi(2, 3 * parity + 2, 16 * (q + parity), s - 1, isinstance(s, int) and s == 1)
                    dense_hidden_hi(s - 1, isinstance(s, int) and s == 1)

            dhi(1, 1, 32, None, True)
            square_sums(1)
            dhi(0, 0, 32, None, True)
            act_hi_of(1)
            dense_step(0, 1, True, True)
            with act.Fori(1, NF // 2) as q:
                dense_step(q, 0, True, True)
                dense_step(q, 1, True, True)
            dense_step(NF // 2, 0, True, True)
            dense_step(NF // 2, 1, False, True)

            u = before_units(1)
            split_unit(1, u)
            square_sums(2)
            split_unit(1, u + 1)
            act_hi_of(2)
            mixer(1)

            def ehi(t, fs, arrivals, used, first=False):
                act.wait_ge(e_raw[3 * t + fs], arrivals)
                if first:
                    act.wait_ge(m_used, last_use(L * NUNIT, SRING, t))
                else:
                    act.wait_ge(e_used[t], used)
                act.copy(w_hi[:, t, :], raw[:, 3 * t + fs, :]).then_inc(e_hi[t], 1)

            def step_gu(e, f, q, fs, first=False):
                for t in range(2):
                    ehi(t, fs, 32 * (per_set(fs) * e + q + 1), NF * e + f, first)

            def step_w2(e, f, q, fs, first=False):
                ehi(2, fs, 16 * (per_set(fs) * e + q + 1), NF * e + f + 1)

            def silu_of(e, f, bank):
                act.wait_ge(e_used[1], NF * e + f + 1)
                act.wait_ge(e_h, NF * e + f + 2)
                act.activation(esilu[:, :], ps[:, bank, 0:FC], ACT.Silu).then_inc(e_silu, 1)

            def hidden_hi(e, f):
                act.wait_ge(e_tr, NF * e + f + 2)
                act.copy(eh_hi[:, :, :].rearrange("p a t -> p (a t)"), ps[:, 3, 0:2 * CAP]).then_inc(e_hhi, 1)

            def tokens_hi(e):
                act.wait_ge(e_gath, e + 1)
                act.copy(xs_hi[:, :, :].rearrange("p a t -> p (a t)"), banks(4, 2)).then_inc(e_xhi, 1)

            def output_hi(e):
                act.wait_ge(e_used[2], NF * (e + 1) + 1)
                act.wait_ge(e_gsel, e + 1)
                act.activation(y_hi[:, :], banks(6, 2), ACT.Copy, scale=gsel[:, 0:1]).then_inc(e_yhi, 1)

            def expert(e, opening):
                fresh = isinstance(e, int) and e == 0
                if not fresh:
                    step_gu(e, 0, 0, 0)
                if not opening:
                    silu_of(e - 1, NF - 1, (NF - 1) % 3)
                tokens_hi(e)
                if not opening:
                    step_w2(e - 1, NF - 2, 3, 0)
                    hidden_hi(e - 1, NF - 2)
                for f in range(1, 5):
                    step_gu(e, f, f // 3, f % 3, fresh and f < 1)
                    silu_of(e, f - 1, (f - 1) % 3)
                    if f == 1:
                        if not opening:
                            step_w2(e - 1, NF - 1, 3, 1)
                            hidden_hi(e - 1, NF - 1)
                        continue
                    step_w2(e, f - 2, 0, f - 2)
                    hidden_hi(e, f - 2)
                    if f == 2 and not opening:
                        output_hi(e - 1)
                act.wait_ge(e_pt, e + 1)
                act.copy(pickT[:, :], ps[:, 4, 0:S]).then_inc(e_ptc, 1)
                with act.Fori(0, (NF - 5) // 3) as j:
                    for i in range(3):
                        step_gu(e, 3 * j + 5 + i, j + (5 + i) // 3, (2 + i) % 3)
                        silu_of(e, 3 * j + 4 + i, (1 + i) % 3)
                        step_w2(e, 3 * j + 3 + i, j + 1, i)
                        hidden_hi(e, 3 * j + 3 + i)

            def expert_pass(k):
                expert(NE * k, True)
                with act.Fori(NE * k + 1, NE * (k + 1)) as e:
                    expert(e, False)
                e = NE * (k + 1) - 1
                silu_of(e, NF - 1, (NF - 1) % 3)
                for f in (NF - 2, NF - 1):
                    step_w2(e, f, 3, f % 3)
                    hidden_hi(e, f)
                output_hi(e)

            ehi(0, 0, 32, None, True)
            square_sums(3)
            ehi(1, 0, 32, None, True)
            act_hi_of(3)
            act.wait_ge(r_v, 1)
            act.activation(wt2[:, :], wt2[:, :], ACT.Exp).then_inc(r_e, 1)

            expert_pass(0)
            act.wait_ge(r_rank, 1)
            fullest = act.value_load(most[0:1, 0:1])
            with act.If(fullest > CAP):
                expert_pass(1)
            square_sums(4)

        @block.vector
        def _(dve):
            chain = [0]

            def link(ins):
                chain[0] += 1
                ins.then_inc(dchain, 1)
                dve.wait_ge(dchain, chain[0])

            def f32(ap):
                return ap.bitcast(F32)

            def normalise_stream(n, scaled):
                for t in range(TT):
                    dve.wait_ge(n_sq, TT * n + t + 1)
                    dve.tensor_scalar(sumsq[:, t:t + 1], sumsq[:, t:t + 1], 1.0 / D, EPS, ALU.mult, ALU.add).then_inc(n_ms, 1)
                    dve.wait_ge(n_rstd, TT * n + t + 1)
                    if t == 0:
                        dve.wait_ge(gain_loaded if n > 0 else gain0_loaded, 16 * max(n, 1))
                    dve.scalar_tensor_tensor(out=hn[:, t, :], in0=xres[:, t, :], scalar=rstd[:, t:t + 1], in1=gains,
                                             op0=ALU.mult, op1=ALU.mult).then_inc(scaled, 1)

            def act_lo_of(n):
                for b in range(4):
                    dve.wait_ge(n_hi, 4 * n + b + 1)
                    o = act_lo[:, 2 * b:2 * b + 2, :].rearrange("p a t -> p (a t)")
                    h = f32(act_hi[:, 2 * b:2 * b + 2, :]).rearrange("p a t -> p (a t)")
                    dve.tensor_tensor(o, banks(4 + b), h, ALU.subtract).then_inc(n_act, 1)

            def log_sigmoid_prep(lin, mn, neg):
                link(dve.tensor_scalar(mn, lin, 0.0, None, ALU.min))
                return dve.scalar_tensor_tensor(out=neg, in0=mn, scalar=2.0, in1=lin, op0=ALU.mult, op1=ALU.subtract)

            def split_unit(u):
                dve.wait_ge(m_hi, u + 1)
                dve.tensor_tensor(w_lo[:, u % SRING, :], raw[:, u % MRING, :], f32(w_hi[:, u % SRING, :]),
                                  ALU.subtract).then_inc(m_lo, 1)

            def mixer(l, ahead):
                G0 = l * NPAN

                def split_panel(p):
                    for u in range(units_until(G0 + p - 1), units_until(G0 + p)):
                        split_unit(u)

                dve.wait_ge(wsm_loaded, 32 * L)
                dve.wait_ge(s_zero, 2)
                cols = ((wsm[:, l, :, 0:HA], slice(0, HA)), (wsm[:, l, :, HA:SM], slice(DR, DR + LR)))
                for w, c in cols:
                    ins = dve.tensor_copy(wsm_hi[:, :, c], w)
                link(ins)
                for w, c in cols:
                    ins = dve.tensor_tensor(wsm_lo[:, :, c], w, f32(wsm_hi[:, :, c]), ALU.subtract)
                ins.then_inc(s_split, 1)
                split_panel(1)
                dve.wait_ge(prm_ready, 1)
                dve.memset(ones8, 1.0).then_inc(dchain, 1)
                chain[0] += 1
                dve.wait_ge(bf_loaded, 16 * L)
                dve.wait_ge(s_done, l + 1)
                link(dve.tensor_scalar(logf, ps[0:HA, BO, 0:S], bf[:, l:l + 1], None, ALU.add))
                log_sigmoid_prep(logf, lsa, lsb).then_inc(s_biased, 1)
                dve.wait_ge(s_ln, l + 1)
                link(dve.tensor_tensor(logf, lsa, lsb, ALU.subtract))
                dve.tensor_tensor_scan(out=f_rows[:, 0, :], data0=ones8, data1=logf, initial=0.0, op0=ALU.mult,
                                       op1=ALU.add).then_inc(s_rows, 1)
                dve.wait_ge(s_rows, 2 * l + 1)
                dve.tensor_scalar(f_rows[:, 1, :], f_rows[:, 0, :], -1.0, None, ALU.mult).then_inc(s_rows, 1)
                split_panel(2)
                dve.wait_ge(g_lin, l + 1)
                for m in range(NPAIR):
                    col = R_BA + l * NPAIR + m
                    link(dve.tensor_scalar(lg[0][:, m * S:(m + 1) * S], ps[:, BX, m * S:(m + 1) * S],
                                           prm[:, col:col + 1], None, ALU.add))
                log_sigmoid_prep(lg[0], lg[1], lg[2]).then_inc(g_neg, 1)
                dve.wait_ge(g_ln, l + 1)
                link(dve.tensor_tensor(lg[0], lg[1], lg[2], ALU.subtract))
                for m in range(NPAIR):
                    dve.tensor_tensor_scan(out=cum[:, m, :], data0=keep[:, :], data1=lg[0][:, m * S:(m + 1) * S],
                                           initial=0.0, op0=ALU.mult, op1=ALU.add).then_inc(dchain, 1)
                chain[0] += NPAIR
                dve.wait_ge(dchain, chain[0])
                c4 = cum[:, :, :].rearrange("p m (c t) -> p m c t", t=CH)
                for m in range(NPAIR):
                    dve.tensor_tensor(lg[3][:, m * S:(m + 1) * S].rearrange("p (c t) -> p c t", t=CH),
                                      c4[:, m, :, CH - 1:CH].to_broadcast([P, S // CH, CH]), c4[:, m, :, :],
                                      ALU.subtract).then_inc(g_cum, 1)

                def evacuate(p):
                    name = NAMES[p]
                    bank = ((G0 + p) % 2) * 2
                    if EVAC[p] != "dve":
                        return
                    if name == "out1":
                        ahead()
                    else:
                        dve.wait_ge(m_used, units_until(G0 + p))
                    src = banks(bank, 2)
                    if name == "cg":
                        dve.wait_ge(evac_act, evacuated(G0 + NAMES.index("u"), "act"))
                        dve.memset(zB[:, :, 0:2], 0.0)
                        link(dve.tensor_tensor(zB[:, :, 2:ZP], zB[:, :, 2:ZP], src.rearrange("p (a t) -> p a t", t=S),
                                               ALU.mult))
                        dve.sem_inc(evac_dve, 1)
                        for tap in range(3):
                            for c in range(4):
                                col = R_CONV + (l * 3 + tap) * 4 + c
                                w = prm[:, col:col + 1]
                                if tap == 0:
                                    link(dve.tensor_scalar(cvB[:, c, :], zB[:, c, 0:S], w, None, ALU.mult))
                                else:
                                    link(dve.scalar_tensor_tensor(out=cvB[:, c, :], in0=zB[:, c, tap:tap + S], scalar=w,
                                                                  in1=cvB[:, c, :], op0=ALU.mult, op1=ALU.add))
                    elif name == "bg":
                        cvf = cvB.rearrange("p a t -> p (a t)")
                        link(dve.tensor_tensor(cvf, cvf, src, ALU.mult))
                        dve.sem_inc(evac_dve, 1)
                        dve.sem_inc(b_y, 1)
                        dve.wait_ge(b_hi, l + 1)
                        dve.tensor_tensor(obc_lo[:, :, :], cvB, f32(obc_hi[:, :, :]), ALU.subtract).then_inc(b_out, 1)
                    elif name.startswith("proj"):
                        half = int(name[5])
                        dve.wait_ge(evac_act, evacuated(G0 + p - 1, "act"))
                        mh = merged[:, half * 4:half * 4 + 4, :].rearrange("p a t -> p (a t)")
                        gs = gate_s.rearrange("p a t -> p (a t)")
                        if name[4] == "1":
                            dve.tensor_tensor(mh, gs, src, ALU.mult).then_inc(evac_dve, 1)
                        else:
                            pr = prod_s.rearrange("p a t -> p (a t)")
                            link(dve.tensor_tensor(pr, gs, src, ALU.mult))
                            dve.sem_inc(evac_dve, 1)
                            ins = dve.tensor_tensor(mh, mh, pr, ALU.add)
                            link(ins)
                    else:
                        half = int(name[3])
                        cols = slice(half * UC, (half + 1) * UC)
                        for t in range(TT):
                            if half == 1:
                                dve.wait_ge(o_tile if t == 0 else m_used, l + 1 if t == 0 else units_until(G0 + p))
                            ins = dve.tensor_tensor(xres[:, t, cols], xres[:, t, cols], src[:, t * UC:(t + 1) * UC], ALU.add)
                            if half == 0:
                                ins.then_inc(dchain, 1)
                                chain[0] += 1
                            else:
                                ins.then_inc(x_ready, 1)
                        if half == 0:
                            dve.wait_ge(dchain, chain[0])
                        else:
                            dve.wait_ge(x_ready, TT * (2 * l + 1))
                        dve.sem_inc(evac_dve, 1)

                def scores(h):
                    a = l * HA + h
                    dve.wait_ge(a_score, a + 1)
                    if h >= 2:
                        dve.wait_ge(a_tr, a - 1)
                    bank = BX + h % 2
                    dve.tensor_tensor_reduce(out=probs[:, h % 2, 0:P], in0=ps[:, bank, 0:P], in1=cmask[:, P:2 * P],
                                             scale=1.0, scalar=-3e38, op0=ALU.add, op1=ALU.max,
                                             accum_out=mx[:, 2 * h:2 * h + 1])
                    link(dve.tensor_tensor_reduce(out=probs[:, h % 2, P:3 * P], in0=ps[:, bank, P:3 * P],
                                                  in1=cmask[:, :], scale=1.0, scalar=-3e38, op0=ALU.add, op1=ALU.max,
                                                  accum_out=mx[:, 2 * h + 1:2 * h + 2]))
                    dve.tensor_scalar(nmx[:, 2 * h:2 * h + 2], mx[:, 2 * h:2 * h + 2], -1.0, None,
                                      ALU.mult).then_inc(a_max, 1)

                def normalise(h):
                    a = l * HA + h
                    dve.wait_ge(a_exp, a + 1)
                    link(dve.reciprocal(rs[:, 2 * h:2 * h + 2], sm[:, 2 * h:2 * h + 2]))
                    dve.tensor_scalar(probs[:, h % 2, 0:P], probs[:, h % 2, 0:P], rs[:, 2 * h:2 * h + 1], None, ALU.mult)
                    dve.tensor_scalar(probs[:, h % 2, P:3 * P], probs[:, h % 2, P:3 * P], rs[:, 2 * h + 1:2 * h + 2],
                                      None, ALU.mult).then_inc(a_prob, 1)

                def head_out(h):
                    if h % 2 == 1:
                        dve.wait_ge(a_ohi, l * HA // 2 + h // 2 + 1)
                        dve.tensor_tensor(oa_lo[:, h // 2, :], ps[:, BO, 0:S], f32(oa_hi[:, h // 2, :]),
                                          ALU.subtract).then_inc(a_out, 1)

                for p in range(2, NPAN):
                    if 0 <= p - HS < HA:
                        scores(p - HS)
                    if p + 1 < NPAN:
                        split_panel(p + 1)
                    if 0 <= p - HS < HA:
                        normalise(p - HS)
                    if 0 <= p - HS - 2 < HA:
                        head_out(p - HS - 2)
                    if NAMES[p] == "cqk":
                        dve.wait_ge(evac_act, evacuated(G0 + p, "act"))
                        dve.wait_ge(g_es, 4 * (l + 1))
                        cq = cqkT[:, 0:NPAIR, :].rearrange("p a t -> p (a t)")
                        ck = cqkT[:, NPAIR:2 * NPAIR, :].rearrange("p a t -> p (a t)")
                        link(dve.tensor_tensor(kst.rearrange("p a t -> p (a t)"), ck, lg[3], ALU.mult))
                        dve.tensor_tensor(ck, ck, lg[1], ALU.mult)
                        link(dve.scalar_tensor_tensor(out=cq, in0=cq, scalar=DK ** -0.5, in1=lg[0], op0=ALU.mult,
                                                      op1=ALU.mult))
                        dve.sem_inc(g_in, 1)
                    if NAMES[p] == "proj11":
                        dve.wait_ge(g_att, l + 1)
                        m3 = gmask[:, :].rearrange("p (a q) -> p a q", a=1).to_broadcast([P, 8, P])
                        dve.tensor_tensor(attC.rearrange("p (a q) -> p a q", q=P),
                                          banks(BX, 2).rearrange("p (a q) -> p a q", q=P), m3, ALU.mult).then_inc(g_attm, 1)
                    if NAMES[p] == "gate00":
                        dve.wait_ge(g_kv, l + 1)
                        link(dve.tensor_copy(states[:, 0, :, :].rearrange("p m e -> p (m e)"), ps[:, BO, 0:NPAIR * DV]))
                        for c in range(1, 3):
                            src = ps[:, BO, 256:512] if c == 2 else ps[:, BT, 0:256]
                            for m in range(NPAIR):
                                ins = dve.scalar_tensor_tensor(out=states[:, c, m, :], in0=states[:, c - 1, m, :],
                                                               scalar=decay[:, m, c:c + 1],
                                                               in1=src[:, m * DV:(m + 1) * DV], op0=ALU.mult, op1=ALU.add)
                            link(ins)
                        dve.sem_inc(g_state, 1)
                    if NAMES[p] == "gate01":
                        dve.wait_ge(g_ocopy, l + 1)
                        o3 = oC.rearrange("p (a e) -> p a e", e=DV)
                        s3 = sqC.rearrange("p a (b e) -> p a b e", e=DV)
                        link(dve.tensor_tensor(sqC, oC.rearrange("p (a t) -> p a t", t=S),
                                               oC.rearrange("p (a t) -> p a t", t=S), ALU.mult))
                        link(dve.tensor_reduce(out=oss[:, :], in_=s3, axis=AX.X, op=ALU.add))
                        dve.tensor_scalar(oss[:, :], oss[:, :], 1.0 / DV, EPS, ALU.mult, ALU.add).then_inc(g_ms, 1)
                        dve.wait_ge(g_rstd, l + 1)
                        link(dve.tensor_tensor(o3, o3, ors[:, :].rearrange("p (a b) -> p a b", b=1).to_broadcast([P, 8, DV]),
                                               ALU.mult))
                        r5 = rC.rearrange("p t (m r e) -> p t m r e", m=NPAIR, r=2)
                        o5 = oC.rearrange("p (r t m e) -> p r t m e", r=2, t=TT, m=NPAIR)
                        for r in range(2):
                            for t in range(TT):
                                ins = dve.tensor_tensor(o5[:, r, t, :, :], o5[:, r, t, :, :], r5[:, t, :, r, :], ALU.mult)
                        ins.then_inc(g_on, 1)
                    if NAMES[p] == "proj01":
                        for h in range(HC):
                            col = R_GG + l * HC + h
                            dve.wait_ge(g_ohi, l * HC + h // 2 * 2 + 2)
                            dve.scalar_tensor_tensor(out=obc_lo[:, h, :], in0=banks(BT, 2)[:, h * S:(h + 1) * S],
                                                     scalar=prm[:, col:col + 1], in1=f32(obc_hi[:, h, :]), op0=ALU.mult,
                                                     op1=ALU.subtract).then_inc(g_out, 1)
                    evacuate(p)
                    if NAMES[p] == "proj21":
                        dve.sem_inc(mg_sum, 1)
                        dve.wait_ge(mg_hi, l + 1)
                        dve.tensor_tensor(act_lo[:, :, :], merged[:, :, :], f32(act_hi[:, :, :]),
                                          ALU.subtract).then_inc(mg_out, 1)

            def dlo(t, slot, s):
                dve.wait_ge(d_hi[t], s + 1)
                dve.tensor_tensor(w_lo[:, t, :], raw[:, slot, :], f32(w_hi[:, t, :]), ALU.subtract).then_inc(d_lo[t], 1)

            normalise_stream(0, n_hn)
            split_unit(0)
            act_lo_of(0)
            split_unit(1)
            dve.wait_ge(consts, 2)
            mixer(0, lambda: dlo(1, 1, 0))
            normalise_stream(1, n_hn)
            dlo(0, 0, 0)
            act_lo_of(1)

            def dense_hidden(s, parity):
                dve.wait_ge(d_silu, s + 1)
                f = dsilu[:, :, :].rearrange("p a t -> p (a t)")
                dve.tensor_tensor(f, f, banks(2 * parity + 1), ALU.mult).then_inc(d_h, 1)

            def dense_hidden_lo(s):
                dve.wait_ge(d_hhi, s + 1)
                dve.tensor_tensor(dh_lo[:, :, :], dsilu[:, :, :], f32(dh_hi[:, :, :]), ALU.subtract).then_inc(d_hT, 1)

            def dense_step(q, parity, up, down):
                s = 2 * q + parity
                if up:
                    for t in range(2):
                        dlo(t, 3 * parity + t, s)
                if down:
                    dense_hidden(s - 1, 1 - parity)
                    dlo(2, 3 * parity + 2, s - 1)
                    dense_hidden_lo(s - 1)

            dense_step(0, 1, True, True)
            with dve.Fori(1, NF // 2) as q:
                dense_step(q, 0, True, True)
                dense_step(q, 1, True, True)
            dense_step(NF // 2, 0, True, True)
            dense_step(NF // 2, 1, False, True)
            u = before_units(1)
            split_unit(u)
            for t in range(TT):
                dve.wait_ge(d_tile if t == 0 else d_used[2], 1 if t == 0 else NF)
                dve.tensor_tensor(xres[:, t, :], xres[:, t, :], banks(4 + 2 * t, 2), ALU.add).then_inc(x_ready, 1)
            normalise_stream(2, n_hn)
            split_unit(u + 1)
            act_lo_of(2)

            def elo(t, fs, s):
                dve.wait_ge(e_hi[t], s + 1)
                dve.tensor_tensor(w_lo[:, t, :], raw[:, 3 * t + fs, :], f32(w_hi[:, t, :]),
                                  ALU.subtract).then_inc(e_lo[t], 1)

            def step_gu(e, f, fs):
                for t in range(2):
                    elo(t, fs, NF * e + f)

            def hidden(e, f, bank):
                dve.wait_ge(e_silu, NF * e + f + 1)
                dve.wait_ge(e_tr, NF * e + f + 1)
                dve.tensor_tensor(hid[:, :], esilu[:, :], ps[:, bank, FC:2 * FC], ALU.mult).then_inc(e_h, 1)

            def hidden_lo(e, f):
                dve.wait_ge(e_hhi, NF * e + f + 1)
                dve.tensor_tensor(eh_lo[:, :, :].rearrange("p a t -> p (a t)"), ps[:, 3, 0:2 * CAP],
                                  f32(eh_hi[:, :, :]).rearrange("p a t -> p (a t)"), ALU.subtract).then_inc(e_hT, 1)

            def pick_of(e, ew):
                for t in range(TT):
                    dve.tensor_scalar(pick[:, t, :], iota[:, :], rank[:, t, ds(ew, 1)], None, ALU.is_equal).then_inc(e_pick, 1)

            def tokens_lo(e):
                dve.wait_ge(e_xhi, e + 1)
                dve.tensor_tensor(xs_lo[:, :, :].rearrange("p a t -> p (a t)"), banks(4, 2),
                                  f32(xs_hi[:, :, :]).rearrange("p a t -> p (a t)"), ALU.subtract).then_inc(e_x, 1)

            def output_lo(e):
                dve.wait_ge(e_yhi, e + 1)
                dve.wait_ge(e_gsel, e + 1)
                dve.scalar_tensor_tensor(out=y_lo[:, :], in0=banks(6, 2), scalar=gsel[:, 0:1], in1=f32(y_hi[:, :]),
                                         op0=ALU.mult, op1=ALU.subtract).then_inc(e_ylo, 1)

            def scatter_add(e, t):
                dve.wait_ge(e_sc, TT * e + t + 1)
                dve.wait_ge(e_add, TT * e + t + 1)
                dve.tensor_tensor(xres[:, t, :], xres[:, t, :], banks(4, 2), ALU.add).then_inc(e_add, 1)

            def wide(v):
                return v[:, :].rearrange("p (t a) -> p t a", a=1).to_broadcast([P, TT, NE])

            def routing_gates():
                dve.wait_ge(r_e, 1)
                link(dve.tensor_scalar(wt1[:, :], wt2[:, :], 1.0, None, ALU.add))
                link(dve.reciprocal(wt1[:, :], wt1[:, :]))
                link(dve.tensor_tensor(wt2[:, :], wt2[:, :], wt1[:, :], ALU.mult))
                link(dve.tensor_tensor(first[:, :, :], first[:, :, :], wide(wt1), ALU.mult))
                link(dve.tensor_tensor(second[:, :, :], second[:, :, :], wide(wt2), ALU.mult))
                dve.tensor_tensor(gates[:, :, :], first[:, :, :], second[:, :, :], ALU.add).then_inc(r_gates, 1)

            def expert(e, ew, opening):
                if not (isinstance(e, int) and e == 0):
                    step_gu(e, 0, 0)
                if not opening:
                    hidden(e - 1, NF - 1, (NF - 1) % 3)
                tokens_lo(e)
                if isinstance(e, int) and e == 0:
                    routing_gates()
                if not opening:
                    elo(2, 0, NF * (e - 1) + NF - 2)
                    hidden_lo(e - 1, NF - 2)
                for f in range(1, 5):
                    step_gu(e, f, f % 3)
                    hidden(e, f - 1, (f - 1) % 3)
                    if f == 1:
                        if not opening:
                            elo(2, 1, NF * (e - 1) + NF - 1)
                            hidden_lo(e - 1, NF - 1)
                        continue
                    if f >= 3 and not opening:
                        scatter_add(e - 1, f - 3)
                    elo(2, f - 2, NF * e + f - 2)
                    hidden_lo(e, f - 2)
                    if f == 2 and not opening:
                        output_lo(e - 1)
                dve.wait_ge(e_pt, e + 1)
                dve.tensor_copy(gsel[:, :], ps[:, 5, ds(ew, 1)]).then_inc(e_gsel, 1)
                pick_of(e + 1, ew + 1)
                with dve.Fori(0, (NF - 5) // 3) as j:
                    for i in range(3):
                        step_gu(e, 3 * j + 5 + i, (2 + i) % 3)
                        hidden(e, 3 * j + 4 + i, (1 + i) % 3)
                        elo(2, i, NF * e + 3 * j + 3 + i)
                        hidden_lo(e, 3 * j + 3 + i)

            def expert_pass(k):
                expert(NE * k, 0, True)
                with dve.Fori(NE * k + 1, NE * (k + 1)) as e:
                    expert(e, e - NE * k, False)
                e = NE * (k + 1) - 1
                hidden(e, NF - 1, (NF - 1) % 3)
                for f in (NF - 2, NF - 1):
                    elo(2, f % 3, NF * e + f)
                    hidden_lo(e, f)
                output_lo(e)
                for t in range(TT):
                    scatter_add(e, t)

            dve.sem_inc(e_h, 2)
            dve.sem_inc(e_add, 1)

            def ahead_of_experts():
                elo(0, 0, 0)
                dve.wait_ge(wr_loaded, 16)
                dve.wait_ge(r_zero, 2)
                link(dve.tensor_copy(xs_hi[:, :, 0:NE], wr[:, :, :]))
                dve.tensor_tensor(xs_lo[:, :, 0:NE], wr[:, :, :], f32(xs_hi[:, :, 0:NE]), ALU.subtract).then_inc(r_split, 1)

            mixer(1, ahead_of_experts)
            normalise_stream(3, n_hn)
            elo(1, 0, 0)
            act_lo_of(3)

            dve.wait_ge(r_iota, 1)
            link(dve.tensor_copy(iota[:, :], iota_i))
            link(dve.memset(one8[:, :], 1.0))
            link(dve.memset(rank[:, :, NE:NE + 1], -1.0))
            dve.wait_ge(r_logit, 1)
            dve.tensor_copy(lgT[:, :], ps[0:NE, 0, 0:S]).then_inc(r_lgT, 1)
            dve.wait_ge(r_logit, 2)
            lf = lgt[:, :, :].rearrange("p t e -> p (t e)")
            link(dve.tensor_copy(lf, ps[:, 1, 0:TT * NE]))

            def first_of_largest(src, v, pickd):
                link(dve.tensor_reduce(out=v[:, :], in_=src[:, :, :], axis=AX.X, op=ALU.max))
                link(dve.tensor_tensor(eq[:, :, :], src[:, :, :], wide(v), ALU.is_equal))
                for t in range(TT):
                    ins = dve.tensor_tensor_scan(out=cnt[:, t, :], data0=eq[:, t, :], data1=one8[:, :], initial=0.0,
                                                 op0=ALU.add, op1=ALU.mult)
                    link(ins)
                link(dve.scalar_tensor_tensor(out=pickd[:, :, :], in0=cnt[:, :, :], scalar=1.0, in1=eq[:, :, :],
                                              op0=ALU.is_le, op1=ALU.mult))
            first_of_largest(lgt, v1, first)
            link(dve.scalar_tensor_tensor(out=lgt2[:, :, :], in0=first[:, :, :], scalar=-3e38, in1=lgt[:, :, :],
                                          op0=ALU.mult, op1=ALU.add))
            first_of_largest(lgt2, v2, second)
            dve.tensor_tensor(wt2[:, :], v2[:, :], v1[:, :], ALU.subtract).then_inc(r_v, 1)
            dve.tensor_tensor(chosen[:, :, :], first[:, :, :], second[:, :, :], ALU.add).then_inc(r_chosen, 1)
            dve.wait_ge(r_cum, 1)
            link(dve.tensor_tensor(rank[:, :, 0:NE], ps[:, BY, 0:TT * NE].rearrange("p (t e) -> p t e", e=NE),
                                   chosen[:, :, :], ALU.mult))
            link(dve.tensor_scalar(rank[:, :, 0:NE], rank[:, :, 0:NE], -1.0, None, ALU.add))
            dve.tensor_reduce(out=most[:, :], in_=ps[:, BY, TT * NE:(TT + 1) * NE], axis=AX.X, op=ALU.max).then_inc(r_rank, 1)

            dve.wait_ge(r_rank, 1)
            pick_of(0, 0)
            expert_pass(0)
            fullest = dve.value_load(most[0:1, 0:1])
            with dve.If(fullest > CAP):
                dve.wait_ge(e_pick, 2 * (NE + 1))
                link(dve.tensor_scalar(rank[:, :, 0:NE], rank[:, :, 0:NE], -float(CAP), None, ALU.add))
                for t in range(TT):
                    dve.tensor_scalar(pick[:, t, :], iota[:, :], rank[:, t, 0:1], None, ALU.is_equal).then_inc(e_again, 1)
                expert_pass(1)
                dve.wait_ge(e_add, 2 * TT * NE + 1)
            dve.wait_ge(e_add, TT * NE + 1)
            dve.sem_inc(x_ready, TT)
            normalise_stream(4, f_scaled)

        @block.tensor
        def _(pe):
            def mm3(o, a_hi, a_lo, b_hi, b_lo, start, stop):
                pe.matmul(o, a_hi, b_hi, start=start, stop=False, skip_group_check=True)
                pe.matmul(o, a_hi, b_lo, start=False, stop=False, skip_group_check=True)
                return pe.matmul(o, a_lo, b_hi, start=False, stop=stop, skip_group_check=True)

            def norm(n):
                for t in range(TT):
                    pe.wait_ge(n_hn, TT * n + t + 1)
                    for k in range(KD):
                        ins = pe.transpose(ps[:, 4 + k // 2, (k % 2) * S + t * P:(k % 2) * S + (t + 1) * P],
                                           hn[:, t, k * P:(k + 1) * P], ident[:, :])
                        if t == TT - 1 and k % 2 == 1:
                            ins.then_inc(n_tr, 1)

            def stream_ready(n, k):
                if k % 2 == 0:
                    pe.wait_ge(n_act, 4 * n + k // 2 + 1)

            def mixer(l):
                n = [before_units(l)]
                G0 = l * NPAN
                operands = {"act": (act_hi, act_lo), "o0": (oa_hi, oa_lo), "o1": (obc_hi, obc_lo),
                            "o2": (obc_hi, obc_lo)}

                def panel(p):
                    name, _, _, ws, kt, operand, _ = panels_of(l)[p]
                    g = G0 + p
                    b0 = (g % 2) * 2
                    if p >= 2:
                        who = EVAC[p - 2]
                        pe.wait_ge(evac_act if who == "act" else evac_dve, evacuated(g - 2, who))
                    if name == "proj10":
                        pe.wait_ge(b_out, l + 1)
                    if name == "proj00":
                        pe.wait_ge(a_out, HA // 2 * (l + 1))
                    if name == "proj20":
                        pe.wait_ge(g_out, HC * (l + 1))
                    if name == "out0":
                        pe.wait_ge(mg_out, l + 1)
                    hi, lo = operands[operand]
                    for j in range(kt // KW):
                        u = n[0]
                        pe.wait_ge(m_lo, u + 1)
                        steps = [(kk, c) for kk in range(KW) for c in range(4)] if ws else \
                            [(kk, c) for c in range(TT) for kk in range(KW)]
                        for kk, c in steps:
                            k = j * KW + kk
                            last = k == kt - 1
                            if p == 0 and c == 0:
                                stream_ready(2 * l, k)
                            if ws:
                                w = slice(kk * UC + c * P, kk * UC + (c + 1) * P)
                                ins = mm3(ps[:, b0 + c // 2, (c % 2) * S:(c % 2 + 1) * S],
                                          w_hi[:, u % SRING, w], w_lo[:, u % SRING, w], hi[:, k, :], lo[:, k, :],
                                          k == 0 and c % 2 == 0, last)
                            else:
                                w = slice(kk * UC, (kk + 1) * UC)
                                tok = slice(c * P, (c + 1) * P)
                                ins = mm3(ps[:, b0 + c, :], hi[:, k, tok], lo[:, k, tok],
                                          w_hi[:, u % SRING, w], w_lo[:, u % SRING, w], k == 0, last)
                                if last and name == "out1" and c == 0:
                                    ins.then_inc(o_tile, 1)
                        ins.then_inc(m_used, 1)
                        n[0] += 1

                def narrow():
                    pe.wait_ge(n_act, 4 * (2 * l + 1))
                    pe.wait_ge(s_split, l + 1)
                    for k in range(KD):
                        ins = mm3(ps[0:NW, BO, 0:S], wsm_hi[:, k, :], wsm_lo[:, k, :], act_hi[:, k, :], act_lo[:, k, :],
                                  k == 0, k == KD - 1)
                    ins.then_inc(s_done, 1)

                def decay_logits():
                    pe.wait_ge(s_aTc, l + 1)
                    pe.wait_ge(wa2_loaded, 16 * (l + 1))
                    for m in range(NPAIR):
                        ins = pe.matmul(ps[:, BX, m * S:(m + 1) * S], wa2[:, m * P:(m + 1) * P], aT,
                                        start=m == 0, stop=True, skip_group_check=True)
                    ins.then_inc(g_lin, 1)

                def head_scores(h):
                    a = l * HA + h
                    if h == 0:
                        pe.wait_ge(s_frow, 64 * (l + 1))
                        pe.wait_ge(evac_act, evacuated(G0 + 1, "act"))
                        pe.wait_ge(s_rows, 2 * (l + 1))
                        pe.wait_ge(g_neg, l + 1)
                    if h >= 2:
                        pe.wait_ge(a_max, a - 1)
                    r, m, g = (h % 2) * DH, h // 2, 32 * (h % 4)
                    bank = BX + h % 2
                    for t, cols in ((0, slice(0, P)), (1, slice(P, 3 * P))):
                        q = slice(t * P, (t + 1) * P)
                        nk = (t + 1) * P
                        pe.matmul(ps[:, bank, cols], qT[r:r + DH, m, q], kT[r:r + DH, m, 0:nk], start=True, stop=False)
                        ins = pe.matmul(ps[:, bank, cols], f_query[g:g + 2, h // 4, q], f_key[g:g + 2, h // 4, 0:nk],
                                        start=False, stop=True)
                    ins.then_inc(a_score, 1)

                def head_transpose(h):
                    a = l * HA + h
                    pe.wait_ge(a_prob, a + 1)
                    if h > 0:
                        pe.wait_ge(a_pt, a)
                    for i in range(3):
                        ins = pe.transpose(ps[:, BT, i * P:(i + 1) * P], probs[:, h % 2, i * P:(i + 1) * P], ident[:, :])
                    ins.then_inc(a_tr, 1)

                def head_values(h):
                    a = l * HA + h
                    pe.wait_ge(a_pt, a + 1)
                    if h % 2 == 0:
                        if h > 0:
                            pe.wait_ge(a_out, HA // 2 * l + h // 2)
                        else:
                            pe.wait_ge(evac_act, evacuated(G0 + 2, "act"))
                    r = (h % 2) * DH
                    v = slice(h * DH, (h + 1) * DH)
                    pe.matmul(ps[r:r + DH, BO, 0:S], vA[:, 0, v], probsT[:, 0:S], start=True, stop=False)
                    pe.matmul(ps[r:r + DH, BO, P:S], vA[:, 1, v], probsT[:, 2 * P:3 * P], start=False,
                              stop=True).then_inc(a_pv, 1)

                def gla_scores():
                    pe.wait_ge(g_in, l + 1)
                    pe.wait_ge(a_max, HA * (l + 1))
                    for r in range(2):
                        for t in range(TT):
                            for m in range(NPAIR):
                                rows, tok = slice(r * DK, (r + 1) * DK), slice(t * P, (t + 1) * P)
                                c = (t * NPAIR + m) * P
                                ins = pe.matmul(ps[:, BX + r, c:c + P], cqkT[rows, NPAIR + m, tok], cqkT[rows, m, tok],
                                                start=c == 0, stop=True, skip_group_check=True)
                    ins.then_inc(g_att, 1)
                    pe.wait_ge(a_pt, HA * (l + 1))
                    for t in range(TT):
                        for m in range(NPAIR):
                            c = (t * NPAIR + m) * P
                            ins = pe.transpose(ps[:, BT, c:c + P], kst[:, m, t * P:(t + 1) * P], ident[:, :])
                    ins.then_inc(g_kstT, 1)

                def gla_states():
                    pe.wait_ge(g_kst, l + 1)
                    pe.wait_ge(a_out, HA // 2 * (l + 1))
                    for i, c in enumerate((0, 2, 1)):
                        bank, col = (BT, 0) if c == 1 else (BO, (c // 2) * NPAIR * DV)
                        rows = slice((c % 2) * CH, (c % 2 + 1) * CH)
                        for m in range(NPAIR):
                            for r in range(2):
                                kc = ((c // 2) * NPAIR + m) * P + r * DK
                                h = 2 * m + r
                                ins = pe.matmul(ps[r * DK:(r + 1) * DK, bank, col + m * DV:col + (m + 1) * DV],
                                                kst_tok[rows, kc:kc + DK], vC[rows, c // 2, h * DV:(h + 1) * DV],
                                                start=(i != 1 and m == 0), stop=True, skip_group_check=True)
                    ins.then_inc(g_kv, 1)

                def gla_out():
                    pe.wait_ge(g_attm, l + 1)
                    for r in range(2):
                        for t in range(TT):
                            for m in range(NPAIR):
                                c = (t * NPAIR + m) * P
                                h = 2 * m + r
                                pe.matmul(ps[:, BX + r, c:c + P], attC[:, r * 4 * P + c:r * 4 * P + c + P],
                                          vC[:, t, h * DV:(h + 1) * DV], start=c == 0, stop=False, skip_group_check=True)
                    pe.wait_ge(g_state, l + 1)
                    for r in range(2):
                        rows = slice(r * DK, (r + 1) * DK)
                        for c in range(1, S // CH):
                            for m in range(NPAIR):
                                col = ((c // 2) * NPAIR + m) * P
                                ins = pe.matmul(ps[(c % 2) * CH:(c % 2 + 1) * CH, BX + r, col:col + P],
                                                cqkT[rows, m, c * CH:(c + 1) * CH], states[rows, c - 1, m, :],
                                                start=False, stop=True, skip_group_check=True)
                    ins.then_inc(g_o, 1)

                def gla_transpose():
                    pe.wait_ge(g_on, l + 1)
                    for h in range(HC):
                        for t in range(TT):
                            c = (((h % 2) * TT + t) * NPAIR + h // 2) * P
                            ins = pe.transpose(banks(BT, 2)[:, h * S + t * P:h * S + (t + 1) * P], oC[:, c:c + P],
                                               ident[:, :])
                    ins.then_inc(g_oT, 1)

                panel(0)
                narrow()
                if l == 0:
                    pe.wait_ge(prm_ready, 1)
                panel(1)
                decay_logits()
                for p in range(2, NPAN):
                    if 0 <= p - HS < HA:
                        head_scores(p - HS)
                    if 0 <= p - HS - 1 < HA:
                        head_transpose(p - HS - 1)
                    if 0 <= p - HS - 2 < HA:
                        head_values(p - HS - 2)
                    if NAMES[p] == "proj11":
                        gla_scores()
                    if NAMES[p] == "gate00":
                        gla_states()
                    if NAMES[p] == "proj00":
                        gla_out()
                    if NAMES[p] == "proj01":
                        gla_transpose()
                    panel(p)

            pe.wait_ge(consts, 1)
            norm(0)
            pe.wait_ge(prm_loaded, 64)
            pe.transpose(ps[:, 3, 0:NPRM], prm_rows, ident[0:NPRM, 0:NPRM]).then_inc(prm_tr, 1)
            mixer(0)
            norm(1)

            def up(s, parity):
                for t in range(2):
                    pe.wait_ge(d_lo[t], s + 1)
                    w_h = w_hi[:, t, :].rearrange("p (k w n) -> p k w n", k=KW, w=2)
                    w_l = w_lo[:, t, :].rearrange("p (k w n) -> p k w n", k=KW, w=2)
                    for kk in range(KW):
                        k = t * KW + kk
                        if isinstance(s, int) and s == 0:
                            stream_ready(1, k)
                        for w in range(2):
                            for c in range(2):
                                cc = slice(c * P, (c + 1) * P)
                                ins = mm3(ps[:, 2 * parity + w, c * S:(c + 1) * S], w_h[:, kk, w, cc], w_l[:, kk, w, cc],
                                          act_hi[:, k, :], act_lo[:, k, :], k == 0 and c == 0, k == KD - 1)
                    ins.then_inc(d_used[t], 1)

            def down(s, stop):
                pe.wait_ge(d_hT, s + 1)
                pe.wait_ge(d_lo[2], s + 1)
                for t in range(TT):
                    for k in range(2):
                        tok = slice(t * P, (t + 1) * P)
                        for half in range(2):
                            cols = slice(k * D + half * UC, k * D + (half + 1) * UC)
                            ins = mm3(ps[:, 4 + 2 * t + half, :], dh_hi[:, k, tok], dh_lo[:, k, tok],
                                      w_hi[:, 2, cols], w_lo[:, 2, cols], False, stop and k == 1)
                    if stop and t == 0:
                        ins.then_inc(d_tile, 1)
                ins.then_inc(d_used[2], 1)

            def open_sums(first, nb):
                for b in range(first, first + nb):
                    pe.matmul(ps[:, b, :], zrow[0:1, 0:P], zrow[0:1, :], start=True, stop=False, skip_group_check=True)

            up(0, 0)
            up(1, 1)
            open_sums(4, 4)
            down(0, False)
            with pe.Fori(0, (NF - 3) // 2) as j:
                for i in range(2):
                    s = 2 * j + 2 + i
                    pe.wait_ge(d_h, s - 1)
                    up(s, i)
                    down(s - 1, False)
            pe.wait_ge(d_h, NF - 2)
            up(NF - 1, (NF - 1) % 2)
            down(NF - 2, False)
            down(NF - 1, True)

            norm(2)
            mixer(1)
            norm(3)

            pe.wait_ge(r_split, 1)
            for k in range(KD):
                stream_ready(3, k)
                ins = mm3(ps[0:NW, 0, 0:S], xs_hi[:, k, 0:NW], xs_lo[:, k, 0:NW], act_hi[:, k, :], act_lo[:, k, :],
                          k == 0, k == KD - 1)
            ins.then_inc(r_logit, 1)
            pe.wait_ge(r_lgT, 1)
            for t in range(TT):
                ins = pe.transpose(ps[:, 1, t * NE:(t + 1) * NE], lgT[:, t * P:(t + 1) * P], ident[0:NE, 0:NE])
            ins.then_inc(r_logit, 1)
            pe.wait_ge(r_chosen, 1)
            for t in range(TT):
                for s in range(TT):
                    ins = pe.matmul(ps[:, BY, t * NE:(t + 1) * NE], tri[:, (1 - s + t) * P:(2 - s + t) * P], chosen[:, s, :],
                                    start=t == 0 and s == 0, stop=s == TT - 1, skip_group_check=True)
            for s in range(TT):
                ins = pe.matmul(ps[:, BY, TT * NE:(TT + 1) * NE], tri[:, 2 * P:3 * P], chosen[:, s, :], start=False,
                                stop=s == TT - 1, skip_group_check=True)
            ins.then_inc(r_cum, 1)

            def eup(e, f, bank):
                for t in range(2):
                    pe.wait_ge(e_lo[t], NF * e + f + 1)
                    for kk in range(KW):
                        k = t * KW + kk
                        cols = slice(kk * UC, (kk + 1) * UC)
                        ins = mm3(ps[:, bank, :], xs_hi[:, k, :], xs_lo[:, k, :], w_hi[:, t, cols], w_lo[:, t, cols],
                                  k == 0, k == KD - 1)
                    ins.then_inc(e_used[t], 1)

            def edown(e, f, stop=False):
                pe.wait_ge(e_hT, NF * e + f + 1)
                pe.wait_ge(e_lo[2], NF * e + f + 1)
                for k in range(2):
                    for half in range(2):
                        cols = slice(k * D + half * UC, k * D + (half + 1) * UC)
                        ins = mm3(ps[:, 6 + half, :], eh_hi[:, k, :], eh_lo[:, k, :], w_hi[:, 2, cols], w_lo[:, 2, cols],
                                  False, stop and k == 1)
                ins.then_inc(e_used[2], 1)

            def etranspose(e, f):
                pe.wait_ge(e_h, NF * e + f + 3)
                for k in range(2):
                    ins = pe.transpose(ps[:, 3, k * CAP:(k + 1) * CAP], hid[:, k * P:(k + 1) * P], ident[:, :])
                ins.then_inc(e_tr, 1)

            def gather(e):
                pe.wait_ge(e_pick, 2 * (e + 1))
                for k in range(KD):
                    for t in range(TT):
                        ins = pe.matmul(ps[:, 4 + k // 4, (k % 4) * CAP:(k % 4 + 1) * CAP], hn[:, t, k * P:(k + 1) * P],
                                        pick[:, t, :], start=k % 4 == 0 and t == 0, stop=t == TT - 1, skip_group_check=True)
                ins.then_inc(e_gath, 1)

            def scatter(e, t):
                if t == 0:
                    pe.wait_ge(e_ylo, e + 1)
                else:
                    pe.wait_ge(e_add, TT * e + 2)
                for half in range(2):
                    cols = slice(half * UC, (half + 1) * UC)
                    pe.matmul(ps[:, 4 + half, :], pickT[:, t * P:(t + 1) * P], y_hi[:, cols], start=True, stop=False)
                    ins = pe.matmul(ps[:, 4 + half, :], pickT[:, t * P:(t + 1) * P], y_lo[:, cols], start=False, stop=True)
                ins.then_inc(e_sc, 1)

            def slots(e):
                for t in range(TT):
                    pe.transpose(ps[:, 4, t * P:(t + 1) * P], pick[:, t, :], ident[:, :])
                for t in range(TT):
                    ins = pe.matmul(ps[:, 5, 0:NE], pick[:, t, :], gates[:, t, :], start=t == 0, stop=t == TT - 1)
                ins.then_inc(e_pt, 1)

            def eup_step(e, f, bank):
                pe.wait_ge(e_h, NF * e + f)
                eup(e, f, bank)

            def expert(e, opening):
                if not (isinstance(e, int) and e == 0):
                    pe.wait_ge(e_ptc, e)
                    pe.wait_ge(e_gsel, e)
                gather(e)
                if not opening:
                    edown(e - 1, NF - 3)
                    etranspose(e - 1, NF - 2)
                pe.wait_ge(e_x, e + 1)
                pe.wait_ge(e_h, NF * e + 1)
                eup(e, 0, 0)
                if not opening:
                    edown(e - 1, NF - 2)
                    etranspose(e - 1, NF - 1)
                pe.wait_ge(e_h, NF * e + 2)
                eup(e, 1, 1)
                if not opening:
                    edown(e - 1, NF - 1, True)
                etranspose(e, 0)
                eup_step(e, 2, 2)
                if not opening:
                    pe.wait_ge(e_ylo, e)
                open_sums(6, 2)
                for f in (3, 4):
                    edown(e, f - 3)
                    etranspose(e, f - 2)
                    if not opening:
                        scatter(e - 1, f - 3)
                    eup_step(e, f, f % 3)
                if not opening:
                    pe.wait_ge(e_add, TT * e + 1)
                if isinstance(e, int) and e == 0:
                    pe.wait_ge(r_gates, 1)
                slots(e)
                with pe.Fori(0, (NF - 5) // 3) as j:
                    for i in range(3):
                        edown(e, 3 * j + 2 + i)
                        etranspose(e, 3 * j + 3 + i)
                        eup_step(e, 3 * j + 5 + i, (2 + i) % 3)

            def expert_pass(k):
                expert(NE * k, True)
                with pe.Fori(NE * k + 1, NE * (k + 1)) as e:
                    expert(e, False)
                e = NE * (k + 1) - 1
                edown(e, NF - 3)
                for f in (NF - 2, NF - 1):
                    etranspose(e, f)
                    edown(e, f, f == NF - 1)
                for t in range(TT):
                    scatter(e, t)

            pe.sem_inc(e_used[2], 1)
            pe.sem_inc(e_tr, 1)
            pe.wait_ge(r_rank, 1)
            expert_pass(0)
            fullest = pe.value_load(most[0:1, 0:1])
            with pe.If(fullest > CAP):
                pe.wait_ge(e_again, TT)
                pe.wait_ge(e_add, TT * NE + 1)
                expert_pass(1)


_INS = ["x", "g_mix", "w_in", "b_f", "conv_w", "w_a2", "b_a", "g_gla", "w_pa", "w_pb", "w_pc", "w_gate", "b_gate",
        "w_o", "g_ffn", "ffn_w1", "ffn_w3", "ffn_w2", "w_router", "moe_w1", "moe_w3", "moe_w2", "g_final"]


def kernel(**inputs):
    import numpy as _np
    import concourse.bacc as _bacc
    from concourse import mybir as _mybir
    from concourse.bass_utils import run_bass_kernel_spmd as _run

    nc = _bacc.Bacc("TRN2", target_bir_lowering=False, num_devices=1)
    arrays, args = {}, []
    for name in _INS:
        a = _np.ascontiguousarray(inputs[name])
        arrays[f"in_{name}"] = a
        args.append(nc.dram_tensor(f"in_{name}", a.shape, _mybir.dt.from_np(a.dtype), kind="ExternalInput").ap())
    shape = arrays["in_x"].shape
    args.append(nc.dram_tensor("out_y", shape, _mybir.dt.float32, kind="ExternalOutput").ap())
    hybrid_trunk(nc, *args)
    r = _run(nc, [arrays], core_ids=[0])
    return r.results[0]["out_y"]
```

```python
import numpy as np
import concourse.bass as bass
from concourse import mybir
from contextlib import ExitStack


def hybrid_trunk(nc, x, g_mix, w_in, b_f, conv_w, w_a2, b_a, g_gla, w_pa, w_pb, w_pc, w_gate,
                 b_gate, w_o, g_ffn, ffn_w1, ffn_w3, ffn_w2, w_router, moe_w1, moe_w3, moe_w2,
                 g_final, out):
    F32, F32R, BF16, I32 = mybir.dt.float32, mybir.dt.float32r, mybir.dt.bfloat16, mybir.dt.int32
    ALU, ACT, AX = mybir.AluOpType, mybir.ActivationFunctionType, mybir.AxisListType
    ds = bass.ds

    P = 128
    S, D = x.shape[1], x.shape[2]
    TT, KD = S // P, D // P
    L = w_in.shape[0]
    HA, DH = b_f.shape[1], 64
    WB = conv_w.shape[2]
    LR, WK = w_a2.shape[1], w_a2.shape[2]
    HC, DK, DV = 4, 64, 128
    CH = 64
    NPAIR = WK // P
    NE, DF = moe_w1.shape[1], moe_w1.shape[3]
    FC = 256
    NF = DF // FC
    KW = 4
    UC = 512
    UN = KW * UC
    EPS = 1e-6
    NEG = -1e30
    CAP = P

    sizes = (WB, WB, WB, HA, WB, WB, WB, WK, WK, WB, LR, WB)
    offs = [sum(sizes[:i]) for i in range(len(sizes))]
    (C_AQ, C_AK, C_AV, C_AF, C_BU, C_BB, C_BC, C_CQ, C_CK, C_CV, C_CA, C_CR) = offs
    SM = HA + LR
    DR = 32
    NW = 96

    def panels_of(l):
        rows = [("k", w_in[l], C_AK, True, KD, "act", "act"), ("q", w_in[l], C_AQ, True, KD, "act", "act"),
                ("v", w_in[l], C_AV, False, KD, "act", "act"), ("cqk", w_in[l], C_CQ, True, KD, "act", "act"),
                ("cv", w_in[l], C_CV, False, KD, "act", "act"), ("cr", w_in[l], C_CR, False, KD, "act", "act"),
                ("u", w_in[l], C_BU, True, KD, "act", "act"), ("cg", w_in[l], C_BC, True, KD, "act", "dve"),
                ("bg", w_in[l], C_BB, True, KD, "act", "dve")]
        for br, wp in ((1, w_pb[l]), (0, w_pa[l]), (2, w_pc[l])):
            for half in range(2):
                rows.append((f"gate{br}{half}", w_gate[l], br * D + half * UC, True, KD, "act", "act"))
                rows.append((f"proj{br}{half}", wp, half * UC, True, WB // P, "o%d" % br, "dve"))
        for half in range(2):
            rows.append((f"out{half}", w_o[l], half * UC, False, KD, "merged", "dve"))
        return rows

    NPAN = len(panels_of(0))
    NUNIT = sum(r[4] // KW for r in panels_of(0))
    NAMES = [r[0] for r in panels_of(0)]
    EVAC = [r[6] for r in panels_of(0)]

    def evacuated(g, engine):
        return sum(EVAC[i % NPAN] == engine for i in range(g + 1))

    def units_until(g):
        return sum(panels_of(0)[i % NPAN][4] // KW for i in range(g + 1))

    HS = 3

    MRING, SRING = 6, 3

    ctx = ExitStack()
    with ctx:
        def sb(name, shape, dt=F32, c=ctx):
            return c.enter_context(nc.sbuf_tensor(name, shape, dt))

        def sem(name):
            return ctx.enter_context(nc.semaphore(name))

        raw = sb("raw", [P, 9, UN])
        w_hi = sb("w_hi", [P, SRING, UN], F32R)
        w_lo = sb("w_lo", [P, SRING, UN], F32R)
        xres = sb("xres", [P, TT, D])
        hn = sb("hn", [P, TT, D])
        act_hi = sb("act_hi", [P, KD, S], F32R)
        act_lo = sb("act_lo", [P, KD, S], F32R)
        merged = sb("merged", [P, KD, S])
        gains = merged[:, 0:4, :].rearrange("p a b -> p (a b)")
        ident = sb("ident", [P, P])
        tri = sb("tri", [P, 3 * P], BF16)
        keep = sb("keep", [P, S])
        sumsq = sb("sumsq", [P, TT])
        rstd = sb("rstd", [P, TT])
        mhalf = sb("mhalf", [P, 8])
        zrow = sb("zrow", [1, UC], BF16)
        prm = sb("prm", [P, P])
        wsm = sb("wsm", [P, L, KD, SM])
        wa2_rows = sb("wa2", [DR + LR, WK])
        wa2 = wa2_rows[DR:DR + LR, :]
        bf = sb("bf", [HA, L])
        wr = sb("wr", [P, KD, NE])
        iota_i = keep[:, 0:P].bitcast(I32)

        NCONV, NBA, NGG, NBG = L * 3 * WB // P, L * WK // P, L * WB // P, L * 3 * D // P
        R_CONV, R_BA, R_GG, R_BG = 0, NCONV, NCONV + NBA, NCONV + NBA + NGG
        NPRM = R_BG + NBG
        prm_rows = merged[0:NPRM, 7, 0:P]

        mix = ExitStack()
        qT = sb("qT", [P, 4, S], c=mix)
        kT = sb("kT", [P, 4, S], c=mix)
        vA = sb("vA", [P, TT, WB], c=mix)
        oa_hi = sb("oa_hi", [P, 4, S], F32R, c=mix)
        oa_lo = sb("oa_lo", [P, 4, S], F32R, c=mix)
        obc_hi = sb("obc_hi", [P, 4, S], F32R, c=mix)
        obc_lo = sb("obc_lo", [P, 4, S], F32R, c=mix)
        probs = sb("probs", [P, 2, 3 * P], c=mix)
        f_query = sb("f_query", [100, 2, S], F32R, c=mix)
        f_key = sb("f_key", [100, 2, S], F32R, c=mix)
        f_sum = merged[0:HA, 4, :]
        f_parts = sb("f_parts", [HA, 4, S], F32R, c=mix)
        logf = merged[0:HA, 2, :]
        lsa = merged[0:HA, 3, :]
        lsb = merged[0:HA, 6, :]
        ones8 = merged[0:HA, 7, :]
        aT = merged[DR:DR + LR, 6, :]
        merged_hi = (oa_hi[:, :, :], act_hi[:, 0:4, :])
        merged_lo = (oa_lo[:, :, :], act_lo[:, 0:4, :])
        wsm_hi = obc_hi[:, :, :].rearrange("p a t -> p (a t)")[:, 0:KD * NW].rearrange("p (k n) -> p k n", n=NW)
        wsm_lo = obc_lo[:, :, :].rearrange("p a t -> p (a t)")[:, 0:KD * NW].rearrange("p (k n) -> p k n", n=NW)
        cum = merged[:, 0:NPAIR, :]
        decay = sb("decay", [P, NPAIR, S // CH], c=mix)
        mx = sb("mx", [P, 2 * HA], c=mix)
        nmx = sb("nmx", [P, 2 * HA], c=mix)
        sm = sb("sm", [P, 2 * HA], c=mix)
        rs = sb("rs", [P, 2 * HA], c=mix)
        cmask = sb("cmask", [P, 2 * P], c=mix)
        gmask = sb("gmask", [P, P], c=mix)
        oss = sb("oss", [P, 2 * HC], c=mix)
        ors = sb("ors", [P, 2 * HC], c=mix)
        spare = raw[:, 6:9, :].rearrange("p a n -> p (a n)")
        ZP = S + 2
        at = [0]

        def carve(n):
            at[0] += n
            return spare[:, at[0] - n:at[0]]
        cqkT = carve(4 * S).rearrange("p (a t) -> p a t", t=S)
        vC = carve(TT * WB).rearrange("p (a t) -> p a t", t=WB)
        rC = carve(TT * WB).rearrange("p (a t) -> p a t", t=WB)
        zB = carve(4 * ZP).rearrange("p (a t) -> p a t", t=ZP)
        cvB = carve(4 * S).rearrange("p (a t) -> p a t", t=S)
        kst = carve(NPAIR * S).rearrange("p (a t) -> p a t", t=S)
        probsT = carve(3 * P)
        assert at[0] <= 3 * UN
        attC = qT[:, :, :].rearrange("p a t -> p (a t)")
        states = kT[:, 0:3, :].rearrange("p a t -> p (a t)").rearrange("p (n m e) -> p n m e", n=3, m=NPAIR)
        oC = vA[:, :, :].rearrange("p a t -> p (a t)")
        kst_tok = cvB[:, 0:2, :].rearrange("p a t -> p (a t)")
        sqC = zB[:, :, 0:S]
        lg = [hn[:, 0, 0:512], hn[:, 0, 512:1024], hn[:, 1, 0:512], hn[:, 1, 512:1024]]
        gate_s = hn[:, 0, :].rearrange("p (a t) -> p a t", t=S)
        prod_s = hn[:, 1, :].rearrange("p (a t) -> p a t", t=S)
        mix.close()

        den = ExitStack()
        dsilu = sb("dsilu", [P, 2, S], c=den)
        dh_hi = sb("dh_hi", [P, 2, S], F32R, c=den)
        dh_lo = sb("dh_lo", [P, 2, S], F32R, c=den)
        dlate_hi = sb("dlate_hi", [P, 2, S], F32R, c=den)
        dlate_lo = sb("dlate_lo", [P, 2, S], F32R, c=den)
        den.close()
        moe = ExitStack()
        pick = sb("pick", [P, TT, CAP], c=moe)
        pickT = sb("pickT", [P, S], F32R, c=moe)
        xs_hi = sb("xs_hi", [P, KD, CAP], F32R, c=moe)
        xs_lo = sb("xs_lo", [P, KD, CAP], F32R, c=moe)
        late_h_hi, late_h_lo = xs_hi[:, 0:2, :], xs_lo[:, 0:2, :]
        esilu = sb("esilu", [P, FC], c=moe)
        hid = sb("hid", [P, FC], c=moe)
        eh_hi = sb("eh_hi", [P, 2, CAP], F32R, c=moe)
        eh_lo = sb("eh_lo", [P, 2, CAP], F32R, c=moe)
        lgT = sb("lgT", [NE, S], c=moe)
        y_hi = sb("y_hi", [P, D], F32R, c=moe)
        y_lo = sb("y_lo", [P, D], F32R, c=moe)
        gsel = sb("gsel", [P, 1], c=moe)
        iota = sb("iota", [P, CAP], c=moe)
        lgt = sb("lgt", [P, TT, NE], c=moe)
        lgt2 = sb("lgt2", [P, TT, NE], c=moe)
        eq = sb("eq", [P, TT, NE], c=moe)
        cnt = sb("cnt", [P, TT, NE], c=moe)
        first = sb("first", [P, TT, NE], c=moe)
        second = sb("second", [P, TT, NE], c=moe)
        one16 = sb("one16", [P, TT, NE], c=moe)
        v1 = sb("v1", [P, TT], c=moe)
        v2 = sb("v2", [P, TT], c=moe)
        wt1 = sb("wt1", [P, TT], c=moe)
        wt2 = sb("wt2", [P, TT], c=moe)
        chosen = sb("chosen", [P, TT, NE], BF16, c=moe)
        gates = sb("gates", [P, TT, NE], c=moe)
        rank = sb("rank", [P, TT, NE + 1], c=moe)
        most = sb("most", [P, 1], I32, c=moe)
        early_raw = sb("early_raw", [P, 2, UN], c=moe)
        moe.close()

        ps = ctx.enter_context(nc.psum_tensor("ps", [P, 8, 512], F32))

        def banks(a, n=1):
            return ps[:, a:a + n, :].rearrange("p b n -> p (b n)")
        BX, BY, BT, BO = 4, 5, 6, 7

        x_loaded = [sem(f"x_loaded{t}") for t in range(TT)]
        prm_loaded, bf_loaded = sem("prm_loaded"), sem("bf_loaded")
        wsm_loaded, wa2_loaded, wr_loaded = sem("wsm_loaded"), sem("wa2_loaded"), sem("wr_loaded")
        gain_loaded, out_stored = sem("gain_loaded"), sem("out_stored")
        consts, cstep = sem("consts"), sem("cstep")
        prm_tr, prm_ready = sem("prm_tr"), sem("prm_ready")
        x_ready, n_sq, n_ms, n_rstd = sem("x_ready"), sem("n_sq"), sem("n_ms"), sem("n_rstd")
        n_hn, n_tr, n_hi, n_act = sem("n_hn"), sem("n_tr"), sem("n_hi"), sem("n_act")
        m_raw = [sem(f"m_raw{i}") for i in range(MRING)]
        m_hi, m_lo, m_used = sem("m_hi"), sem("m_lo"), sem("m_used")
        evac_act, evac_dve = sem("evac_act"), sem("evac_dve")
        s_zero, s_split, s_done, s_biased = sem("s_zero"), sem("s_split"), sem("s_done"), sem("s_biased")
        s_aTc, s_ln, s_rows, s_fone = sem("s_aTc"), sem("s_ln"), sem("s_rows"), sem("s_fone")
        s_frow = [sem(f"s_frow{j}") for j in range(2)]
        gain0_loaded = sem("gain0_loaded")
        o_tile = sem("o_tile")
        g_lin, g_neg, g_ln, g_cum = sem("g_lin"), sem("g_neg"), sem("g_ln"), sem("g_cum")
        g_es, g_in = sem("g_es"), sem("g_in")
        a_score, a_max, a_exp, a_prob = sem("a_score"), sem("a_max"), sem("a_exp"), sem("a_prob")
        a_tr, a_pt, a_pv, a_ohi, a_out = sem("a_tr"), sem("a_pt"), sem("a_pv"), sem("a_ohi"), sem("a_out")
        b_y, b_hi, b_out = sem("b_y"), sem("b_hi"), sem("b_out")
        g_att, g_attm, g_kstT, g_kst, g_kv = sem("g_att"), sem("g_attm"), sem("g_kstT"), sem("g_kst"), sem("g_kv")
        g_state, g_o, g_ocopy, g_ms, g_rstd = sem("g_state"), sem("g_o"), sem("g_ocopy"), sem("g_ms"), sem("g_rstd")
        g_on, g_oT, g_ohi, g_out = sem("g_on"), sem("g_oT"), sem("g_ohi"), sem("g_out")
        mg_sum, mg_hi, mg_out = sem("mg_sum"), sem("mg_hi"), sem("mg_out")
        dchain, achain = sem("dchain"), sem("achain")
        d_raw = [sem(f"d_raw{i}") for i in range(6)]
        d_hi = [sem(f"d_hi{t}") for t in range(3)]
        d_lo = [sem(f"d_lo{t}") for t in range(3)]
        d_used = [sem(f"d_used{t}") for t in range(3)]
        d_silu, d_h, d_hhi, d_hT = sem("d_silu"), sem("d_h"), sem("d_hhi"), sem("d_hT")
        d_tile = sem("d_tile")
        e_raw = [sem(f"e_raw{i}") for i in range(9)]
        e_hi = [sem(f"e_hi{t}") for t in range(3)]
        e_lo = [sem(f"e_lo{t}") for t in range(3)]
        e_used = [sem(f"e_used{t}") for t in range(3)]
        e_silu, e_h, e_tr, e_hhi, e_hT = sem("e_silu"), sem("e_h"), sem("e_tr"), sem("e_hhi"), sem("e_hT")
        e_pick, e_again, e_gath, e_xhi, e_x = sem("e_pick"), sem("e_again"), sem("e_gath"), sem("e_xhi"), sem("e_x")
        e_pt, e_ptc, e_gsel, e_yhi, e_ylo = sem("e_pt"), sem("e_ptc"), sem("e_gsel"), sem("e_yhi"), sem("e_ylo")
        e_sc, e_add = sem("e_sc"), sem("e_add")
        l_yhi, l_ylo = sem("l_yhi"), sem("l_ylo")
        r_zero, r_split, r_logit, r_lgT, r_iota = sem("r_zero"), sem("r_split"), sem("r_logit"), sem("r_lgT"), sem("r_iota")
        r_gates = sem("r_gates")
        r_v, r_e, r_chosen, r_cum, r_rank = sem("r_v"), sem("r_e"), sem("r_chosen"), sem("r_cum"), sem("r_rank")
        f_scaled = sem("f_scaled")

        block = ctx.enter_context(nc.Block())

        def last_use(n_units, ring, slot):
            return max(n for n in range(n_units) if n % ring == slot) + 1

        def per_set(s):
            return len(range(s, NF, 3))

        def before_units(l):
            return l * NUNIT

        EARLY = 4

        def arriving(e, f, t, fs):
            first_early = isinstance(e, int) and e == 0 and isinstance(f, int) and f == EARLY
            return early_raw[:, t, :] if first_early else raw[:, 3 * t + fs, :]

        def split_slot(e, f, t):
            return 2 if isinstance(e, int) and e == 0 and isinstance(f, int) and f == 1 and t == 0 else t

        def late_bank(t):
            return 4 if t == 0 else 0

        w1e = moe_w1[0].rearrange("e (k p) n -> e p k n", p=P)
        w3e = moe_w3[0].rearrange("e (k p) n -> e p k n", p=P)
        w2e = moe_w2[0].rearrange("e (k p) n -> e p k n", p=P)

        @block.sync
        def _(sp):
            for t in range(TT):
                sp.dma_start(xres[:, t, :], x[0, t * P:(t + 1) * P, :]).then_inc(x_loaded[t], 16)
                if t == 0:
                    sp.dma_start(gains, g_mix[0:1, :].to_broadcast([P, D])).then_inc(gain0_loaded, 16)

            def mixer_stream(l):
                n = before_units(l)
                for name, w, c0, ws, kt, _, _ in panels_of(l):
                    wv = w.rearrange("(k p) n -> p k n", p=P)
                    for j in range(kt // KW):
                        slot = n % MRING
                        if n >= before_units(l) + MRING:
                            sp.wait_ge(m_lo, n - MRING + 1)
                        elif l > 0:
                            sp.wait_ge(d_lo[slot % 3], NF)
                        sp.dma_start(raw[:, slot, :].rearrange("p (k n) -> p k n", k=KW),
                                     wv[:, j * KW:(j + 1) * KW, c0:c0 + UC]).then_inc(m_raw[slot], 16)
                        n += 1
                        if n == 3:
                            small_inputs()

            def small_inputs():
                for l in range(L):
                    wl_ = w_in[l].rearrange("(k p) n -> p k n", p=P)
                    sp.dma_start(wsm[:, l, :, 0:HA], wl_[:, :, C_AF:C_AF + HA]).then_inc(wsm_loaded, 16)
                    sp.dma_start(wsm[:, l, :, HA:SM], wl_[:, :, C_CA:C_CA + LR]).then_inc(wsm_loaded, 16)
                for l in range(L):
                    sp.dma_start(bf[:, l:l + 1], b_f[l].rearrange("(h a) -> h a", a=1)).then_inc(bf_loaded, 16)
                sp.dma_start(wr[:, :, :], w_router[0].rearrange("(k p) n -> p k n", p=P)).then_inc(wr_loaded, 16)

            mixer_stream(0)

            w1d = ffn_w1[0].rearrange("(k p) n -> p k n", p=P)
            w3d = ffn_w3[0].rearrange("(k p) n -> p k n", p=P)
            w2d = ffn_w2[0].rearrange("(k p) n -> p k n", p=P)

            def dense_step(s, parity, has_gu, has_w2, peeled):
                for t in range(2 if has_gu else 0):
                    slot = parity * 3 + t
                    if peeled:
                        sp.wait_ge(m_lo, last_use(NUNIT, MRING, slot))
                    else:
                        sp.wait_ge(d_lo[t], s - 1)
                    dst = raw[:, slot, :].rearrange("p (k w n) -> p k w n", k=KW, w=2)
                    sp.dma_start(dst[:, :, 0, :], w1d[:, t * KW:(t + 1) * KW, ds(s * FC, FC)]).then_inc(d_raw[slot], 16)
                    sp.dma_start(dst[:, :, 1, :], w3d[:, t * KW:(t + 1) * KW, ds(s * FC, FC)]).then_inc(d_raw[slot], 16)
                if has_w2:
                    slot = parity * 3 + 2
                    if peeled:
                        sp.wait_ge(m_lo, last_use(NUNIT, MRING, slot))
                    else:
                        sp.wait_ge(d_lo[2], s - 2)
                    sp.dma_start(raw[:, slot, :].rearrange("p (k n) -> p k n", k=2),
                                 w2d[:, ds((s - 1) * 2, 2), :]).then_inc(d_raw[slot], 16)

            dense_step(0, 0, True, False, True)
            dense_step(1, 1, True, True, True)
            for t in range(2):
                sp.wait_ge(d_lo[t], 1)
                dst = raw[:, t, :].rearrange("p (k w n) -> p k w n", k=KW, w=2)
                sp.dma_start(dst[:, :, 0, :], w1d[:, t * KW:(t + 1) * KW, 2 * FC:3 * FC]).then_inc(d_raw[t], 16)
                sp.dma_start(dst[:, :, 1, :], w3d[:, t * KW:(t + 1) * KW, 2 * FC:3 * FC]).then_inc(d_raw[t], 16)
            sp.wait_ge(m_lo, last_use(NUNIT, MRING, 2))
            sp.dma_start(raw[:, 2, :].rearrange("p (k n) -> p k n", k=2), w2d[:, 2:4, :]).then_inc(d_raw[2], 16)
            with sp.Fori(0, (NF - 3) // 2) as j:
                dense_step(2 * j + 3, 1, True, True, False)
                dense_step(2 * j + 4, 0, True, True, False)
            dense_step(NF, 1, False, True, False)

            mixer_stream(1)

            def expert_gu(e, ew, f, fs, fresh):
                for t in range(2):
                    slot = 3 * t + fs
                    if not fresh:
                        prev = NF * e + f - 3 + 1 if not isinstance(f, int) or f >= 3 else \
                            NF * (e - 1) + 3 * (per_set(fs) - 1) + fs + 1
                        sp.wait_ge(e_lo[t], prev)
                    dst = arriving(e, f, t, fs).rearrange("p (k w n) -> p k w n", k=KW, w=2)
                    for w, src in ((0, w1e), (1, w3e)):
                        sp.dma_start(dst[:, :, w, :],
                                     src[ds(ew, 1), :, t * KW:(t + 1) * KW, ds(f * FC, FC)].rearrange(
                                         "a p k n -> p (a k) n")).then_inc(e_raw[slot], 16)

            def expert_w2(e, ew, f, fs, fresh):
                slot = 6 + fs
                if not fresh:
                    prev = NF * e + f - 3 + 1 if not isinstance(f, int) or f >= 3 else \
                        NF * (e - 1) + 3 * (per_set(fs) - 1) + fs + 1
                    sp.wait_ge(e_lo[2], prev)
                sp.dma_start(raw[:, slot, :].rearrange("p (k n) -> p k n", k=2),
                             w2e[ds(ew, 1), :, ds(f * 2, 2), :].rearrange("a p k n -> p (a k) n")).then_inc(e_raw[slot], 16)

            def expert_stream(e, ew, opening):
                fresh = isinstance(e, int) and e == 0
                for f in range(5):
                    expert_gu(e, ew, f, f % 3, fresh and f < 3)
                    if fresh and f == 2:
                        sp.wait_ge(x_ready, 3 * TT)
                        for g in range(3):
                            expert_w2(e, ew, g, g, True)
                    elif f >= 2 and not fresh:
                        expert_w2(e, ew, f - 2, f - 2, False)
                    elif not opening:
                        expert_w2(e - 1, ew - 1, NF - 2 + f, (NF - 2 + f) % 3, False)
                with sp.Fori(0, (NF - 5) // 3) as j:
                    for i in range(3):
                        expert_gu(e, ew, 3 * j + 5 + i, (i + 2) % 3, False)
                        expert_w2(e, ew, 3 * j + 3 + i, i, False)

            def experts_stream(k):
                expert_stream(NE * k, 0, True)
                with sp.Fori(NE * k + 1, NE * (k + 1)) as e:
                    expert_stream(e, e - NE * k, False)
                for f in (NF - 2, NF - 1):
                    expert_w2(NE * (k + 1) - 1, NE - 1, f, f % 3, False)

            sp.wait_ge(m_lo, L * NUNIT)
            experts_stream(0)
            sp.wait_ge(r_rank, 1)
            fullest = sp.value_load(most[0:1, 0:1])
            with sp.If(fullest > CAP):
                experts_stream(1)

            for t in range(TT):
                sp.wait_ge(f_scaled, t + 1)
                sp.dma_start(out[0, t * P:(t + 1) * P, :], hn[:, t, :]).then_inc(out_stored, 16)
            sp.wait_ge(out_stored, 16 * TT)

        @block.gpsimd
        def _(pool):
            def inverse_root(n):
                gain = (g_mix if n % 2 == 0 else g_ffn)[n // 2:n // 2 + 1, :] if n < 2 * L else \
                    g_final.rearrange("(a n) -> a n", a=1)
                if n % 2 == 1:
                    pool.wait_ge(mg_out, n + 1)
                elif n > 0:
                    pool.wait_ge(n_hn, TT * n)
                if n > 0:
                    pool.dma_start(gains, gain.to_broadcast([P, D])).then_inc(gain_loaded, 16)
                if n == 2 * L - 1:
                    pool.iota(iota_i, pattern=[[1, CAP]], base=0, channel_multiplier=0).then_inc(r_iota, 1)
                    pool.memset(xs_hi[:, :, :].bitcast(F32), 0.0).then_inc(r_zero, 1)
                    pool.memset(xs_lo[:, :, :].bitcast(F32), 0.0).then_inc(r_zero, 1)
                for t in range(TT):
                    pool.wait_ge(n_ms, TT * n + t + 1)
                    pool.tensor_tensor(rstd[:, t:t + 1], sumsq[:, t:t + 1], mhalf[:, 0:1], ALU.pow).then_inc(n_rstd, 1)

            step = [0]

            def link(ins):
                step[0] += 1
                ins.then_inc(cstep, 1)
                pool.wait_ge(cstep, step[0])
            link(pool.memset(ident[:, :], 0.0))
            link(pool.affine_select(out=ident[:, :], in_=ident[:, :], compare_op=ALU.not_equal, fill=1.0,
                                    base=0, pattern=[[-1, P]], channel_multiplier=1))
            pool.memset(mhalf[:, :], -0.5).then_inc(consts, 1)
            pool.wait_ge(consts, 1)
            inverse_root(0)
            pool.memset(wsm_hi.bitcast(F32), 0.0).then_inc(s_zero, 1)
            pool.memset(wsm_lo.bitcast(F32), 0.0).then_inc(s_zero, 1)
            for src, r0 in ((conv_w.rearrange("l t (c p) -> (l t c) p", p=P), R_CONV),
                            (b_a.rearrange("l (c p) -> (l c) p", p=P), R_BA),
                            (g_gla.rearrange("l (c p) -> (l c) p", p=P), R_GG),
                            (b_gate.rearrange("l (c p) -> (l c) p", p=P), R_BG)):
                pool.dma_start(prm_rows[r0:r0 + src.shape[0], :], src).then_inc(prm_loaded, 16)
            link(pool.memset(tri[:, :], 1.0))
            link(pool.memset(tri[:, 0:P], 0.0))
            link(pool.affine_select(out=tri[:, P:2 * P], in_=tri[:, P:2 * P], compare_op=ALU.is_ge, fill=0.0,
                                    base=0, pattern=[[1, P]], channel_multiplier=-1))
            link(pool.memset(cmask[:, :], 0.0))
            link(pool.affine_select(out=cmask[:, P:2 * P], in_=cmask[:, P:2 * P], compare_op=ALU.is_ge, fill=NEG,
                                    base=0, pattern=[[-1, P]], channel_multiplier=1))
            link(pool.memset(gmask[:, :], 1.0))
            link(pool.affine_select(out=gmask[:, :], in_=gmask[:, :], compare_op=ALU.is_ge, fill=0.0,
                                    base=0, pattern=[[1, P]], channel_multiplier=-1))
            link(pool.affine_select(out=gmask[:, CH:P], in_=gmask[:, CH:P], compare_op=ALU.is_ge, fill=0.0,
                                    base=-CH, pattern=[[0, P - CH]], channel_multiplier=1))
            link(pool.memset(keep[:, :], 1.0))
            for c in range(S // CH):
                link(pool.memset(keep[:, c * CH:c * CH + 1], 0.0))
            pool.memset(zrow[:, :], 0.0).then_inc(consts, 1)
            pool.memset(f_query[:, :, :].bitcast(F32), 1.0).then_inc(s_fone, 1)
            pool.memset(f_key[:, :, :].bitcast(F32), 1.0).then_inc(s_fone, 1)
            pool.wait_ge(s_fone, 2)

            for l in range(L):
                if l > 0:
                    inverse_root(2 * l)
                    pool.wait_ge(g_lin, l)
                pool.dma_start(wa2[:, :], w_a2[l]).then_inc(wa2_loaded, 16)
                pool.wait_ge(s_rows, 3 * (l + 1))
                for j in range(2):
                    for i in range(2):
                        pool.dma_start(f_query[i:97 + i:32, j, :], f_parts[4 * j:4 * j + 4, i, :]).then_inc(s_frow[j], 16)
                        pool.dma_start(f_key[2 + i:99 + i:32, j, :], f_parts[4 * j:4 * j + 4, 2 + i, :]).then_inc(s_frow[j], 16)
                pool.wait_ge(g_ms, l + 1)
                pool.tensor_tensor(ors[:, :], oss[:, :], mhalf[:, 0:2 * HC], ALU.pow).then_inc(g_rstd, 1)
                inverse_root(2 * l + 1)
            inverse_root(2 * L)

        @block.scalar
        def _(act):
            chain = [0]

            def link(ins):
                chain[0] += 1
                ins.then_inc(achain, 1)
                act.wait_ge(achain, chain[0])

            def square_sums(n):
                for t in range(TT):
                    if n == 0:
                        act.wait_ge(x_loaded[t], 16)
                    else:
                        act.wait_ge(x_ready, TT * (n - 1) + t + 1)
                    act.activation(hn[:, t, :], xres[:, t, :], ACT.Square, accum_out=sumsq[:, t:t + 1]).then_inc(n_sq, 1)

            def act_hi_of(n):
                for b in range(4):
                    act.wait_ge(n_tr, 4 * n + b + 1)
                    act.copy(act_hi[:, 2 * b:2 * b + 2, :].rearrange("p a t -> p (a t)"), banks(4 + b)).then_inc(n_hi, 1)

            def split_unit(l, u):
                act.wait_ge(m_raw[u % MRING], 16 * (u // MRING + 1))
                if u >= before_units(l) + SRING:
                    act.wait_ge(m_used, u - SRING + 1)
                elif l > 0:
                    act.wait_ge(d_used[(2, 1, 2)[u % SRING]], (NF, NF, NF - 1)[u % SRING])
                act.copy(w_hi[:, u % SRING, :], raw[:, u % MRING, :]).then_inc(m_hi, 1)

            def mixer(l):
                G0 = l * NPAN

                split = [before_units(l) + 2]

                def split_to(count):
                    for u in range(split[0], min(count, before_units(l + 1))):
                        split_unit(l, u)
                    split[0] = count

                def done(p):
                    act.wait_ge(m_used, units_until(G0 + p))

                split_to(units_until(G0 + 1))
                if l == 0:
                    act.wait_ge(prm_tr, 1)
                    act.copy(prm[:, 0:NPRM], ps[:, BT, 0:NPRM]).then_inc(prm_ready, 1)
                act.wait_ge(s_done, l + 1)
                act.copy(aT, ps[DR:DR + LR, BO, 0:S]).then_inc(s_aTc, 1)
                act.wait_ge(s_biased, l + 1)
                link(act.activation(lsb, lsb, ACT.Exp))
                act.activation(lsb, lsb, ACT.Ln, bias=1.0).then_inc(s_ln, 1)
                done(0)
                act.copy(kT[:, :, :].rearrange("p a t -> p (a t)"), banks(0 if G0 % 2 == 0 else 2, 2)).then_inc(evac_act, 1)
                split_to(units_until(G0 + 2) + 1)
                act.wait_ge(g_neg, l + 1)
                link(act.activation(lg[2], lg[2], ACT.Exp))
                act.activation(lg[2], lg[2], ACT.Ln, bias=1.0).then_inc(g_ln, 1)
                act.wait_ge(g_cum, 2 * (l + 1))
                cumf = cum[:, :, :].rearrange("p a t -> p (a t)")
                act.activation(lg[0], cumf, ACT.Exp, scale=1.0 / 16).then_inc(g_es, 1)
                act.activation(lg[1], cumf, ACT.Exp, scale=-1.0 / 16).then_inc(g_es, 1)
                act.activation(lg[3], lg[3], ACT.Exp, scale=1.0 / 16).then_inc(g_es, 1)
                act.activation(decay[:, :, :], cum[:, :, CH - 1::CH], ACT.Exp, scale=1.0 / 16).then_inc(g_es, 1)
                done(1)
                act.mul(qT[:, :, :].rearrange("p a t -> p (a t)"), banks(2 if G0 % 2 == 0 else 0, 2), DH ** -0.5).then_inc(evac_act, 1)

                def evacuate(p):
                    name = NAMES[p]
                    bank = ((G0 + p) % 2) * 2
                    if EVAC[p] != "act":
                        return
                    done(p)
                    src = banks(bank, 2)
                    if name == "v":
                        act.copy(vA[:, :, :].rearrange("p a t -> p (a t)"), src).then_inc(evac_act, 1)
                    elif name == "cqk":
                        act.copy(cqkT.rearrange("p a t -> p (a t)"), src).then_inc(evac_act, 1)
                    elif name == "cv":
                        act.copy(vC.rearrange("p a t -> p (a t)"), src).then_inc(evac_act, 1)
                    elif name == "cr":
                        act.activation(rC.rearrange("p a t -> p (a t)"), src, ACT.Silu).then_inc(evac_act, 1)
                    elif name == "u":
                        act.copy(zB[:, :, 2:ZP], src.rearrange("p (a t) -> p a t", t=S)).then_inc(evac_act, 1)
                    else:
                        br, half = int(name[4]), int(name[5])
                        if NAMES[p] == "gate10":
                            act.wait_ge(g_in, l + 1)
                        else:
                            act.wait_ge(evac_dve, evacuated(G0 + p - 1, "dve"))
                        for c in range(4):
                            col = R_BG + l * 3 * KD + br * KD + half * 4 + c
                            ins = act.activation(gate_s[:, c, :], src[:, c * S:(c + 1) * S], ACT.Sigmoid,
                                                 bias=prm[:, col:col + 1])
                        ins.then_inc(evac_act, 1)

                def exps(h):
                    a = l * HA + h
                    act.wait_ge(a_max, a + 1)
                    act.activation(probs[:, h % 2, 0:P], probs[:, h % 2, 0:P], ACT.Exp, bias=nmx[:, 2 * h:2 * h + 1],
                                   accum_out=sm[:, 2 * h:2 * h + 1])
                    act.activation(probs[:, h % 2, P:3 * P], probs[:, h % 2, P:3 * P], ACT.Exp,
                                   bias=nmx[:, 2 * h + 1:2 * h + 2], accum_out=sm[:, 2 * h + 1:2 * h + 2]).then_inc(a_exp, 1)

                def probs_T(h):
                    a = l * HA + h
                    act.wait_ge(a_tr, a + 1)
                    if h > 0:
                        act.wait_ge(a_pv, a)
                    act.copy(probsT, ps[:, BT, 0:3 * P]).then_inc(a_pt, 1)

                def head_out(h):
                    if h % 2 == 1:
                        act.wait_ge(a_pv, l * HA + h + 1)
                        act.copy(oa_hi[:, h // 2, :], ps[:, BO, 0:S]).then_inc(a_ohi, 1)

                for p in range(2, NPAN):
                    split_to(units_until(G0 + p) + 2)
                    if 0 <= p - HS < HA:
                        exps(p - HS)
                    if 0 <= p - HS - 1 < HA:
                        probs_T(p - HS - 1)
                    if 0 <= p - HS - 2 < HA:
                        head_out(p - HS - 2)
                    if NAMES[p] == "proj11":
                        act.wait_ge(g_kstT, l + 1)
                        act.copy(kst_tok, banks(BT)).then_inc(g_kst, 1)
                    if NAMES[p] == "proj00":
                        act.wait_ge(g_o, l + 1)
                        act.copy(oC, banks(BX, 2)).then_inc(g_ocopy, 1)
                    if NAMES[p] == "gate20":
                        act.wait_ge(g_oT, l + 1)
                        for h in range(HC):
                            col = R_GG + l * HC + h
                            act.activation(obc_hi[:, h, :], banks(BT, 2)[:, h * S:(h + 1) * S], ACT.Copy,
                                           scale=prm[:, col:col + 1]).then_inc(g_ohi, 1)
                    evacuate(p)
                    if NAMES[p] == "bg":
                        act.wait_ge(b_y, l + 1)
                        act.copy(obc_hi[:, :, :], cvB).then_inc(b_hi, 1)
                    if NAMES[p] in ("proj20", "proj21"):
                        half = int(NAMES[p][5])
                        act.wait_ge(mg_sum, 2 * l + half + 1)
                        act.copy(merged_hi[half], merged[:, 4 * half:4 * half + 4, :]).then_inc(mg_hi, 1)

            square_sums(0)
            split_unit(0, 0)
            act_hi_of(0)
            split_unit(0, 1)
            mixer(0)

            def dhi(t, slot, arrivals, used, first=False):
                act.wait_ge(d_raw[slot], arrivals)
                if first:
                    act.wait_ge(m_used, last_use(NUNIT, SRING, t))
                else:
                    act.wait_ge(d_used[t], used)
                act.copy(w_hi[:, t, :], raw[:, slot, :]).then_inc(d_hi[t], 1)

            def dense_hidden(s, parity, first):
                act.wait_ge(d_used[1], s + 1)
                if not first:
                    act.wait_ge(d_hT, s)
                act.activation(dsilu[:, :, :].rearrange("p a t -> p (a t)"), banks(2 * parity), ACT.Silu).then_inc(d_silu, 1)

            def dense_hidden_hi(s, first):
                act.wait_ge(d_h, s + 1)
                if not first:
                    act.wait_ge(d_used[2], s)
                act.copy(dh_hi[:, :, :], dsilu[:, :, :]).then_inc(d_hhi, 1)

            def dense_step(q, parity, up, down):
                s = 2 * q + parity
                if up and not (isinstance(s, int) and s == 0):
                    for t in range(2):
                        dhi(t, 3 * parity + t, 32 * (q + 1), s)
                if down:
                    dense_hidden(s - 1, 1 - parity, isinstance(s, int) and s == 1)
                    dhi(2, 3 * parity + 2, 16 * (q + parity), s - 1, isinstance(s, int) and s == 1)
                    dense_hidden_hi(s - 1, isinstance(s, int) and s == 1)

            dhi(1, 1, 32, None, True)
            square_sums(1)
            dhi(0, 0, 32, None, True)
            act_hi_of(1)
            dense_step(0, 1, True, True)
            with act.Fori(1, NF // 2) as q:
                dense_step(q, 0, True, True)
                dense_step(q, 1, True, True)
            dense_step(NF // 2, 0, True, True)
            act.wait_ge(d_raw[5], 16 * ((NF + 1) // 2))
            act.wait_ge(d_used[0], NF)
            act.copy(w_hi[:, 0, :], raw[:, 5, :]).then_inc(d_hi[2], 1)
            dense_hidden(NF - 1, 0, False)
            act.wait_ge(d_h, NF)
            act.copy(dlate_hi[:, :, :], dsilu[:, :, :]).then_inc(d_hhi, 1)

            u = before_units(1)
            split_unit(1, u)
            square_sums(2)
            split_unit(1, u + 1)
            act_hi_of(2)
            mixer(1)

            def ehi(src, t, slot, sem_raw, arrivals, used):
                act.wait_ge(sem_raw, arrivals)
                if used is None:
                    act.wait_ge(m_used, last_use(L * NUNIT, SRING, slot))
                else:
                    act.wait_ge(e_used[t], used)
                act.copy(w_hi[:, slot, :], src).then_inc(e_hi[t], 1)

            def half_gu(t, e, f, q, fs, first=False):
                ehi(arriving(e, f, t, fs), t, split_slot(e, f, t), e_raw[3 * t + fs], 32 * (per_set(fs) * e + q + 1),
                    None if first else NF * e + f)

            def step_gu(e, f, q, fs):
                for t in range(2):
                    half_gu(t, e, f, q, fs)

            def step_w2(e, f, q, fs):
                ehi(raw[:, 6 + fs, :], 2, 2, e_raw[6 + fs], 16 * (per_set(fs) * e + q + 1), NF * e + f + 1)

            def late_w2(e, f, slot):
                act.wait_ge(e_raw[6 + f % 3], 16 * (per_set(f % 3) * e + f // 3 + 1))
                act.wait_ge(e_used[slot], NF * (e + 1))
                act.copy(w_hi[:, slot, :], raw[:, 6 + f % 3, :]).then_inc(e_hi[2], 1)

            def silu_of(e, f, bank):
                act.wait_ge(e_used[1], NF * e + f + 1)
                act.wait_ge(e_h, NF * e + f + 2)
                act.activation(esilu[:, :], ps[:, bank, 0:FC], ACT.Silu).then_inc(e_silu, 1)

            def hidden_hi(e, f, to=eh_hi[:, :, :]):
                act.wait_ge(e_tr, NF * e + f + 2)
                act.copy(to.rearrange("p a t -> p (a t)"), ps[:, 3, 0:2 * CAP]).then_inc(e_hhi, 1)

            def tokens_hi(e):
                for b in range(2):
                    act.wait_ge(e_gath, 2 * e + b + 1)
                    act.copy(xs_hi[:, 4 * b:4 * b + 4, :].rearrange("p a t -> p (a t)"), banks(4 + b)).then_inc(e_xhi, 1)

            def output_hi(e):
                act.wait_ge(e_used[2], NF * (e + 1) + 1)
                act.wait_ge(e_gsel, e + 1)
                act.activation(y_hi[:, :], banks(6, 2), ACT.Copy, scale=gsel[:, 0:1]).then_inc(e_yhi, 1)

            def expert(e, opening):
                fresh = isinstance(e, int) and e == 0
                if not fresh:
                    step_gu(e, 0, 0, 0)
                if not opening:
                    silu_of(e - 1, NF - 1, (NF - 1) % 3)
                tokens_hi(e)
                if not opening:
                    step_w2(e - 1, NF - 2, 3, 0)
                    hidden_hi(e - 1, NF - 2)
                for f in range(1, 5):
                    if fresh and f == 1:
                        half_gu(1, e, f, 0, 1)
                    else:
                        step_gu(e, f, f // 3, f % 3)
                    silu_of(e, f - 1, (f - 1) % 3)
                    if f == 1:
                        if not opening:
                            step_w2(e - 1, NF - 1, 3, 1)
                            hidden_hi(e - 1, NF - 1)
                        continue
                    if f == 2 and not opening:
                        output_hi(e - 1)
                    if f == 4:
                        act.wait_ge(e_pt, e + 1)
                        act.copy(pickT[:, :], ps[:, 4, 0:S]).then_inc(e_ptc, 1)
                    step_w2(e, f - 2, 0, f - 2)
                    hidden_hi(e, f - 2)
                with act.Fori(0, (NF - 5) // 3) as j:
                    for i in range(3):
                        step_gu(e, 3 * j + 5 + i, j + (5 + i) // 3, (2 + i) % 3)
                        silu_of(e, 3 * j + 4 + i, (1 + i) % 3)
                        step_w2(e, 3 * j + 3 + i, j + 1, i)
                        hidden_hi(e, 3 * j + 3 + i)

            def expert_pass(k):
                expert(NE * k, True)
                with act.Fori(NE * k + 1, NE * (k + 1)) as e:
                    expert(e, False)
                e = NE * (k + 1) - 1
                late_w2(e, NF - 2, 0)
                silu_of(e, NF - 1, (NF - 1) % 3)
                late_w2(e, NF - 1, 1)
                hidden_hi(e, NF - 2)
                hidden_hi(e, NF - 1, late_h_hi)
                act.wait_ge(e_used[2], NF * (e + 1) + 1)
                act.wait_ge(e_gsel, e + 1)
                for half in range(2):
                    act.activation(y_hi[:, half * UC:(half + 1) * UC], ps[:, 6 + half, :], ACT.Copy,
                                   scale=gsel[:, 0:1]).then_inc(l_yhi if half == 0 else e_yhi, 1)

            half_gu(0, 0, 0, 0, 0, True)
            square_sums(3)
            half_gu(1, 0, 0, 0, 0, True)
            act_hi_of(3)
            half_gu(0, 0, 1, 0, 1, True)
            act.wait_ge(r_v, 1)
            act.activation(wt2[:, :], wt2[:, :], ACT.Exp).then_inc(r_e, 1)
            act.activation(esilu[:, 0:TT], ident[:, 0:TT], ACT.Silu)

            expert_pass(0)
            act.wait_ge(r_rank, 1)
            fullest = act.value_load(most[0:1, 0:1])
            with act.If(fullest > CAP):
                expert_pass(1)
            square_sums(4)

        @block.vector
        def _(dve):
            chain = [0]

            def link(ins):
                chain[0] += 1
                ins.then_inc(dchain, 1)
                dve.wait_ge(dchain, chain[0])

            def f32(ap):
                return ap.bitcast(F32)

            def normalise_stream(n, scaled):
                for t in range(TT):
                    dve.wait_ge(n_sq, TT * n + t + 1)
                    dve.tensor_scalar(sumsq[:, t:t + 1], sumsq[:, t:t + 1], 1.0 / D, EPS, ALU.mult, ALU.add).then_inc(n_ms, 1)
                for t in range(TT):
                    dve.wait_ge(n_rstd, TT * n + t + 1)
                    if t == 0:
                        dve.wait_ge(gain_loaded if n > 0 else gain0_loaded, 16 * max(n, 1))
                    dve.scalar_tensor_tensor(out=hn[:, t, :], in0=xres[:, t, :], scalar=rstd[:, t:t + 1], in1=gains,
                                             op0=ALU.mult, op1=ALU.mult).then_inc(scaled, 1)

            def act_lo_of(n):
                for b in range(4):
                    dve.wait_ge(n_hi, 4 * n + b + 1)
                    o = act_lo[:, 2 * b:2 * b + 2, :].rearrange("p a t -> p (a t)")
                    h = f32(act_hi[:, 2 * b:2 * b + 2, :]).rearrange("p a t -> p (a t)")
                    dve.tensor_tensor(o, banks(4 + b), h, ALU.subtract).then_inc(n_act, 1)

            def log_sigmoid_prep(lin, mn, neg):
                link(dve.tensor_scalar(mn, lin, 0.0, None, ALU.min))
                return dve.scalar_tensor_tensor(out=neg, in0=mn, scalar=2.0, in1=lin, op0=ALU.mult, op1=ALU.subtract)

            def split_unit(u):
                dve.wait_ge(m_hi, u + 1)
                dve.tensor_tensor(w_lo[:, u % SRING, :], raw[:, u % MRING, :], f32(w_hi[:, u % SRING, :]),
                                  ALU.subtract).then_inc(m_lo, 1)

            def mixer(l, ahead):
                G0 = l * NPAN

                split = [before_units(l) + 2]

                def split_to(count):
                    for u in range(split[0], min(count, before_units(l + 1))):
                        split_unit(u)
                    split[0] = count

                dve.wait_ge(wsm_loaded, 32 * L)
                dve.wait_ge(s_zero, 2)
                cols = ((wsm[:, l, :, 0:HA], slice(0, HA)), (wsm[:, l, :, HA:SM], slice(DR, DR + LR)))
                for w, c in cols:
                    ins = dve.tensor_copy(wsm_hi[:, :, c], w)
                link(ins)
                for w, c in cols:
                    ins = dve.tensor_tensor(wsm_lo[:, :, c], w, f32(wsm_hi[:, :, c]), ALU.subtract)
                ins.then_inc(s_split, 1)
                split_to(units_until(G0 + 1))
                dve.wait_ge(prm_ready, 1)
                dve.memset(ones8, 1.0).then_inc(dchain, 1)
                chain[0] += 1
                dve.wait_ge(bf_loaded, 16 * L)
                dve.wait_ge(s_done, l + 1)
                link(dve.tensor_scalar(logf, ps[0:HA, BO, 0:S], bf[:, l:l + 1], None, ALU.add))
                log_sigmoid_prep(logf, lsa, lsb).then_inc(s_biased, 1)
                dve.wait_ge(s_ln, l + 1)
                link(dve.tensor_tensor(logf, lsa, lsb, ALU.subtract))
                link(dve.tensor_tensor_scan(out=f_sum, data0=ones8, data1=logf, initial=0.0, op0=ALU.mult, op1=ALU.add))
                dve.tensor_copy(f_parts[:, 0, :], f_sum).then_inc(s_rows, 1)
                dve.wait_ge(s_rows, 3 * l + 1)
                dve.tensor_tensor(f_parts[:, 1, :], f_sum, f32(f_parts[:, 0, :]), ALU.subtract).then_inc(s_rows, 1)
                dve.wait_ge(s_rows, 3 * l + 2)
                dve.tensor_scalar(f_parts[:, 2:4, :], f32(f_parts[:, 0:2, :]), -1.0, None, ALU.mult).then_inc(s_rows, 1)
                split_to(units_until(G0 + 2))
                dve.wait_ge(g_lin, l + 1)
                for m in range(NPAIR):
                    col = R_BA + l * NPAIR + m
                    link(dve.tensor_scalar(lg[0][:, m * S:(m + 1) * S], ps[:, BX, m * S:(m + 1) * S],
                                           prm[:, col:col + 1], None, ALU.add))
                log_sigmoid_prep(lg[0], lg[1], lg[2]).then_inc(g_neg, 1)
                split_to(units_until(G0 + 2) + 1)
                dve.wait_ge(g_ln, l + 1)
                link(dve.tensor_tensor(lg[0], lg[1], lg[2], ALU.subtract))
                for m in range(NPAIR):
                    dve.tensor_tensor_scan(out=cum[:, m, :], data0=keep[:, :], data1=lg[0][:, m * S:(m + 1) * S],
                                           initial=0.0, op0=ALU.mult, op1=ALU.add).then_inc(dchain, 1)
                chain[0] += NPAIR
                dve.wait_ge(dchain, chain[0])
                c4 = cum[:, :, :].rearrange("p m (c t) -> p m c t", t=CH)
                for m in range(NPAIR):
                    dve.tensor_tensor(lg[3][:, m * S:(m + 1) * S].rearrange("p (c t) -> p c t", t=CH),
                                      c4[:, m, :, CH - 1:CH].to_broadcast([P, S // CH, CH]), c4[:, m, :, :],
                                      ALU.subtract).then_inc(g_cum, 1)

                def evacuate(p):
                    name = NAMES[p]
                    bank = ((G0 + p) % 2) * 2
                    if EVAC[p] != "dve":
                        return
                    if name == "out1":
                        ahead()
                    else:
                        dve.wait_ge(m_used, units_until(G0 + p))
                    src = banks(bank, 2)
                    if name == "cg":
                        dve.wait_ge(evac_act, evacuated(G0 + NAMES.index("u"), "act"))
                        dve.memset(zB[:, :, 0:2], 0.0)
                        link(dve.tensor_tensor(zB[:, :, 2:ZP], zB[:, :, 2:ZP], src.rearrange("p (a t) -> p a t", t=S),
                                               ALU.mult))
                        dve.sem_inc(evac_dve, 1)
                        for tap in range(3):
                            for c in range(4):
                                col = R_CONV + (l * 3 + tap) * 4 + c
                                w = prm[:, col:col + 1]
                                if tap == 0:
                                    link(dve.tensor_scalar(cvB[:, c, :], zB[:, c, 0:S], w, None, ALU.mult))
                                else:
                                    link(dve.scalar_tensor_tensor(out=cvB[:, c, :], in0=zB[:, c, tap:tap + S], scalar=w,
                                                                  in1=cvB[:, c, :], op0=ALU.mult, op1=ALU.add))
                    elif name == "bg":
                        cvf = cvB.rearrange("p a t -> p (a t)")
                        link(dve.tensor_tensor(cvf, cvf, src, ALU.mult))
                        dve.sem_inc(evac_dve, 1)
                        dve.sem_inc(b_y, 1)
                        dve.wait_ge(b_hi, l + 1)
                        dve.tensor_tensor(obc_lo[:, :, :], cvB, f32(obc_hi[:, :, :]), ALU.subtract).then_inc(b_out, 1)
                    elif name.startswith("proj"):
                        half = int(name[5])
                        dve.wait_ge(evac_act, evacuated(G0 + p - 1, "act"))
                        mh = merged[:, half * 4:half * 4 + 4, :].rearrange("p a t -> p (a t)")
                        gs = gate_s.rearrange("p a t -> p (a t)")
                        if name[4] == "1":
                            dve.tensor_tensor(mh, gs, src, ALU.mult).then_inc(evac_dve, 1)
                        else:
                            pr = prod_s.rearrange("p a t -> p (a t)")
                            link(dve.tensor_tensor(pr, gs, src, ALU.mult))
                            dve.sem_inc(evac_dve, 1)
                            ins = dve.tensor_tensor(mh, mh, pr, ALU.add)
                            link(ins)
                    else:
                        half = int(name[3])
                        cols = slice(half * UC, (half + 1) * UC)
                        for t in range(TT):
                            if half == 1:
                                dve.wait_ge(o_tile if t == 0 else m_used, l + 1 if t == 0 else units_until(G0 + p))
                            ins = dve.tensor_tensor(xres[:, t, cols], xres[:, t, cols], src[:, t * UC:(t + 1) * UC], ALU.add)
                            if half == 0:
                                ins.then_inc(dchain, 1)
                                chain[0] += 1
                            else:
                                ins.then_inc(x_ready, 1)
                        if half == 0:
                            dve.wait_ge(dchain, chain[0])
                        else:
                            dve.wait_ge(x_ready, TT * (2 * l + 1))
                        dve.sem_inc(evac_dve, 1)

                def scores(h):
                    a = l * HA + h
                    dve.wait_ge(a_score, a + 1)
                    if h >= 2:
                        dve.wait_ge(a_tr, a - 1)
                    bank = BX + h % 2
                    dve.tensor_tensor_reduce(out=probs[:, h % 2, 0:P], in0=ps[:, bank, 0:P], in1=cmask[:, P:2 * P],
                                             scale=1.0, scalar=-3e38, op0=ALU.add, op1=ALU.max,
                                             accum_out=mx[:, 2 * h:2 * h + 1])
                    link(dve.tensor_tensor_reduce(out=probs[:, h % 2, P:3 * P], in0=ps[:, bank, P:3 * P],
                                                  in1=cmask[:, :], scale=1.0, scalar=-3e38, op0=ALU.add, op1=ALU.max,
                                                  accum_out=mx[:, 2 * h + 1:2 * h + 2]))
                    dve.tensor_scalar(nmx[:, 2 * h:2 * h + 2], mx[:, 2 * h:2 * h + 2], -1.0, None,
                                      ALU.mult).then_inc(a_max, 1)

                def normalise(h):
                    a = l * HA + h
                    dve.wait_ge(a_exp, a + 1)
                    link(dve.reciprocal(rs[:, 2 * h:2 * h + 2], sm[:, 2 * h:2 * h + 2]))
                    dve.tensor_scalar(probs[:, h % 2, 0:P], probs[:, h % 2, 0:P], rs[:, 2 * h:2 * h + 1], None, ALU.mult)
                    dve.tensor_scalar(probs[:, h % 2, P:3 * P], probs[:, h % 2, P:3 * P], rs[:, 2 * h + 1:2 * h + 2],
                                      None, ALU.mult).then_inc(a_prob, 1)

                def head_out(h):
                    if h % 2 == 1:
                        dve.wait_ge(a_ohi, l * HA // 2 + h // 2 + 1)
                        dve.tensor_tensor(oa_lo[:, h // 2, :], ps[:, BO, 0:S], f32(oa_hi[:, h // 2, :]),
                                          ALU.subtract).then_inc(a_out, 1)

                for p in range(2, NPAN):
                    if 0 <= p - HS < HA:
                        scores(p - HS)
                    if NAMES[p] == "gate01":
                        dve.wait_ge(g_ocopy, l + 1)
                        s3 = sqC.rearrange("p a (b e) -> p a b e", e=DV)
                        link(dve.tensor_tensor(sqC, oC.rearrange("p (a t) -> p a t", t=S),
                                               oC.rearrange("p (a t) -> p a t", t=S), ALU.mult))
                        link(dve.tensor_reduce(out=oss[:, :], in_=s3, axis=AX.X, op=ALU.add))
                        dve.tensor_scalar(oss[:, :], oss[:, :], 1.0 / DV, EPS, ALU.mult, ALU.add).then_inc(g_ms, 1)
                    split_to(units_until(G0 + p) + 2)
                    if 0 <= p - HS < HA:
                        normalise(p - HS)
                    if 0 <= p - HS - 2 < HA:
                        head_out(p - HS - 2)
                    if NAMES[p] == "cqk":
                        dve.wait_ge(evac_act, evacuated(G0 + p, "act"))
                        dve.wait_ge(g_es, 4 * (l + 1))
                        cq = cqkT[:, 0:NPAIR, :].rearrange("p a t -> p (a t)")
                        ck = cqkT[:, NPAIR:2 * NPAIR, :].rearrange("p a t -> p (a t)")
                        link(dve.tensor_tensor(kst.rearrange("p a t -> p (a t)"), ck, lg[3], ALU.mult))
                        dve.tensor_tensor(ck, ck, lg[1], ALU.mult)
                        link(dve.scalar_tensor_tensor(out=cq, in0=cq, scalar=DK ** -0.5, in1=lg[0], op0=ALU.mult,
                                                      op1=ALU.mult))
                        dve.sem_inc(g_in, 1)
                    if NAMES[p] == "proj11":
                        dve.wait_ge(g_att, l + 1)
                        m3 = gmask[:, :].rearrange("p (a q) -> p a q", a=1).to_broadcast([P, 8, P])
                        dve.tensor_tensor(attC.rearrange("p (a q) -> p a q", q=P),
                                          banks(BX, 2).rearrange("p (a q) -> p a q", q=P), m3, ALU.mult).then_inc(g_attm, 1)
                    if NAMES[p] == "gate00":
                        dve.wait_ge(g_kv, l + 1)
                        link(dve.tensor_copy(states[:, 0, :, :].rearrange("p m e -> p (m e)"), ps[:, BO, 0:NPAIR * DV]))
                        for c in range(1, 3):
                            src = ps[:, BO, 256:512] if c == 2 else ps[:, BT, 0:256]
                            for m in range(NPAIR):
                                ins = dve.scalar_tensor_tensor(out=states[:, c, m, :], in0=states[:, c - 1, m, :],
                                                               scalar=decay[:, m, c:c + 1],
                                                               in1=src[:, m * DV:(m + 1) * DV], op0=ALU.mult, op1=ALU.add)
                            link(ins)
                        dve.sem_inc(g_state, 1)
                    if NAMES[p] == "gate01":
                        o3 = oC.rearrange("p (a e) -> p a e", e=DV)
                        dve.wait_ge(g_rstd, l + 1)
                        link(dve.tensor_tensor(o3, o3, ors[:, :].rearrange("p (a b) -> p a b", b=1).to_broadcast([P, 8, DV]),
                                               ALU.mult))
                        r5 = rC.rearrange("p t (m r e) -> p t m r e", m=NPAIR, r=2)
                        o5 = oC.rearrange("p (r t m e) -> p r t m e", r=2, t=TT, m=NPAIR)
                        for r in range(2):
                            for t in range(TT):
                                ins = dve.tensor_tensor(o5[:, r, t, :, :], o5[:, r, t, :, :], r5[:, t, :, r, :], ALU.mult)
                        ins.then_inc(g_on, 1)
                    if NAMES[p] == "gate20":
                        for h in range(HC):
                            col = R_GG + l * HC + h
                            dve.wait_ge(g_ohi, l * HC + h // 2 * 2 + 2)
                            dve.scalar_tensor_tensor(out=obc_lo[:, h, :], in0=banks(BT, 2)[:, h * S:(h + 1) * S],
                                                     scalar=prm[:, col:col + 1], in1=f32(obc_hi[:, h, :]), op0=ALU.mult,
                                                     op1=ALU.subtract).then_inc(g_out, 1)
                    evacuate(p)
                    if NAMES[p] in ("proj20", "proj21"):
                        half = int(NAMES[p][5])
                        dve.sem_inc(mg_sum, 1)
                        dve.wait_ge(mg_hi, 2 * l + half + 1)
                        dve.tensor_tensor(merged_lo[half], merged[:, 4 * half:4 * half + 4, :], f32(merged_hi[half]),
                                          ALU.subtract).then_inc(mg_out, 1)

            def dlo(t, slot, s):
                dve.wait_ge(d_hi[t], s + 1)
                dve.tensor_tensor(w_lo[:, t, :], raw[:, slot, :], f32(w_hi[:, t, :]), ALU.subtract).then_inc(d_lo[t], 1)

            normalise_stream(0, n_hn)
            split_unit(0)
            act_lo_of(0)
            split_unit(1)
            dve.wait_ge(consts, 2)
            mixer(0, lambda: dlo(1, 1, 0))
            normalise_stream(1, n_hn)
            dlo(0, 0, 0)
            act_lo_of(1)

            def dense_hidden(s, parity):
                dve.wait_ge(d_silu, s + 1)
                f = dsilu[:, :, :].rearrange("p a t -> p (a t)")
                dve.tensor_tensor(f, f, banks(2 * parity + 1), ALU.mult).then_inc(d_h, 1)

            def dense_hidden_lo(s):
                dve.wait_ge(d_hhi, s + 1)
                dve.tensor_tensor(dh_lo[:, :, :], dsilu[:, :, :], f32(dh_hi[:, :, :]), ALU.subtract).then_inc(d_hT, 1)

            def dense_step(q, parity, up, down):
                s = 2 * q + parity
                if up:
                    for t in range(2):
                        dlo(t, 3 * parity + t, s)
                if down:
                    dense_hidden(s - 1, 1 - parity)
                    dlo(2, 3 * parity + 2, s - 1)
                    dense_hidden_lo(s - 1)

            dense_step(0, 1, True, True)
            with dve.Fori(1, NF // 2) as q:
                dense_step(q, 0, True, True)
                dense_step(q, 1, True, True)
            dense_step(NF // 2, 0, True, True)
            dve.wait_ge(d_hi[2], NF)
            dve.tensor_tensor(w_lo[:, 0, :], raw[:, 5, :], f32(w_hi[:, 0, :]), ALU.subtract).then_inc(d_lo[2], 1)
            dense_hidden(NF - 1, 0)
            dve.wait_ge(d_hhi, NF)
            dve.tensor_tensor(dlate_lo[:, :, :], dsilu[:, :, :], f32(dlate_hi[:, :, :]), ALU.subtract).then_inc(d_hT, 1)
            u = before_units(1)
            split_unit(u)
            for t in range(TT):
                dve.wait_ge(d_tile if t == 0 else d_used[2], 1 if t == 0 else NF)
                dve.tensor_tensor(xres[:, t, :], xres[:, t, :], banks(4 + 2 * t, 2), ALU.add).then_inc(x_ready, 1)
            normalise_stream(2, n_hn)
            act_lo_of(2)
            split_unit(u + 1)

            def elo(t, fs, s, slot=None, src=None):
                slot = t if slot is None else slot
                dve.wait_ge(e_hi[t], s + 1)
                dve.tensor_tensor(w_lo[:, slot, :], raw[:, 3 * t + fs, :] if src is None else src, f32(w_hi[:, slot, :]),
                                  ALU.subtract).then_inc(e_lo[t], 1)

            def half_gu(t, e, f, fs):
                elo(t, fs, NF * e + f, split_slot(e, f, t), arriving(e, f, t, fs))

            def step_gu(e, f, fs):
                for t in range(2):
                    half_gu(t, e, f, fs)

            def hidden(e, f, bank):
                dve.wait_ge(e_silu, NF * e + f + 1)
                dve.wait_ge(e_tr, NF * e + f + 1)
                dve.tensor_tensor(hid[:, :], esilu[:, :], ps[:, bank, FC:2 * FC], ALU.mult).then_inc(e_h, 1)

            def hidden_lo(e, f, hi=eh_hi[:, :, :], to=eh_lo[:, :, :]):
                dve.wait_ge(e_hhi, NF * e + f + 1)
                dve.tensor_tensor(to.rearrange("p a t -> p (a t)"), ps[:, 3, 0:2 * CAP],
                                  f32(hi).rearrange("p a t -> p (a t)"), ALU.subtract).then_inc(e_hT, 1)

            def pick_of(e, ew):
                for t in range(TT):
                    dve.tensor_scalar(pick[:, t, :], iota[:, :], rank[:, t, ds(ew, 1)], None, ALU.is_equal).then_inc(e_pick, 1)

            def tokens_lo(e):
                for b in range(2):
                    dve.wait_ge(e_xhi, 2 * e + b + 1)
                    dve.tensor_tensor(xs_lo[:, 4 * b:4 * b + 4, :].rearrange("p a t -> p (a t)"), banks(4 + b),
                                      f32(xs_hi[:, 4 * b:4 * b + 4, :]).rearrange("p a t -> p (a t)"),
                                      ALU.subtract).then_inc(e_x, 1)

            def output_lo(e):
                dve.wait_ge(e_yhi, e + 1)
                dve.wait_ge(e_gsel, e + 1)
                dve.scalar_tensor_tensor(out=y_lo[:, :], in0=banks(6, 2), scalar=gsel[:, 0:1], in1=f32(y_hi[:, :]),
                                         op0=ALU.mult, op1=ALU.subtract).then_inc(e_ylo, 1)

            def scatter_add(e, t, bank=4):
                dve.wait_ge(e_sc, TT * e + t + 1)
                dve.wait_ge(e_add, TT * e + t + 1)
                dve.tensor_tensor(xres[:, t, :], xres[:, t, :], banks(bank, 2), ALU.add).then_inc(e_add, 1)

            def wide(v):
                return v[:, :].rearrange("p (t a) -> p t a", a=1).to_broadcast([P, TT, NE])

            def routing_gates():
                dve.wait_ge(r_e, 1)
                link(dve.tensor_scalar(wt1[:, :], wt2[:, :], 1.0, None, ALU.add))
                link(dve.reciprocal(wt1[:, :], wt1[:, :]))
                link(dve.tensor_tensor(wt2[:, :], wt2[:, :], wt1[:, :], ALU.mult))
                link(dve.tensor_tensor(first[:, :, :], first[:, :, :], wide(wt1), ALU.mult))
                link(dve.tensor_tensor(second[:, :, :], second[:, :, :], wide(wt2), ALU.mult))
                dve.tensor_tensor(gates[:, :, :], first[:, :, :], second[:, :, :], ALU.add).then_inc(r_gates, 1)

            def expert(e, ew, opening):
                if not (isinstance(e, int) and e == 0):
                    step_gu(e, 0, 0)
                tokens_lo(e)
                if not opening:
                    hidden(e - 1, NF - 1, (NF - 1) % 3)
                if isinstance(e, int) and e == 0:
                    routing_gates()
                if not opening:
                    elo(2, 0, NF * (e - 1) + NF - 2)
                    hidden_lo(e - 1, NF - 2)
                for f in range(1, 5):
                    if isinstance(e, int) and e == 0 and f == 1:
                        half_gu(1, e, f, 1)
                    else:
                        step_gu(e, f, f % 3)
                    hidden(e, f - 1, (f - 1) % 3)
                    if f == 1:
                        if not opening:
                            elo(2, 1, NF * (e - 1) + NF - 1)
                            hidden_lo(e - 1, NF - 1)
                        continue
                    if f == 2 and not opening:
                        output_lo(e - 1)
                    if f == 3 and not opening:
                        scatter_add(e - 1, 1)
                    elo(2, f - 2, NF * e + f - 2)
                    hidden_lo(e, f - 2)
                    if f == 2 and not opening:
                        scatter_add(e - 1, 0)
                dve.wait_ge(e_pt, e + 1)
                dve.tensor_copy(gsel[:, :], ps[:, 5, ds(ew, 1)]).then_inc(e_gsel, 1)
                pick_of(e + 1, ew + 1)
                with dve.Fori(0, (NF - 5) // 3) as j:
                    for i in range(3):
                        step_gu(e, 3 * j + 5 + i, (2 + i) % 3)
                        hidden(e, 3 * j + 4 + i, (1 + i) % 3)
                        elo(2, i, NF * e + 3 * j + 3 + i)
                        hidden_lo(e, 3 * j + 3 + i)

            def expert_pass(k):
                expert(NE * k, 0, True)
                with dve.Fori(NE * k + 1, NE * (k + 1)) as e:
                    expert(e, e - NE * k, False)
                e = NE * (k + 1) - 1
                elo(2, (NF - 2) % 3, NF * e + NF - 2, 0)

                def late_half(h):
                    cols = slice(h * UN // 2, (h + 1) * UN // 2)
                    return dve.tensor_tensor(w_lo[:, 1, cols], raw[:, 6 + (NF - 1) % 3, cols], f32(w_hi[:, 1, cols]),
                                             ALU.subtract)
                dve.wait_ge(e_hi[2], NF * (e + 1))
                late_half(0)
                hidden(e, NF - 1, (NF - 1) % 3)
                hidden_lo(e, NF - 2)
                late_half(1).then_inc(e_lo[2], 1)
                hidden_lo(e, NF - 1, late_h_hi, late_h_lo)
                for half in range(2):
                    cols = slice(half * UC, (half + 1) * UC)
                    dve.wait_ge(l_yhi if half == 0 else e_yhi, k + 1 if half == 0 else e + 1)
                    dve.wait_ge(e_gsel, e + 1)
                    dve.scalar_tensor_tensor(out=y_lo[:, cols], in0=ps[:, 6 + half, :], scalar=gsel[:, 0:1],
                                             in1=f32(y_hi[:, cols]), op0=ALU.mult,
                                             op1=ALU.subtract).then_inc(l_ylo if half == 0 else e_ylo, 1)
                for t in range(TT):
                    scatter_add(e, t, late_bank(t))

            dve.sem_inc(e_h, 2)
            dve.sem_inc(e_add, 1)

            def ahead_of_experts():
                dve.wait_ge(wr_loaded, 16)
                dve.wait_ge(r_zero, 2)
                link(dve.tensor_copy(xs_hi[:, :, 0:NE], wr[:, :, :]))
                dve.tensor_tensor(xs_lo[:, :, 0:NE], wr[:, :, :], f32(xs_hi[:, :, 0:NE]), ALU.subtract).then_inc(r_split, 1)
                dve.wait_ge(r_iota, 1)
                link(dve.tensor_copy(iota[:, :], iota_i))
                link(dve.memset(one16[:, :, :], 1.0))
                link(dve.memset(one16[:, :, 0:1], 0.0))
                link(dve.memset(rank[:, :, NE:NE + 1], -1.0))
                elo(0, 0, 0)

            mixer(1, ahead_of_experts)
            normalise_stream(3, n_hn)
            act_lo_of(3)
            elo(1, 0, 0)

            dve.wait_ge(r_logit, 1)
            dve.tensor_copy(lgT[:, :], ps[0:NE, 0, 0:S]).then_inc(r_lgT, 1)
            dve.wait_ge(r_logit, 2)
            lf = lgt[:, :, :].rearrange("p t e -> p (t e)")
            link(dve.tensor_copy(lf, ps[:, 1, 0:TT * NE]))

            def flat(v):
                return v[:, :, :].rearrange("p t e -> p (t e)")

            def first_of_largest(src, v, pickd):
                link(dve.tensor_reduce(out=v[:, :], in_=src[:, :, :], axis=AX.X, op=ALU.max))
                link(dve.tensor_tensor(eq[:, :, :], src[:, :, :], wide(v), ALU.is_equal))
                link(dve.tensor_tensor_scan(out=flat(cnt), data0=flat(one16), data1=flat(eq), initial=0.0,
                                            op0=ALU.mult, op1=ALU.add))
                link(dve.scalar_tensor_tensor(out=pickd[:, :, :], in0=cnt[:, :, :], scalar=1.0, in1=eq[:, :, :],
                                              op0=ALU.is_le, op1=ALU.mult))
            first_of_largest(lgt, v1, first)
            link(dve.scalar_tensor_tensor(out=lgt2[:, :, :], in0=first[:, :, :], scalar=-3e38, in1=lgt[:, :, :],
                                          op0=ALU.mult, op1=ALU.add))
            first_of_largest(lgt2, v2, second)
            dve.tensor_tensor(wt2[:, :], v2[:, :], v1[:, :], ALU.subtract).then_inc(r_v, 1)
            dve.tensor_tensor(chosen[:, :, :], first[:, :, :], second[:, :, :], ALU.add).then_inc(r_chosen, 1)
            dve.wait_ge(r_cum, 1)
            link(dve.tensor_tensor(rank[:, :, 0:NE], ps[:, BY, 0:TT * NE].rearrange("p (t e) -> p t e", e=NE),
                                   chosen[:, :, :], ALU.mult))
            link(dve.tensor_scalar(rank[:, :, 0:NE], rank[:, :, 0:NE], -1.0, None, ALU.add))
            dve.tensor_reduce(out=most[:, :], in_=ps[:, BY, TT * NE:(TT + 1) * NE], axis=AX.X, op=ALU.max).then_inc(r_rank, 1)

            dve.wait_ge(r_rank, 1)
            pick_of(0, 0)
            half_gu(0, 0, 1, 1)
            expert_pass(0)
            fullest = dve.value_load(most[0:1, 0:1])
            with dve.If(fullest > CAP):
                dve.wait_ge(e_pick, 2 * (NE + 1))
                link(dve.tensor_scalar(rank[:, :, 0:NE], rank[:, :, 0:NE], -float(CAP), None, ALU.add))
                for t in range(TT):
                    dve.tensor_scalar(pick[:, t, :], iota[:, :], rank[:, t, 0:1], None, ALU.is_equal).then_inc(e_again, 1)
                expert_pass(1)
                dve.wait_ge(e_add, 2 * TT * NE + 1)
            dve.wait_ge(e_add, TT * NE + 1)
            dve.sem_inc(x_ready, TT)
            normalise_stream(4, f_scaled)

        @block.tensor
        def _(pe):
            def mm3(o, a_hi, a_lo, b_hi, b_lo, start, stop):
                pe.matmul(o, a_hi, b_hi, start=start, stop=False, skip_group_check=True)
                pe.matmul(o, a_hi, b_lo, start=False, stop=False, skip_group_check=True)
                return pe.matmul(o, a_lo, b_hi, start=False, stop=stop, skip_group_check=True)

            def norm(n):
                for t in range(TT):
                    pe.wait_ge(n_hn, TT * n + t + 1)
                    for k in range(KD):
                        ins = pe.transpose(ps[:, 4 + k // 2, (k % 2) * S + t * P:(k % 2) * S + (t + 1) * P],
                                           hn[:, t, k * P:(k + 1) * P], ident[:, :])
                        if t == TT - 1 and k % 2 == 1:
                            ins.then_inc(n_tr, 1)

            def keep_warm(count):
                for _ in range(count):
                    pe.matmul(ps[:, 3, 0:3 * P], tri[:, 0:P], tri[:, :], start=True, stop=True, skip_group_check=True)

            def stream_ready(n, k):
                if k % 2 == 0:
                    pe.wait_ge(n_act, 4 * n + k // 2 + 1)

            def mixer(l):
                n = [before_units(l)]
                G0 = l * NPAN
                operands = {"act": (act_hi, act_lo), "o0": (oa_hi, oa_lo), "o1": (obc_hi, obc_lo),
                            "o2": (obc_hi, obc_lo), "merged": None}

                def panel(p):
                    name, _, _, ws, kt, operand, _ = panels_of(l)[p]
                    g = G0 + p
                    b0 = (g % 2) * 2
                    if p >= 2:
                        who = EVAC[p - 2]
                        pe.wait_ge(evac_act if who == "act" else evac_dve, evacuated(g - 2, who))
                    if name == "proj10":
                        pe.wait_ge(b_out, l + 1)
                    if name == "proj00":
                        pe.wait_ge(a_out, HA // 2 * (l + 1))
                    if name == "proj20":
                        pe.wait_ge(g_out, HC * (l + 1))
                    for j in range(kt // KW):
                        u = n[0]
                        if name == "out0":
                            pe.wait_ge(mg_out, 2 * l + j + 1)
                        hi, lo = operands[operand] if operand != "merged" else (merged_hi[j], merged_lo[j])
                        pe.wait_ge(m_lo, u + 1)
                        steps = [(kk, c) for kk in range(KW) for c in range(4)] if ws else \
                            [(kk, c) for c in range(TT) for kk in range(KW)]
                        for kk, c in steps:
                            k = j * KW + kk
                            last = k == kt - 1
                            ko = kk if operand == "merged" else k
                            if p == 0 and c == 0:
                                stream_ready(2 * l, k)
                            if ws:
                                w = slice(kk * UC + c * P, kk * UC + (c + 1) * P)
                                ins = mm3(ps[:, b0 + c // 2, (c % 2) * S:(c % 2 + 1) * S],
                                          w_hi[:, u % SRING, w], w_lo[:, u % SRING, w], hi[:, ko, :], lo[:, ko, :],
                                          k == 0 and c % 2 == 0, last)
                            else:
                                w = slice(kk * UC, (kk + 1) * UC)
                                tok = slice(c * P, (c + 1) * P)
                                ins = mm3(ps[:, b0 + c, :], hi[:, ko, tok], lo[:, ko, tok],
                                          w_hi[:, u % SRING, w], w_lo[:, u % SRING, w], k == 0, last)
                                if last and name == "out1" and c == 0:
                                    ins.then_inc(o_tile, 1)
                        ins.then_inc(m_used, 1)
                        n[0] += 1

                def narrow():
                    pe.wait_ge(n_act, 4 * (2 * l + 1))
                    pe.wait_ge(s_split, l + 1)
                    for k in range(KD):
                        ins = mm3(ps[0:NW, BO, 0:S], wsm_hi[:, k, :], wsm_lo[:, k, :], act_hi[:, k, :], act_lo[:, k, :],
                                  k == 0, k == KD - 1)
                    ins.then_inc(s_done, 1)

                def decay_logits():
                    pe.wait_ge(s_aTc, l + 1)
                    pe.wait_ge(wa2_loaded, 16 * (l + 1))
                    for m in range(NPAIR):
                        ins = pe.matmul(ps[:, BX, m * S:(m + 1) * S], wa2[:, m * P:(m + 1) * P], aT,
                                        start=m == 0, stop=True, skip_group_check=True)
                    ins.then_inc(g_lin, 1)

                def head_scores(h):
                    a = l * HA + h
                    if h == 0:
                        pe.wait_ge(s_frow[0], 64 * (l + 1))
                        pe.wait_ge(evac_act, evacuated(G0 + 1, "act"))
                        pe.wait_ge(g_neg, l + 1)
                    if h == 4:
                        pe.wait_ge(s_frow[1], 64 * (l + 1))
                    if h >= 2:
                        pe.wait_ge(a_max, a - 1)
                    r, m, g = (h % 2) * DH, h // 2, 32 * (h % 4)
                    bank = BX + h % 2
                    for t, cols in ((0, slice(0, P)), (1, slice(P, 3 * P))):
                        q = slice(t * P, (t + 1) * P)
                        nk = (t + 1) * P
                        pe.matmul(ps[:, bank, cols], qT[r:r + DH, m, q], kT[r:r + DH, m, 0:nk], start=True, stop=False)
                        ins = pe.matmul(ps[:, bank, cols], f_query[g:g + 4, h // 4, q], f_key[g:g + 4, h // 4, 0:nk],
                                        start=False, stop=True)
                    ins.then_inc(a_score, 1)

                def head_transpose(h):
                    a = l * HA + h
                    pe.wait_ge(a_prob, a + 1)
                    if h > 0:
                        pe.wait_ge(a_pt, a)
                    for i in range(3):
                        ins = pe.transpose(ps[:, BT, i * P:(i + 1) * P], probs[:, h % 2, i * P:(i + 1) * P], ident[:, :])
                    ins.then_inc(a_tr, 1)

                def head_values(h):
                    a = l * HA + h
                    pe.wait_ge(a_pt, a + 1)
                    if h % 2 == 0:
                        if h > 0:
                            pe.wait_ge(a_out, HA // 2 * l + h // 2)
                        else:
                            pe.wait_ge(evac_act, evacuated(G0 + 2, "act"))
                    r = (h % 2) * DH
                    v = slice(h * DH, (h + 1) * DH)
                    pe.matmul(ps[r:r + DH, BO, 0:S], vA[:, 0, v], probsT[:, 0:S], start=True, stop=False)
                    pe.matmul(ps[r:r + DH, BO, P:S], vA[:, 1, v], probsT[:, 2 * P:3 * P], start=False,
                              stop=True).then_inc(a_pv, 1)

                def gla_scores():
                    pe.wait_ge(g_in, l + 1)
                    pe.wait_ge(a_max, HA * (l + 1))
                    for r in range(2):
                        for t in range(TT):
                            for m in range(NPAIR):
                                rows, tok = slice(r * DK, (r + 1) * DK), slice(t * P, (t + 1) * P)
                                c = (t * NPAIR + m) * P
                                ins = pe.matmul(ps[:, BX + r, c:c + P], cqkT[rows, NPAIR + m, tok], cqkT[rows, m, tok],
                                                start=c == 0, stop=True, skip_group_check=True)
                    ins.then_inc(g_att, 1)
                    pe.wait_ge(a_pt, HA * (l + 1))
                    for t in range(TT):
                        for m in range(NPAIR):
                            c = (t * NPAIR + m) * P
                            ins = pe.transpose(ps[:, BT, c:c + P], kst[:, m, t * P:(t + 1) * P], ident[:, :])
                    ins.then_inc(g_kstT, 1)

                def gla_states():
                    pe.wait_ge(g_kst, l + 1)
                    pe.wait_ge(a_out, HA // 2 * (l + 1))
                    for i, c in enumerate((0, 2, 1)):
                        bank, col = (BT, 0) if c == 1 else (BO, (c // 2) * NPAIR * DV)
                        rows = slice((c % 2) * CH, (c % 2 + 1) * CH)
                        for m in range(NPAIR):
                            for r in range(2):
                                kc = ((c // 2) * NPAIR + m) * P + r * DK
                                h = 2 * m + r
                                ins = pe.matmul(ps[r * DK:(r + 1) * DK, bank, col + m * DV:col + (m + 1) * DV],
                                                kst_tok[rows, kc:kc + DK], vC[rows, c // 2, h * DV:(h + 1) * DV],
                                                start=(i != 1 and m == 0), stop=True, skip_group_check=True)
                    ins.then_inc(g_kv, 1)

                def gla_out():
                    pe.wait_ge(g_attm, l + 1)
                    for r in range(2):
                        for t in range(TT):
                            for m in range(NPAIR):
                                c = (t * NPAIR + m) * P
                                h = 2 * m + r
                                pe.matmul(ps[:, BX + r, c:c + P], attC[:, r * 4 * P + c:r * 4 * P + c + P],
                                          vC[:, t, h * DV:(h + 1) * DV], start=c == 0, stop=False, skip_group_check=True)
                    pe.wait_ge(g_state, l + 1)
                    for r in range(2):
                        rows = slice(r * DK, (r + 1) * DK)
                        for c in range(1, S // CH):
                            for m in range(NPAIR):
                                col = ((c // 2) * NPAIR + m) * P
                                ins = pe.matmul(ps[(c % 2) * CH:(c % 2 + 1) * CH, BX + r, col:col + P],
                                                cqkT[rows, m, c * CH:(c + 1) * CH], states[rows, c - 1, m, :],
                                                start=False, stop=True, skip_group_check=True)
                    ins.then_inc(g_o, 1)

                def gla_transpose():
                    pe.wait_ge(g_on, l + 1)
                    for h in range(HC):
                        for t in range(TT):
                            c = (((h % 2) * TT + t) * NPAIR + h // 2) * P
                            ins = pe.transpose(banks(BT, 2)[:, h * S + t * P:h * S + (t + 1) * P], oC[:, c:c + P],
                                               ident[:, :])
                    ins.then_inc(g_oT, 1)

                panel(0)
                narrow()
                if l == 0:
                    pe.wait_ge(prm_loaded, 64)
                    pe.transpose(ps[:, BT, 0:NPRM], prm_rows, ident[0:NPRM, 0:NPRM]).then_inc(prm_tr, 1)
                panel(1)
                decay_logits()
                for p in range(2, NPAN):
                    if 0 <= p - HS < HA:
                        head_scores(p - HS)
                    if 0 <= p - HS - 1 < HA:
                        head_transpose(p - HS - 1)
                    if 0 <= p - HS - 2 < HA:
                        head_values(p - HS - 2)
                    if NAMES[p] == "proj11":
                        gla_scores()
                    if NAMES[p] == "gate00":
                        gla_states()
                    if NAMES[p] == "proj00":
                        gla_out()
                    if NAMES[p] == "gate20":
                        gla_transpose()
                    panel(p)

            pe.wait_ge(consts, 1)
            norm(0)
            mixer(0)
            norm(1)

            def up(s, parity):
                for t in range(2):
                    pe.wait_ge(d_lo[t], s + 1)
                    w_h = w_hi[:, t, :].rearrange("p (k w n) -> p k w n", k=KW, w=2)
                    w_l = w_lo[:, t, :].rearrange("p (k w n) -> p k w n", k=KW, w=2)
                    for kk in range(KW):
                        k = t * KW + kk
                        if isinstance(s, int) and s == 0:
                            stream_ready(1, k)
                        for w in range(2):
                            for c in range(2):
                                cc = slice(c * P, (c + 1) * P)
                                ins = mm3(ps[:, 2 * parity + w, c * S:(c + 1) * S], w_h[:, kk, w, cc], w_l[:, kk, w, cc],
                                          act_hi[:, k, :], act_lo[:, k, :], k == 0 and c == 0, k == KD - 1)
                    ins.then_inc(d_used[t], 1)

            def down(s, stop, slot=2, h_hi=dh_hi, h_lo=dh_lo):
                pe.wait_ge(d_hT, s + 1)
                pe.wait_ge(d_lo[2], s + 1)
                for t in range(TT):
                    for k in range(2):
                        tok = slice(t * P, (t + 1) * P)
                        for half in range(2):
                            cols = slice(k * D + half * UC, k * D + (half + 1) * UC)
                            ins = mm3(ps[:, 4 + 2 * t + half, :], h_hi[:, k, tok], h_lo[:, k, tok],
                                      w_hi[:, slot, cols], w_lo[:, slot, cols], False, stop and k == 1)
                    if stop and t == 0:
                        ins.then_inc(d_tile, 1)
                ins.then_inc(d_used[2], 1)

            def open_sums(first, nb):
                for b in range(first, first + nb):
                    pe.matmul(ps[:, b, :], zrow[0:1, 0:P], zrow[0:1, :], start=True, stop=False, skip_group_check=True)

            up(0, 0)
            up(1, 1)
            open_sums(4, 4)
            down(0, False)
            with pe.Fori(0, (NF - 3) // 2) as j:
                for i in range(2):
                    s = 2 * j + 2 + i
                    pe.wait_ge(d_h, s - 1)
                    up(s, i)
                    down(s - 1, False)
            pe.wait_ge(d_h, NF - 2)
            up(NF - 1, (NF - 1) % 2)
            down(NF - 2, False)
            down(NF - 1, True, 0, dlate_hi, dlate_lo)

            norm(2)
            mixer(1)
            norm(3)

            pe.wait_ge(r_split, 1)
            for k in range(KD):
                stream_ready(3, k)
                ins = mm3(ps[0:NW, 0, 0:S], xs_hi[:, k, 0:NW], xs_lo[:, k, 0:NW], act_hi[:, k, :], act_lo[:, k, :],
                          k == 0, k == KD - 1)
            ins.then_inc(r_logit, 1)
            pe.wait_ge(r_lgT, 1)
            for t in range(TT):
                ins = pe.transpose(ps[:, 1, t * NE:(t + 1) * NE], lgT[:, t * P:(t + 1) * P], ident[0:NE, 0:NE])
            ins.then_inc(r_logit, 1)
            keep_warm(12)
            pe.wait_ge(r_chosen, 1)
            for t in range(TT):
                for s in range(TT):
                    ins = pe.matmul(ps[:, BY, t * NE:(t + 1) * NE], tri[:, (1 - s + t) * P:(2 - s + t) * P], chosen[:, s, :],
                                    start=t == 0 and s == 0, stop=s == TT - 1, skip_group_check=True)
            for s in range(TT):
                ins = pe.matmul(ps[:, BY, TT * NE:(TT + 1) * NE], tri[:, 2 * P:3 * P], chosen[:, s, :], start=False,
                                stop=s == TT - 1, skip_group_check=True)
            ins.then_inc(r_cum, 1)

            def eup(e, f, bank, fresh=False):
                for t in range(2):
                    if fresh:
                        pe.wait_ge(e_x, 2 * e + t + 1)
                    pe.wait_ge(e_lo[t], NF * e + f + 1)
                    slot = split_slot(e, f, t)
                    for kk in range(KW):
                        k = t * KW + kk
                        cols = slice(kk * UC, (kk + 1) * UC)
                        ins = mm3(ps[:, bank, :], xs_hi[:, k, :], xs_lo[:, k, :], w_hi[:, slot, cols], w_lo[:, slot, cols],
                                  k == 0, k == KD - 1)
                    ins.then_inc(e_used[t], 1)

            def edown(e, f, stop=False, slot=2, h=None):
                h_hi, h_lo = h or (eh_hi, eh_lo)
                pe.wait_ge(e_hT, NF * e + f + 1)
                pe.wait_ge(e_lo[2], NF * e + f + 1)
                for k in range(2):
                    for half in range(2):
                        cols = slice(k * D + half * UC, k * D + (half + 1) * UC)
                        ins = mm3(ps[:, 6 + half, :], h_hi[:, k, :], h_lo[:, k, :], w_hi[:, slot, cols], w_lo[:, slot, cols],
                                  False, stop and k == 1)
                ins.then_inc(e_used[2], 1)

            def etranspose(e, f):
                pe.wait_ge(e_h, NF * e + f + 3)
                for k in range(2):
                    ins = pe.transpose(ps[:, 3, k * CAP:(k + 1) * CAP], hid[:, k * P:(k + 1) * P], ident[:, :])
                ins.then_inc(e_tr, 1)

            def gather(e):
                pe.wait_ge(e_pick, 2 * (e + 1))
                for k in range(KD):
                    for t in range(TT):
                        ins = pe.matmul(ps[:, 4 + k // 4, (k % 4) * CAP:(k % 4 + 1) * CAP], hn[:, t, k * P:(k + 1) * P],
                                        pick[:, t, :], start=k % 4 == 0 and t == 0, stop=t == TT - 1, skip_group_check=True)
                    if k % 4 == 3:
                        ins.then_inc(e_gath, 1)

            def scatter(e, t):
                if t == 0:
                    pe.wait_ge(e_ylo, e + 1)
                else:
                    pe.wait_ge(e_add, TT * e + 2)
                for half in range(2):
                    cols = slice(half * UC, (half + 1) * UC)
                    pe.matmul(ps[:, 4 + half, :], pickT[:, t * P:(t + 1) * P], y_hi[:, cols], start=True, stop=False)
                    ins = pe.matmul(ps[:, 4 + half, :], pickT[:, t * P:(t + 1) * P], y_lo[:, cols], start=False, stop=True)
                ins.then_inc(e_sc, 1)

            def slots(e):
                for t in range(TT):
                    pe.transpose(ps[:, 4, t * P:(t + 1) * P], pick[:, t, :], ident[:, :])
                for t in range(TT):
                    ins = pe.matmul(ps[:, 5, 0:NE], pick[:, t, :], gates[:, t, :], start=t == 0, stop=t == TT - 1)
                ins.then_inc(e_pt, 1)

            def eup_step(e, f, bank):
                pe.wait_ge(e_h, NF * e + f)
                eup(e, f, bank)

            def expert(e, opening):
                if not (isinstance(e, int) and e == 0):
                    pe.wait_ge(e_ptc, e)
                    pe.wait_ge(e_gsel, e)
                gather(e)
                if not opening:
                    edown(e - 1, NF - 3)
                    etranspose(e - 1, NF - 2)
                pe.wait_ge(e_h, NF * e + 1)
                eup(e, 0, 0, True)
                if not opening:
                    edown(e - 1, NF - 2)
                    etranspose(e - 1, NF - 1)
                pe.wait_ge(e_h, NF * e + 2)
                eup(e, 1, 1)
                if not opening:
                    edown(e - 1, NF - 1, True)
                etranspose(e, 0)
                eup_step(e, 2, 2)
                if not opening:
                    pe.wait_ge(e_ylo, e)
                open_sums(6, 2)
                if not opening:
                    scatter(e - 1, 0)
                edown(e, 0)
                etranspose(e, 1)
                if not opening:
                    scatter(e - 1, 1)
                eup_step(e, 3, 0)
                edown(e, 1)
                etranspose(e, 2)
                if not opening:
                    pe.wait_ge(e_add, TT * e + 1)
                if isinstance(e, int) and e == 0:
                    pe.wait_ge(r_gates, 1)
                slots(e)
                eup_step(e, 4, 1)
                with pe.Fori(0, (NF - 5) // 3) as j:
                    for i in range(3):
                        edown(e, 3 * j + 2 + i)
                        etranspose(e, 3 * j + 3 + i)
                        eup_step(e, 3 * j + 5 + i, (2 + i) % 3)

            def expert_pass(k):
                expert(NE * k, True)
                with pe.Fori(NE * k + 1, NE * (k + 1)) as e:
                    expert(e, False)
                e = NE * (k + 1) - 1
                edown(e, NF - 3)
                etranspose(e, NF - 2)
                pe.wait_ge(e_hT, NF * e + NF - 1)
                etranspose(e, NF - 1)
                edown(e, NF - 2, False, 0)
                edown(e, NF - 1, True, 1, (late_h_hi, late_h_lo))
                for half in range(2):
                    pe.wait_ge(l_ylo if half == 0 else e_ylo, k + 1 if half == 0 else e + 1)
                    cols = slice(half * UC, (half + 1) * UC)
                    for t in range(TT):
                        o = ps[:, late_bank(t) + half, :]
                        pe.matmul(o, pickT[:, t * P:(t + 1) * P], y_hi[:, cols], start=True, stop=False)
                        ins = pe.matmul(o, pickT[:, t * P:(t + 1) * P], y_lo[:, cols], start=False, stop=True)
                        if half == 1:
                            ins.then_inc(e_sc, 1)

            pe.sem_inc(e_used[2], 1)
            pe.sem_inc(e_tr, 1)
            keep_warm(6)
            pe.wait_ge(r_rank, 1)
            expert_pass(0)
            fullest = pe.value_load(most[0:1, 0:1])
            with pe.If(fullest > CAP):
                pe.wait_ge(e_again, TT)
                pe.wait_ge(e_add, TT * NE + 1)
                expert_pass(1)


_INS = ["x", "g_mix", "w_in", "b_f", "conv_w", "w_a2", "b_a", "g_gla", "w_pa", "w_pb", "w_pc", "w_gate", "b_gate",
        "w_o", "g_ffn", "ffn_w1", "ffn_w3", "ffn_w2", "w_router", "moe_w1", "moe_w3", "moe_w2", "g_final"]


def kernel(**inputs):
    import numpy as _np
    import concourse.bacc as _bacc
    from concourse import mybir as _mybir
    from concourse.bass_utils import run_bass_kernel_spmd as _run

    nc = _bacc.Bacc("TRN2", target_bir_lowering=False, num_devices=1)
    arrays, args = {}, []
    for name in _INS:
        a = _np.ascontiguousarray(inputs[name])
        arrays[f"in_{name}"] = a
        args.append(nc.dram_tensor(f"in_{name}", a.shape, _mybir.dt.from_np(a.dtype), kind="ExternalInput").ap())
    shape = arrays["in_x"].shape
    args.append(nc.dram_tensor("out_y", shape, _mybir.dt.float32, kind="ExternalOutput").ap())
    hybrid_trunk(nc, *args)
    r = _run(nc, [arrays], core_ids=[0])
    return r.results[0]["out_y"]
```
